# Optimizing a Trainium2 kernel written in Bass

```python
import math
import jax, jax.numpy as jnp
from jax import lax
import numpy as np

D_MODEL = 1024
BATCH = 1
SEQ = 256
DEPTH = 2

MIX_WIDTH = D_MODEL
HEAD_DIM = 64
ATTN_WIDTH = D_MODEL // 2
N_Q_HEADS = ATTN_WIDTH // HEAD_DIM
N_KV_HEADS = N_Q_HEADS // 4
KV_WIDTH = N_KV_HEADS * HEAD_DIM
WINDOW = 128
BLOCK = 128
ROPE_THETA = 500000.0
ROPE_DIM = HEAD_DIM // 4
CONV_WIDTH = D_MODEL // 4
CONV_K = 3
POOL_WIDTH = D_MODEL // 4
POOL_WINDOWS = (2, 4, 8, 16)
POOL_GROUP = POOL_WIDTH // len(POOL_WINDOWS)
IN_WIDTH = ATTN_WIDTH + 2 * KV_WIDTH + 3 * CONV_WIDTH + POOL_WIDTH
IN_SPLITS = (ATTN_WIDTH,
             ATTN_WIDTH + KV_WIDTH,
             ATTN_WIDTH + 2 * KV_WIDTH,
             ATTN_WIDTH + 2 * KV_WIDTH + CONV_WIDTH,
             ATTN_WIDTH + 2 * KV_WIDTH + 2 * CONV_WIDTH,
             ATTN_WIDTH + 2 * KV_WIDTH + 3 * CONV_WIDTH)
PEER_HEADS = 8
PEER_NKEYS = 128
PEER_EXPERTS = PEER_NKEYS * PEER_NKEYS
PEER_QDIM = 256
PEER_TOPK = 16
PEER_CHUNK = 128
EPS = 1e-6
MASK_VALUE = -1e30


def rms_norm(t, g):
    tf = t.astype(jnp.float32)
    y = tf * lax.rsqrt(jnp.mean(tf * tf, axis=-1, keepdims=True) + EPS)
    return (y * g.astype(jnp.float32)).astype(t.dtype)

def rope_tables(positions):
    inv = ROPE_THETA ** (-jnp.arange(0, ROPE_DIM, 2, dtype=jnp.float32) / ROPE_DIM)
    ang = positions.astype(jnp.float32)[..., None] * inv
    return jnp.cos(ang)[:, :, None, :], jnp.sin(ang)[:, :, None, :]

def partial_rope(t, cos, sin):
    half = ROPE_DIM // 2
    t1 = t[..., :half].astype(jnp.float32)
    t2 = t[..., half:ROPE_DIM].astype(jnp.float32)
    rot = jnp.concatenate([t1 * cos - t2 * sin, t2 * cos + t1 * sin], axis=-1).astype(t.dtype)
    return jnp.concatenate([rot, t[..., ROPE_DIM:]], axis=-1)

def windowed_gqa(q, k, v, sink):
    b, s = q.shape[0], q.shape[1]
    nb = s // BLOCK
    grp = N_Q_HEADS // N_KV_HEADS
    qb = q.reshape(b, nb, BLOCK, N_KV_HEADS, grp, HEAD_DIM)

    def bands(t):
        tp = jnp.pad(t, ((0, 0), (BLOCK, BLOCK), (0, 0), (0, 0)))
        tp = tp.reshape(b, nb + 2, BLOCK, N_KV_HEADS, HEAD_DIM)
        return jnp.concatenate([tp[:, :-2], tp[:, 1:-1], tp[:, 2:]], axis=2)

    kb, vb = bands(k), bands(v)
    scores = jnp.einsum('bnqhgd,bnkhd->bnhgqk', qb, kb).astype(jnp.float32) * (HEAD_DIM ** -0.5)
    qpos = jnp.arange(s).reshape(nb, BLOCK, 1)
    kpos = (jnp.arange(nb)[:, None, None] - 1) * BLOCK + jnp.arange(3 * BLOCK)[None, None, :]
    valid = (jnp.abs(qpos - kpos) <= WINDOW) & (kpos >= 0) & (kpos < s)
    scores = jnp.where(valid[None, :, None, None], scores, MASK_VALUE)
    sink_col = jnp.broadcast_to(
        sink.astype(jnp.float32).reshape(1, 1, N_KV_HEADS, grp, 1, 1), scores.shape[:-1] + (1,))
    probs = jax.nn.softmax(jnp.concatenate([scores, sink_col], axis=-1), axis=-1)[..., :-1]
    out = jnp.einsum('bnhgqk,bnkhd->bnqhgd', probs.astype(v.dtype), vb)
    return out.reshape(b, s, N_Q_HEADS * HEAD_DIM)

def short_conv(u, w):
    up = jnp.pad(u, ((0, 0), (1, 1), (0, 0)))
    return w[0] * up[:, :-2] + w[1] * up[:, 1:-1] + w[2] * up[:, 2:]

def multiscale_pool(u):
    s = u.shape[1]
    t = jnp.arange(s)
    uf = u.astype(jnp.float32)
    cs = jnp.pad(jnp.cumsum(uf, axis=1), ((0, 0), (1, 0), (0, 0)))
    outs = []
    for gi, w in enumerate(POOL_WINDOWS):
        lo = jnp.clip(t - w // 2, 0, s)
        hi = jnp.clip(t + w // 2, 0, s)
        csg = cs[..., gi * POOL_GROUP:(gi + 1) * POOL_GROUP]
        cnt = (hi - lo).astype(jnp.float32)[None, :, None]
        mean = (jnp.take(csg, hi, axis=1) - jnp.take(csg, lo, axis=1)) / cnt
        outs.append(mean - uf[..., gi * POOL_GROUP:(gi + 1) * POOL_GROUP])
    return jnp.stack(outs, axis=2).astype(u.dtype)

def peer_ffn(h, w_q, sub_keys, expert_u, expert_v):
    b, s, d = h.shape
    n_tok = b * s
    ht = h.reshape(n_tok, d)
    q = (ht @ w_q).reshape(n_tok, PEER_HEADS, PEER_QDIM)
    half = PEER_QDIM // 2
    s1 = jnp.einsum('thd,kd->thk', q[..., :half], sub_keys[0]).astype(jnp.float32)
    s2 = jnp.einsum('thd,kd->thk', q[..., half:], sub_keys[1]).astype(jnp.float32)
    v1, i1 = lax.top_k(s1, PEER_TOPK)
    v2, i2 = lax.top_k(s2, PEER_TOPK)
    cand = (v1[..., :, None] + v2[..., None, :]).reshape(n_tok, PEER_HEADS, PEER_TOPK * PEER_TOPK)
    cidx = (i1[..., :, None] * PEER_NKEYS + i2[..., None, :]).reshape(n_tok, PEER_HEADS, PEER_TOPK * PEER_TOPK)
    top, pos = lax.top_k(cand, PEER_TOPK)
    eidx = jnp.take_along_axis(cidx, pos, axis=-1)
    gate = jax.nn.softmax(top, axis=-1).astype(h.dtype)
    n_chunks = n_tok // PEER_CHUNK

    def chunk(args):
        hc, ec, gc = args
        u = expert_u[ec]
        act = jax.nn.gelu(jnp.einsum('td,thkd->thk', hc, u), approximate=False)
        return jnp.einsum('thk,thkd->td', gc * act, expert_v[ec])

    y = lax.map(chunk, (ht.reshape(n_chunks, PEER_CHUNK, d),
                        eidx.reshape(n_chunks, PEER_CHUNK, PEER_HEADS, PEER_TOPK),
                        gate.reshape(n_chunks, PEER_CHUNK, PEER_HEADS, PEER_TOPK)))
    return y.reshape(b, s, d)

def first_inputs(seed: int = 0) -> dict:
    key = jax.random.key(seed)
    ks = jax.random.split(key, 20)
    L, D = DEPTH, D_MODEL

    def nrm(k, shape, scale):
        return jax.random.normal(k, shape, jnp.float32) * scale

    return {
        "x": nrm(ks[0], (BATCH, SEQ, D), 1.0),
        "c": nrm(ks[1], (BATCH, D), 1.0),
        "positions": jnp.arange(SEQ, dtype=jnp.int32)[None, :]
                     + jax.random.randint(ks[2], (BATCH, 1), 0, 1024, dtype=jnp.int32),
        "norm1_g": 1.0 + nrm(ks[3], (L, D), 0.02),
        "norm2_g": 1.0 + nrm(ks[4], (L, D), 0.02),
        "w_ada": nrm(ks[5], (L, D, 6 * D), 0.5 * D ** -0.5),
        "b_ada": nrm(ks[6], (L, 6 * D), 0.02),
        "w_in": nrm(ks[7], (L, D, IN_WIDTH), D ** -0.5),
        "q_norm_g": 1.0 + nrm(ks[8], (L, HEAD_DIM), 0.02),
        "k_norm_g": 1.0 + nrm(ks[9], (L, HEAD_DIM), 0.02),
        "attn_sink": nrm(ks[10], (L, N_Q_HEADS), 0.5),
        "conv_w": nrm(ks[11], (L, CONV_K, CONV_WIDTH), CONV_K ** -0.5),
        "pool_w": nrm(ks[12], (L, len(POOL_WINDOWS), POOL_GROUP, POOL_GROUP), POOL_GROUP ** -0.5),
        "pool_scale": 1.0 + nrm(ks[13], (L, POOL_WIDTH), 0.1),
        "w_out": nrm(ks[14], (L, MIX_WIDTH, D), MIX_WIDTH ** -0.5),
        "peer_wq": nrm(ks[15], (L, D, PEER_HEADS * PEER_QDIM), D ** -0.5),
        "peer_keys": nrm(ks[16], (L, 2, PEER_NKEYS, PEER_QDIM // 2), (PEER_QDIM // 2) ** -0.5),
        "peer_u": nrm(ks[17], (L, PEER_EXPERTS, D), D ** -0.5),
        "peer_v": nrm(ks[18], (L, PEER_EXPERTS, D), PEER_HEADS ** -0.5),
    }

def first_block(x, c, positions, norm1_g, norm2_g, w_ada, b_ada, w_in, q_norm_g, k_norm_g,
              attn_sink, conv_w, pool_w, pool_scale, w_out, peer_wq, peer_keys, peer_u, peer_v):
    b, s, d = x.shape
    cos, sin = rope_tables(positions)
    c_act = jax.nn.silu(c)
    for l in range(DEPTH):
        mod = (c_act @ w_ada[l] + b_ada[l])[:, None, :]
        shift1, scale1, gate1, shift2, scale2, gate2 = jnp.split(mod, 6, axis=-1)

        h = rms_norm(x, norm1_g[l]) * (1.0 + scale1) + shift1
        z = h @ w_in[l]
        q, k, v, conv_x, conv_b, conv_c, pool_x = jnp.split(z, IN_SPLITS, axis=-1)

        q = q.reshape(b, s, N_Q_HEADS, HEAD_DIM)
        k = k.reshape(b, s, N_KV_HEADS, HEAD_DIM)
        v = v.reshape(b, s, N_KV_HEADS, HEAD_DIM)
        q = partial_rope(rms_norm(q, q_norm_g[l]), cos, sin)
        k = partial_rope(rms_norm(k, k_norm_g[l]), cos, sin)
        attn_o = windowed_gqa(q, k, v, attn_sink[l])

        conv_o = conv_b * short_conv(conv_c * conv_x, conv_w[l])

        pooled = multiscale_pool(pool_x)
        pool_o = jnp.einsum('bsgc,gce->bsge', pooled, pool_w[l]).reshape(b, s, POOL_WIDTH) * pool_scale[l]

        mix = jnp.concatenate([attn_o, conv_o, pool_o], axis=-1) @ w_out[l]
        x = x + gate1 * mix

        h2 = rms_norm(x, norm2_g[l]) * (1.0 + scale2) + shift2
        x = x + gate2 * peer_ffn(h2, peer_wq[l], peer_keys[l], peer_u[l], peer_v[l])
    return x


N_A_LAYERS = DEPTH // 2
N_B_LAYERS = DEPTH - N_A_LAYERS
D_FF = 2816
D_RNN = 1344
N_LRU_BLOCKS = 16
LRU_BLOCK = D_RNN // N_LRU_BLOCKS
CONV_WIDTH_2 = 4
LRU_C = 8.0
N_HEADS = 16
D_ATTN = N_HEADS * HEAD_DIM
Q_BLOCK = 128


def rms_norm_2(x, g):
    xf = x.astype(jnp.float32)
    y = xf * lax.rsqrt(jnp.mean(xf * xf, axis=-1, keepdims=True) + EPS)
    return (y * g.astype(jnp.float32)).astype(x.dtype)

def swiglu(x, w_gate, w_up, w_down):
    return (jax.nn.silu(x @ w_gate) * (x @ w_up)) @ w_down

def causal_depthwise_conv(x, w, b):
    S = x.shape[1]
    xp = jnp.pad(x, ((0, 0), (CONV_WIDTH_2 - 1, 0), (0, 0)))
    y = b
    for k in range(CONV_WIDTH_2):
        y = y + xp[:, k:k + S] * w[k]
    return y

def rg_lru(x, w_a, b_a, w_x, b_x, lam):
    Bn, S, _ = x.shape
    xb = x.reshape(Bn, S, N_LRU_BLOCKS, LRU_BLOCK)
    r = jax.nn.sigmoid(jnp.einsum('bsnc,ncd->bsnd', xb, w_a).reshape(Bn, S, D_RNN) + b_a)
    i = jax.nn.sigmoid(jnp.einsum('bsnc,ncd->bsnd', xb, w_x).reshape(Bn, S, D_RNN) + b_x)
    log_a = -LRU_C * r.astype(jnp.float32) * jax.nn.softplus(-lam.astype(jnp.float32))
    a = jnp.exp(log_a)
    u = jnp.sqrt(-jnp.expm1(2.0 * log_a)) * (i * x).astype(jnp.float32)

    def combine(c1, c2):
        a1, b1 = c1
        a2, b2 = c2
        return a1 * a2, a2 * b1 + b2

    _, h = lax.associative_scan(combine, (a, u), axis=1)
    return h.astype(x.dtype)

def recurrent_block(x, w_in, conv_w, conv_b, w_a, b_a, w_x, b_x, lam, w_out):
    gx = x @ w_in
    gate, rec = gx[..., :D_RNN], gx[..., D_RNN:]
    rec = causal_depthwise_conv(rec, conv_w, conv_b)
    rec = rg_lru(rec, w_a, b_a, w_x, b_x, lam)
    return (jax.nn.gelu(gate) * rec) @ w_out

def shared_kv(h, g, w_kv, w_f, b_f):
    Bn, S, _ = h.shape
    hn = rms_norm_2(h, g)
    kv = (hn @ w_kv).reshape(Bn, S, 2, N_HEADS, HEAD_DIM)
    k = kv[:, :, 0].transpose(0, 2, 1, 3)
    v = kv[:, :, 1].transpose(0, 2, 1, 3)
    log_f = jax.nn.log_sigmoid((hn @ w_f + b_f).astype(jnp.float32))
    c = jnp.cumsum(log_f, axis=1).transpose(0, 2, 1)
    return k, v, c

def forgetting_attention(xq, w_q, w_o, k, v, c):
    Bn, S, _ = xq.shape
    q = (xq @ w_q).reshape(Bn, S, N_HEADS, HEAD_DIM).transpose(0, 2, 1, 3) * (HEAD_DIM ** -0.5)
    outs = []
    for blk in range(S // Q_BLOCK):
        q0 = blk * Q_BLOCK
        end = q0 + Q_BLOCK
        logits = jnp.einsum('bhqd,bhkd->bhqk', q[:, :, q0:end], k[:, :, :end]).astype(jnp.float32)
        logits = logits + c[:, :, q0:end, None] - c[:, :, None, :end]
        qpos = q0 + jnp.arange(Q_BLOCK)
        kpos = jnp.arange(end)
        logits = jnp.where(kpos[None, :] <= qpos[:, None], logits, -jnp.inf)
        p = jax.nn.softmax(logits, axis=-1).astype(v.dtype)
        outs.append(jnp.einsum('bhqk,bhkd->bhqd', p, v[:, :, :end]))
    o = jnp.concatenate(outs, axis=2).transpose(0, 2, 1, 3).reshape(Bn, S, D_ATTN)
    return o @ w_o

def second_inputs(seed: int = 0) -> dict:
    key = jax.random.key(seed)
    ks = iter(jax.random.split(key, 40))
    f32 = jnp.float32

    def nrm(shape, fan_in):
        return jax.random.normal(next(ks), shape, f32) * (fan_in ** -0.5)

    def gain(shape):
        return 1.0 + 0.05 * jax.random.normal(next(ks), shape, f32)

    def small(shape):
        return 0.02 * jax.random.normal(next(ks), shape, f32)

    L, NA, NB = DEPTH, N_A_LAYERS, N_B_LAYERS
    x = jax.random.normal(next(ks), (BATCH, SEQ, D_MODEL), f32)
    u = jax.random.uniform(next(ks), (NA, D_RNN), f32, minval=0.9, maxval=0.999)
    a0 = u ** (1.0 / LRU_C)
    rg_lambda = jnp.log(a0) - jnp.log1p(-a0)
    return {
        "x": x,
        "ffn1_pre_g": gain((L, D_MODEL)),
        "ffn1_w_gate": nrm((L, D_MODEL, D_FF), D_MODEL),
        "ffn1_w_up": nrm((L, D_MODEL, D_FF), D_MODEL),
        "ffn1_w_down": nrm((L, D_FF, D_MODEL), D_FF),
        "ffn1_post_g": gain((L, D_MODEL)),
        "mix_pre_g": gain((L, D_MODEL)),
        "mix_post_g": gain((L, D_MODEL)),
        "ffn2_pre_g": gain((L, D_MODEL)),
        "ffn2_w_gate": nrm((L, D_MODEL, D_FF), D_MODEL),
        "ffn2_w_up": nrm((L, D_MODEL, D_FF), D_MODEL),
        "ffn2_w_down": nrm((L, D_FF, D_MODEL), D_FF),
        "ffn2_post_g": gain((L, D_MODEL)),
        "rg_w_in": nrm((NA, D_MODEL, 2 * D_RNN), D_MODEL),
        "rg_conv_w": nrm((NA, CONV_WIDTH_2, D_RNN), CONV_WIDTH_2),
        "rg_conv_b": small((NA, D_RNN)),
        "rg_w_a": nrm((NA, N_LRU_BLOCKS, LRU_BLOCK, LRU_BLOCK), LRU_BLOCK),
        "rg_b_a": small((NA, D_RNN)),
        "rg_w_x": nrm((NA, N_LRU_BLOCKS, LRU_BLOCK, LRU_BLOCK), LRU_BLOCK),
        "rg_b_x": small((NA, D_RNN)),
        "rg_lambda": rg_lambda,
        "rg_w_out": nrm((NA, D_RNN, D_MODEL), D_RNN),
        "kv_norm_g": gain((D_MODEL,)),
        "w_kv": nrm((D_MODEL, 2 * D_ATTN), D_MODEL),
        "w_fgate": nrm((D_MODEL, N_HEADS), D_MODEL),
        "b_fgate": jax.random.uniform(next(ks), (N_HEADS,), f32, minval=1.0, maxval=4.0),
        "attn_w_q": nrm((NB, D_MODEL, D_ATTN), D_MODEL),
        "attn_w_o": nrm((NB, D_ATTN, D_MODEL), D_ATTN),
    }

def second_block(x, ffn1_pre_g, ffn1_w_gate, ffn1_w_up, ffn1_w_down, ffn1_post_g,
              mix_pre_g, mix_post_g,
              ffn2_pre_g, ffn2_w_gate, ffn2_w_up, ffn2_w_down, ffn2_post_g,
              rg_w_in, rg_conv_w, rg_conv_b, rg_w_a, rg_b_a, rg_w_x, rg_b_x, rg_lambda, rg_w_out,
              kv_norm_g, w_kv, w_fgate, b_fgate, attn_w_q, attn_w_o):
    h = x
    k = v = c = None
    for layer in range(DEPTH):
        if layer == N_A_LAYERS:
            k, v, c = shared_kv(h, kv_norm_g, w_kv, w_fgate, b_fgate)
        f = swiglu(rms_norm_2(h, ffn1_pre_g[layer]), ffn1_w_gate[layer], ffn1_w_up[layer], ffn1_w_down[layer])
        h = h + 0.5 * rms_norm_2(f, ffn1_post_g[layer])
        hn = rms_norm_2(h, mix_pre_g[layer])
        if layer < N_A_LAYERS:
            j = layer
            m = recurrent_block(hn, rg_w_in[j], rg_conv_w[j], rg_conv_b[j], rg_w_a[j], rg_b_a[j],
                                rg_w_x[j], rg_b_x[j], rg_lambda[j], rg_w_out[j])
        else:
            j = layer - N_A_LAYERS
            m = forgetting_attention(hn, attn_w_q[j], attn_w_o[j], k, v, c)
        h = h + rms_norm_2(m, mix_post_g[layer])
        f = swiglu(rms_norm_2(h, ffn2_pre_g[layer]), ffn2_w_gate[layer], ffn2_w_up[layer], ffn2_w_down[layer])
        h = h + 0.5 * rms_norm_2(f, ffn2_post_g[layer])
    return h


def setup_inputs(seed=0):
    out = dict(first_inputs(seed))
    for name, value in second_inputs(seed + 1).items():
        if name != "x":
            out[name + "_2"] = value
    return out


def reference(
    x, c, positions, norm1_g, norm2_g, w_ada, b_ada, w_in, q_norm_g, k_norm_g, attn_sink,
    conv_w, pool_w, pool_scale, w_out, peer_wq, peer_keys, peer_u, peer_v, ffn1_pre_g_2,
    ffn1_w_gate_2, ffn1_w_up_2, ffn1_w_down_2, ffn1_post_g_2, mix_pre_g_2, mix_post_g_2,
    ffn2_pre_g_2, ffn2_w_gate_2, ffn2_w_up_2, ffn2_w_down_2, ffn2_post_g_2, rg_w_in_2,
    rg_conv_w_2, rg_conv_b_2, rg_w_a_2, rg_b_a_2, rg_w_x_2, rg_b_x_2, rg_lambda_2, rg_w_out_2,
    kv_norm_g_2, w_kv_2, w_fgate_2, b_fgate_2, attn_w_q_2, attn_w_o_2,
):
    x = first_block(
        x, c, positions, norm1_g, norm2_g, w_ada, b_ada, w_in, q_norm_g, k_norm_g, attn_sink,
        conv_w, pool_w, pool_scale, w_out, peer_wq, peer_keys, peer_u, peer_v,
    )
    return second_block(
        x, ffn1_pre_g_2, ffn1_w_gate_2, ffn1_w_up_2, ffn1_w_down_2, ffn1_post_g_2, mix_pre_g_2,
        mix_post_g_2, ffn2_pre_g_2, ffn2_w_gate_2, ffn2_w_up_2, ffn2_w_down_2, ffn2_post_g_2,
        rg_w_in_2, rg_conv_w_2, rg_conv_b_2, rg_w_a_2, rg_b_a_2, rg_w_x_2, rg_b_x_2,
        rg_lambda_2, rg_w_out_2, kv_norm_g_2, w_kv_2, w_fgate_2, b_fgate_2, attn_w_q_2,
        attn_w_o_2,
    )


_drawn_inputs = setup_inputs


def setup_inputs(seed=0):
    import zlib

    import numpy as np

    out = dict(_drawn_inputs(seed))
    spreads = {}
    factors = {'norm1_g': 2.974,
     'norm2_g': 22.135,
     'q_norm_g': 8.0,
     'k_norm_g': 8.0,
     'attn_sink': 8.0,
     'rg_b_a_2': 64.0,
     'rg_b_x_2': 53.217,
     'pool_scale': 3.328,
     'ffn1_pre_g_2': 7.647,
     'ffn1_post_g_2': 8.0,
     'mix_pre_g_2': 4.591,
     'mix_post_g_2': 5.218,
     'ffn2_pre_g_2': 7.686,
     'ffn2_post_g_2': 8.0,
     'rg_conv_b_2': 2.679,
     'kv_norm_g_2': 6.375}
    for name, (base, spread) in spreads.items():
        noise = np.random.default_rng([zlib.crc32(name.encode()), seed]).standard_normal(out[name].shape)
        drawn = base * np.exp(spread * noise) if base else spread * noise
        out[name] = __import__('jax').numpy.asarray(drawn.astype(out[name].dtype))
    for name, factor in factors.items():
        out[name] = (out[name] * factor).astype(out[name].dtype)
    return out
```

```python
from contextlib import ExitStack

import numpy as np

import concourse.bass as bass
from concourse import mybir

ALU = mybir.AluOpType
ACT = mybir.ActivationFunctionType
F32 = mybir.dt.float32
I32 = mybir.dt.int32
U32 = mybir.dt.uint32
AX_X = mybir.AxisListType.X

P = 128
SEQ = 256
D = 1024
KC = D // P
TILES = SEQ // P
DEPTH = 2
EPS = 1e-6
MASKED = -1e30
LEAST = -3.0e38

HEAD = 64
Q_HEADS = 8
KV_HEADS = 2
GROUP = Q_HEADS // KV_HEADS
ROPE = HEAD // 4
ROPE_THETA = 500000.0
WINDOWS = (2, 4, 8, 16)
PAD = WINDOWS[-1]
PADDED = SEQ + 2 * PAD
ATTN_W = Q_HEADS * HEAD
KV_W = KV_HEADS * HEAD
EXPERT_HEADS = 8
KEYS = 128
EXPERTS = KEYS * KEYS
TOPK = 16
UNITS = TILES * EXPERT_HEADS
U_SLOTS = 8
V_SLOTS = 16
GRP = 8

D_FF = 2816
FF_CHUNKS = D_FF // P
D_RNN = 1344
RC = 112
R_CHUNKS = D_RNN // RC
LRU = 84
SUPER = 4
CONV_K = 4
HEADS2 = 16

SLOTS = 4
SLOT = 4096
N = 512


def program(nc, A, out):
    with ExitStack() as ctx:
        def sb(name, shape, dt=F32):
            return ctx.enter_context(nc.sbuf_tensor(name, shape, dt))

        def sem(name):
            return ctx.enter_context(nc.semaphore(name))

        ps = ctx.enter_context(nc.psum_tensor("ps", [P, 8, N], F32))
        WORK = 4

        ring = sb("weight_ring", [P, SLOTS, SLOT])
        x = sb("x", [P, TILES, D])
        h_ext = sb("h_ext", [P, TILES * D + D])
        h = h_ext[:, 0:TILES * D].rearrange("p (t d) -> p t d", t=TILES)
        junk = h_ext[:, TILES * D:]
        hT = sb("hT", [P, KC, SEQ])
        gain_pre = sb("gain_pre", [P, D])
        gain_post = sb("gain_post", [P, D])
        ident = sb("ident", [P, P])
        zeros = sb("zeros", [P, P])
        ones = sb("ones", [P, P])
        upto = sb("upto", [P, P])
        window = sb("window_mask", [P, TILES, SEQ])
        eps = sb("eps", [P, 1])
        iota16 = sb("iota16", [P, TOPK])
        window_count = sb("window_count", [P, 2, SEQ])
        c_rows = sb("c_rows", [KC, P])
        c_act = sb("c_act", [P, KC])
        c_wide = sb("c_wide", [P, KC, P])
        pos_i = sb("pos_i", [TILES, P], I32)
        pos_f = sb("pos_f", [TILES, P])
        pos = sb("pos", [P, TILES])
        inv_freq = sb("inv_freq", [P, ROPE // 2])
        angle = sb("angle", [P, 4, TILES, ROPE // 2])
        cosine = sb("cosine", [P, TILES, ROPE // 2])
        sine = sb("sine", [P, TILES, ROPE // 2])
        mix_rows = sb("mix_rows", [8, P])
        mix_cols = sb("mix_cols", [P, 8])
        pool_w = sb("pool_w", [P, 2, P])
        keys_raw = sb("keys_raw", [P, 2, KEYS])
        keysT = sb("keysT", [P, 2, KEYS])
        sink = sb("sink", [P, Q_HEADS])
        expert_base = sb("expert_base", [P, 1])
        mean_sq = sb("mean_sq", [P, TILES])
        rms = sb("rms", [P, TILES])
        rstd = sb("rstd", [P, TILES])
        head_sq = sb("head_sq", [P, TILES, Q_HEADS + KV_HEADS])
        head_rms = sb("head_rms", [P, TILES, Q_HEADS + KV_HEADS])
        row_max = sb("row_max", [P, 2, GROUP])
        neg_max = sb("neg_max", [P, 2, GROUP])
        sink_d = sb("sink_d", [P, 2, GROUP])
        sink_e = sb("sink_e", [P, 2, GROUP])
        row_sum = sb("row_sum", [P, 2, GROUP])
        row_inv = sb("row_inv", [P, 2, GROUP])
        best = sb("best", [P, 2, TOPK])
        best_i = sb("best_i", [P, 2, TOPK], U32)
        best_f = sb("best_f", [P, 2, TOPK])
        place = sb("place", [P, TOPK], U32)
        place2 = sb("place2", [P, 2, TOPK], U32)
        place_f = sb("place_f", [P, 2, TOPK])
        chosen = sb("chosen", [P, 2, TOPK])
        expert_f = sb("expert_f", [P, TOPK])
        expert = sb("expert", [P, 2, TOPK], U32)
        top = sb("top", [P, 2, TOPK])
        neg_top = sb("neg_top", [P, 2, 1])
        gate_e = sb("gate_e", [P, 2, TOPK])
        gate_sum = sb("gate_sum", [P, 2, 1])
        gate_inv = sb("gate_inv", [P, 1])
        gate = sb("gate", [P, TOPK])
        dots = sb("dots", [P, 2, GRP])
        acts = sb("acts", [P, 2, GRP])
        rnn_rows = sb("rnn_rows", [8 * R_CHUNKS, RC])
        rnn_cols = sb("rnn_cols", [RC, 8, R_CHUNKS])
        decay = sb("decay", [RC, 6, R_CHUNKS])
        decay_neg = sb("decay_neg", [RC, R_CHUNKS])
        decay_pos = sb("decay_pos", [RC, R_CHUNKS])
        wf = sb("wf", [P, KC, HEADS2])
        bf = sb("bf", [1, HEADS2])
        f_tok = sb("f_tok", [P, TILES * HEADS2])
        logs = sb("logs", [P, 6, TILES * HEADS2])
        log_f = sb("log_f", [P, TILES * HEADS2])
        c_tok = sb("c_tok", [P, TILES * HEADS2])

        ARENA = 21824
        arena = sb("arena", [P, ARENA])

        class Carve:

            def __init__(self, start=0):
                self.at = start

            def __call__(self, size, pattern=None, **kw):
                part = arena[:, self.at:self.at + size]
                self.at += size
                assert self.at <= ARENA, self.at
                return part.rearrange(pattern, **kw) if pattern else part

        c1 = Carve()
        mod = c1(6 * D, "p (s d) -> p s d", s=6)
        qTz = c1(Q_HEADS * SEQ, "p (h t) -> p h t", h=Q_HEADS)
        shared = c1.at
        QK = Q_HEADS + KV_HEADS
        qk = c1(TILES * QK * HEAD, "p (t h d) -> p t h d", t=TILES, h=QK)
        qk_sq = c1(TILES * QK * HEAD, "p (t h d) -> p t h d", t=TILES, h=QK)
        qk_gain = c1(QK * HEAD, "p (h d) -> p h d", h=QK)
        v_tok = c1(TILES * KV_W, "p (t d) -> p t d", t=TILES)
        kT = c1(SEQ)
        zc = c1(8 * SEQ, "p (c t) -> p c t", c=8)
        pT = c1(2 * GROUP * P, "p (i t) -> p i t", t=P)
        attn = c1(TILES * ATTN_W, "p (t d) -> p t d", t=TILES)
        mixT = c1(KC * SEQ, "p (c t) -> p c t", c=KC)
        conv_u = c1(2 * SEQ, "p (c t) -> p c t", c=2)
        conv_o = c1(2 * SEQ, "p (c t) -> p c t", c=2)
        conv_t = c1(2 * SEQ, "p (c t) -> p c t", c=2)
        pool_in = c1(2 * PADDED, "p (c t) -> p c t", c=2)
        pool_s = [c1(2 * PADDED, "p (c t) -> p c t", c=2) for _ in range(2)]
        pooled = c1(2 * SEQ, "p (c t) -> p c t", c=2)
        rope_t = h_ext[:, 0:4 * TILES * QK * ROPE // 2].rearrange("p (n t h d) -> p n t h d", n=4, t=TILES, h=QK)
        scores = h_ext[:, 0:2 * GROUP * SEQ].rearrange("p (b i t) -> p b i t", b=2, i=GROUP)
        c2 = Carve(shared)
        u_ring = c2(U_SLOTS * D, "p (s d) -> p s d", s=U_SLOTS)
        diag = c2(2 * GRP * P, "p (s t) -> p s t", t=P)
        half_s = c2(2 * KEYS, "p (h k) -> p h k", h=2)
        half_r = c2(2 * KEYS, "p (h k) -> p h k", h=2)
        cand = c2(TOPK * TOPK)
        cand_r = c2(TOPK * TOPK)
        onehot = c2(TOPK * TOPK, "p (k j) -> p k j", k=TOPK)
        qpT = arena[:, shared:shared + 16 * SEQ].rearrange("p (c t) -> p c t", c=16)
        key_s = arena[:, 0:UNITS * 2 * KEYS].rearrange("p (n h k) -> p n h k", n=UNITS, h=2)
        v_ring = ring[:, :, :].rearrange("p s (b d) -> p (s b) d", d=D)
        ada_bias = hT[0:4, :, :].rearrange("p c t -> p (c t)")
        ff = Carve(ARENA - 4 * SEQ)
        silu_g = ff(2 * SEQ, "p (b t) -> p b t", b=2)
        ff_a = ff(2 * SEQ, "p (b t) -> p b t", b=2)
        c3 = Carve()
        gate_g = c3(R_CHUNKS * SEQ, "p (c t) -> p c t", c=R_CHUNKS)[0:RC]
        rec_width = SEQ + CONV_K - 1
        rec_at = c3.at
        rec_in = c3(R_CHUNKS * rec_width, "p (c t) -> p c t", c=R_CHUNKS)[0:RC]
        gate_i = arena[0:RC, rec_at:rec_at + R_CHUNKS * SEQ].rearrange("p (c t) -> p c t", c=R_CHUNKS)
        rec = c3(R_CHUNKS * SEQ, "p (c t) -> p c t", c=R_CHUNKS)[0:RC]
        gate_r = c3(R_CHUNKS * SEQ, "p (c t) -> p c t", c=R_CHUNKS)[0:RC]
        wide = 3 * RC
        w_gates = [c3(SUPER * 3 * wide, "p (s i d) -> p s i d", s=SUPER, i=3)[0:RC] for _ in range(2)]
        decay_a = h_ext[0:RC, :].rearrange("p (c t) -> p c t", c=R_CHUNKS)
        c4 = Carve()
        kT2 = c4(8 * SEQ, "p (c t) -> p c t", c=8)
        v2 = c4(TILES * D, "p (t d) -> p t d", t=TILES)
        qTz2 = c4(HEADS2 * SEQ, "p (h t) -> p h t", h=HEADS2)
        head_pick = c4(HEADS2 * P, "p (h t) -> p h t", h=HEADS2)
        scores2 = c4(2 * GROUP * SEQ, "p (b i t) -> p b i t", b=2, i=GROUP)
        pT2 = c4(2 * GROUP * P, "p (i t) -> p i t", t=P)
        c_pad = c4(TILES * P, "p (t j) -> p t j", t=TILES)
        neg_cT = c4(SEQ)

        consts = sem("consts")
        const_steps = sem("const_steps")
        x_loaded = sem("x_loaded")
        c_loaded = sem("c_loaded")
        pos_loaded = sem("pos_loaded")
        pos_float = sem("pos_float")
        pos_turned = sem("pos_turned")
        angle_ready = sem("angle_ready")
        rope_ready = sem("rope_ready")
        c_turned = sem("c_turned")
        c_act_ready = sem("c_act_ready")
        c_wide_ready = sem("c_wide_ready")
        slot_in = [sem(f"slot_in{i}") for i in range(SLOTS)]
        slot_free = sem("slot_free")
        pre_in, pre_free = sem("pre_in"), sem("pre_free")
        post_in, post_free = sem("post_in"), sem("post_free")
        pe_params, dve_params, params_free = sem("pe_params"), sem("dve_params"), sem("params_free")
        bias_in = sem("bias_in")
        params_turned = sem("params_turned")
        x_ready = sem("x_ready")
        rms_ready = sem("rms_ready")
        h_ready = sem("h_ready")
        hT_turned = sem("hT_turned")
        hT_ready = sem("hT_ready")
        job_done, job_taken = sem("job_done"), sem("job_taken")
        mod_ready = sem("mod_ready")
        qk_ready = sem("qk_ready")
        head_sq_ready, head_rms_ready = sem("head_sq_ready"), sem("head_rms_ready")
        zc_ready = sem("zc_ready")
        qk_done = sem("qk_done")
        qk_turned = sem("qk_turned")
        qkT_ready = sem("qkT_ready")
        scores_done = sem("scores_done")
        scores_ready = sem("scores_ready")
        probs_ready = sem("probs_ready")
        sums_ready = sem("sums_ready")
        p_turned, pT_ready = sem("p_turned"), sem("pT_ready")
        pv_done, attn_done = sem("pv_done"), sem("attn_done")
        pooled_ready, pool_done = sem("pooled_ready"), sem("pool_done")
        attn_turned, mixT_ready = sem("attn_turned"), sem("mixT_ready")
        rows_done = sem("rows_done")
        rms2_ready = sem("rms2_ready")
        key_s_done, key_s_ready = sem("key_s_done"), sem("key_s_ready")
        expert_ready = sem("expert_ready")
        top_ready, gate_ready = sem("top_ready"), sem("gate_ready")
        u_in = [sem(f"u_in{i}") for i in range(U_SLOTS)]
        u_free = sem("u_free")
        v_in = [sem(f"v_in{i}") for i in range(V_SLOTS)]
        v_free = sem("v_free")
        dots_ready, acts_ready = sem("dots_ready"), sem("acts_ready")
        diag_ready, diag_free = sem("diag_ready"), sem("diag_free")
        y_ready = sem("y_ready")
        block1_done = sem("block1_done")
        gu_done, silu_ready, ff_ready = sem("gu_done"), sem("silu_ready"), sem("ff_ready")
        rnn_rows_in, rnn_turned, rnn_cols_ready = sem("rnn_rows_in"), sem("rnn_turned"), sem("rnn_cols_ready")
        rnn_zeroed, rnn_w_in = sem("rnn_zeroed"), sem("rnn_w_in")
        lam_abs, lam_exp, decay_ready = sem("lam_abs"), sem("lam_exp"), sem("decay_ready")
        rec_in_ready, rec_ready = sem("rec_in_ready"), sem("rec_ready")
        gates_ready, root_in, root_ready = sem("gates_ready"), sem("root_in"), sem("root_ready")
        rnn_out_ready = sem("rnn_out_ready")
        rnn_over = sem("rnn_over")
        wf_in = sem("wf_in")
        heads_zeroed = sem("heads_zeroed")
        f_ready, f_abs, f_exp, log_f_ready = sem("f_ready"), sem("f_abs"), sem("f_exp"), sem("log_f_ready")
        c_summed, c_ready, c_back, neg_cT_ready = sem("c_summed"), sem("c_ready"), sem("c_back"), sem("neg_cT_ready")
        x_final = sem("x_final")
        out_stored = sem("out_stored")
        act_steps, dve_steps, pool_steps = sem("act_steps"), sem("dve_steps"), sem("pool_steps")

        def fan(eng, s):
            eng.drain().then_inc(s, 1)

        class Count:

            def __init__(self):
                self.value = 0

            def next(self):
                self.value += 1
                return self.value

            def reset(self):
                value, self.value = self.value, 0
                assert value
                return value

        FF_NAMES = [("ffn1", 0), ("ffn2", 0), ("ffn1", 1), ("ffn2", 1)]
        first = {}
        at = 0
        for name, count in (("ff0", FF_CHUNKS), ("rnn_in", 6), ("rnn_out", 3), ("ff1", FF_CHUNKS), ("kv", 4),
                            ("ff2", FF_CHUNKS), ("q", 2), ("o", 2), ("ff3", FF_CHUNKS)):
            first[name] = at
            at += count
        PEEL = FF_CHUNKS % SLOTS
        TURNS = FF_CHUNKS // SLOTS

        def attention_units(second):
            return [(t, list(range(GROUP * g, GROUP * g + GROUP)))
                    for t in range(TILES) for g in range((HEADS2 if second else Q_HEADS) // GROUP)]

        block = ctx.enter_context(nc.Block())

        @block.sync
        def _(sp):
            sp.dma_start(x[:], A["x"].rearrange("o (t p) d -> p (o t) d", p=P)).then_inc(x_loaded, 16)
            sp.dma_start(c_rows[:], A["c"].rearrange("o (k p) -> (o k) p", p=P)).then_inc(c_loaded, 16)
            sp.dma_start(pos_i[:], A["positions"].rearrange("o (t p) -> (o t) p", p=P)).then_inc(pos_loaded, 16)

            def slot(n):
                sp.wait_ge(slot_free, 1)
                sp.sem_inc(slot_free, -1)
                return ring[:, n % SLOTS, :], slot_in[n % SLOTS]

            def load(n, parts):
                where, s = slot(n)
                for off, rows, k, m, src in parts:
                    sp.dma_start(where[0:rows, off:off + k * m].rearrange("p (k m) -> p k m", k=k), src).then_inc(s, 16)

            with sp.Fori(0, DEPTH) as l:
                def of(name):
                    return A[name][bass.ds(l, 1)].rearrange("o a b -> (o a) b")

                sp.wait_ge(params_free, 1)
                sp.sem_inc(params_free, -1)
                sp.dma_start(mix_rows[0:6, :], A["conv_w"][bass.ds(l, 1)].rearrange("o k (c p) -> (o k c) p", p=P)).then_inc(pe_params, 16)
                sp.dma_start(mix_rows[6:8, :], A["pool_scale"][bass.ds(l, 1)].rearrange("o (c p) -> (o c) p", p=P)).then_inc(pe_params, 16)
                sp.dma_start(keys_raw[:], A["peer_keys"][bass.ds(l, 1)].rearrange("o s k d -> k (o s) d")).then_inc(pe_params, 16)
                groups = A["pool_w"][bass.ds(l, 1)].rearrange("o (c s) i e -> s i (o c) e", s=2)
                for s in range(2):
                    sp.dma_start(pool_w[HEAD * s:HEAD * s + HEAD, :, HEAD * s:HEAD * s + HEAD], groups[s]).then_inc(pe_params, 16)
                sp.dma_start(ada_bias[:, 0:3 * N].rearrange("p (i n) -> p i n", n=N),
                             A["b_ada"][bass.ds(l, 1)].rearrange("o (i u n) -> (o u) i n", u=4, n=N)).then_inc(bias_in, 16)
                sp.wait_ge(pre_free, 1)
                sp.sem_inc(pre_free, -1)
                sp.dma_start(gain_pre[:], A["norm1_g"][bass.ds(l, 1)].to_broadcast([P, D])).then_inc(pre_in, 16)
                sp.wait_ge(post_free, 1)
                sp.sem_inc(post_free, -1)
                sp.dma_start(gain_post[:], A["norm2_g"][bass.ds(l, 1)].to_broadcast([P, D])).then_inc(post_in, 16)
                w_ada = of("w_ada").rearrange("(k p) n -> p k n", p=P)
                with sp.Fori(0, 3) as i:
                    for u in range(4):
                        load(u, [(0, P, KC, N, w_ada[:, :, bass.ds(i * (4 * N) + u * N, N)])])
                sp.dma_start(qk_gain[:, 0:Q_HEADS, :], A["q_norm_g"][bass.ds(l, 1)].unsqueeze(1).to_broadcast([P, Q_HEADS, HEAD])).then_inc(dve_params, 16)
                sp.dma_start(qk_gain[:, Q_HEADS:QK, :], A["k_norm_g"][bass.ds(l, 1)].unsqueeze(1).to_broadcast([P, KV_HEADS, HEAD])).then_inc(dve_params, 16)
                sp.dma_start(sink[:], A["attn_sink"][bass.ds(l, 1)].to_broadcast([P, Q_HEADS])).then_inc(dve_params, 16)
                w_in = of("w_in").rearrange("(k p) n -> p k n", p=P)
                cut = [0, ATTN_W, ATTN_W + 2 * KV_W, ATTN_W + 2 * KV_W + N, ATTN_W + 2 * KV_W + 2 * N]
                for u in range(4):
                    load(u, [(0, P, KC, cut[u + 1] - cut[u], w_in[:, :, cut[u]:cut[u + 1]])])
                w_out = of("w_out").rearrange("(k p) n -> p k n", p=P)
                for u in range(4):
                    load(u, [(0, P, 2, D, w_out[:, 2 * u:2 * u + 2, :])])
                w_q = of("peer_wq").rearrange("(k p) n -> p k n", p=P)
                for u in range(4):
                    load(u, [(0, P, KC, N, w_q[:, :, u * N:(u + 1) * N])])

            def gain(name, layer, pre):
                src = A[name][layer:layer + 1, :] if layer is not None else A[name].unsqueeze(0)
                sp.wait_ge(pre_free if pre else post_free, 1)
                sp.sem_inc(pre_free if pre else post_free, -1)
                sp.dma_start((gain_pre if pre else gain_post)[:], src.to_broadcast([P, D])).then_inc(pre_in if pre else post_in, 16)

            def feed_forward(f):
                name, layer = FF_NAMES[f]
                w_g = A[name + "_w_gate_2"][layer].rearrange("(k p) n -> p k n", p=P)
                w_u = A[name + "_w_up_2"][layer].rearrange("(k p) n -> p k n", p=P)
                w_d = A[name + "_w_down_2"][layer].rearrange("(j p) n -> p j n", p=P)
                gain(name + "_pre_g_2", layer, True)

                def chunk(n, j):
                    load(n, [(0, P, KC, P, w_g[:, :, bass.ds(j * P, P)]),
                             (KC * P, P, KC, P, w_u[:, :, bass.ds(j * P, P)]),
                             (2 * KC * P, P, 1, D, w_d[:, bass.ds(j, 1), :])])

                n0 = first[f"ff{f}"]
                for j in range(PEEL):
                    chunk(n0 + j, j)
                with sp.Fori(0, TURNS) as i:
                    for u in range(SLOTS):
                        chunk(n0 + PEEL + u, i * SLOTS + (PEEL + u))
                gain(name + "_post_g_2", layer, False)

            feed_forward(0)
            rows = [("rg_conv_w_2", 0, CONV_K), ("rg_conv_b_2", 4, 1), ("rg_b_a_2", 5, 1), ("rg_b_x_2", 6, 1), ("rg_lambda_2", 7, 1)]
            for name, row, count in rows:
                src = A[name][0] if count > 1 else A[name]
                sp.dma_start(rnn_rows[row * R_CHUNKS:(row + count) * R_CHUNKS, :], src.rearrange("k (c p) -> (k c) p", p=RC)).then_inc(rnn_rows_in, 16)
            gain("mix_pre_g_2", 0, True)
            w = A["rg_w_in_2"][0].rearrange("(k p) n -> p k n", p=P)
            for u in range(6):
                load(first["rnn_in"] + u, [(0, P, KC, 4 * RC, w[:, :, u * 4 * RC:(u + 1) * 4 * RC])])
            gain("mix_post_g_2", 0, False)
            w = A["rg_w_out_2"][0].rearrange("(c p) n -> p c n", p=RC)
            for u in range(3):
                load(first["rnn_out"] + u, [(0, RC, 4, D, w[:, 4 * u:4 * u + 4, :])])
            feed_forward(1)
            sp.dma_start(wf[:], A["w_fgate_2"].rearrange("(k p) n -> p k n", p=P)).then_inc(wf_in, 16)
            sp.dma_start(bf[:], A["b_fgate_2"].unsqueeze(0)).then_inc(wf_in, 16)
            gain("kv_norm_g_2", None, True)
            w = A["w_kv_2"].rearrange("(k p) n -> p k n", p=P)
            for u in range(4):
                load(first["kv"] + u, [(0, P, KC, N, w[:, :, u * N:(u + 1) * N])])
            feed_forward(2)
            gain("mix_pre_g_2", 1, True)
            w = A["attn_w_q_2"][0].rearrange("(k p) n -> p k n", p=P)
            for u in range(2):
                load(first["q"] + u, [(0, P, KC, N, w[:, :, u * N:(u + 1) * N])])
            gain("mix_post_g_2", 1, False)
            w = A["attn_w_o_2"][0].rearrange("(k p) n -> p k n", p=P)
            for u in range(2):
                load(first["o"] + u, [(0, P, 4, D, w[:, 4 * u:4 * u + 4, :])])
            feed_forward(3)
            sp.wait_ge(x_final, TILES)
            sp.sem_inc(x_final, -TILES)
            sp.dma_start(out.rearrange("o (t p) d -> p (o t) d", p=P), x[:]).then_inc(out_stored, 16)
            sp.wait_ge(out_stored, 16)

        @block.gpsimd
        def _(pool):
            g = nc.gpsimd
            build = Count()

            g.memset(zeros[:], 0.0).then_inc(const_steps, 1)
            pool.wait_ge(const_steps, build.next())
            g.memset(ones[:], 1.0).then_inc(const_steps, 1)
            pool.wait_ge(const_steps, build.next())
            g.affine_select(out=ident[:], in_=zeros[:], compare_op=ALU.not_equal, fill=1.0, base=0,
                            pattern=[[-1, P]], channel_multiplier=1).then_inc(const_steps, 1)
            pool.wait_ge(const_steps, build.next())
            g.affine_select(out=upto[:], in_=ones[:], compare_op=ALU.is_ge, fill=0.0, base=0,
                            pattern=[[1, P]], channel_multiplier=-1).then_inc(const_steps, 1)
            pool.wait_ge(const_steps, build.next())
            g.memset(window[:], 0.0).then_inc(const_steps, 1)
            pool.wait_ge(const_steps, build.next())
            g.affine_select(out=window[:, 0, P:SEQ], in_=window[:, 0, P:SEQ], compare_op=ALU.is_ge, fill=MASKED,
                            base=0, pattern=[[-1, P]], channel_multiplier=1).then_inc(const_steps, 1)
            pool.wait_ge(const_steps, build.next())
            g.affine_select(out=window[:, 1, 0:P], in_=window[:, 1, 0:P], compare_op=ALU.is_ge, fill=MASKED,
                            base=0, pattern=[[1, P]], channel_multiplier=-1).then_inc(const_steps, 1)
            pool.wait_ge(const_steps, build.next())
            g.memset(eps[:], EPS).then_inc(const_steps, 1)
            pool.wait_ge(const_steps, build.next())
            g.iota(iota16[:], pattern=[[1, TOPK]], base=0, channel_multiplier=0, allow_small_or_imprecise_dtypes=True).then_inc(const_steps, 1)
            pool.wait_ge(const_steps, build.next())
            for i in range(ROPE // 2):
                g.memset(inv_freq[:, i:i + 1], float(ROPE_THETA ** (-2.0 * i / ROPE))).then_inc(const_steps, 1)
                pool.wait_ge(const_steps, build.next())
            g.iota(pool_in[:, 0, 0:SEQ], pattern=[[1, SEQ]], base=0, channel_multiplier=0, allow_small_or_imprecise_dtypes=True).then_inc(const_steps, 1)
            pool.wait_ge(const_steps, build.next())
            for n, w in enumerate(WINDOWS):
                rows, cc = slice(HEAD * (n % 2), HEAD * (n % 2) + HEAD), n // 2
                g.tensor_scalar(pool_s[0][rows, cc, 0:SEQ], pool_in[rows, 0, 0:SEQ], float(w // 2), float(SEQ), ALU.add, ALU.min).then_inc(const_steps, 1)
                pool.wait_ge(const_steps, build.next())
                g.tensor_scalar(pool_s[1][rows, cc, 0:SEQ], pool_in[rows, 0, 0:SEQ], float(-(w // 2)), 0.0, ALU.add, ALU.max).then_inc(const_steps, 1)
                pool.wait_ge(const_steps, build.next())
            g.tensor_tensor(window_count[:], pool_s[0][:, :, 0:SEQ], pool_s[1][:, :, 0:SEQ], ALU.subtract).then_inc(const_steps, 1)
            pool.wait_ge(const_steps, build.next())
            g.memset(qTz[:], 0.0).then_inc(const_steps, 1)
            pool.wait_ge(const_steps, build.next())
            g.memset(expert_base[:], float(-EXPERTS)).then_inc(const_steps, 1)
            pool.wait_ge(const_steps, build.next())
            g.memset(pool_w[:], 0.0).then_inc(const_steps, 1)
            pool.wait_ge(const_steps, build.next())
            pool.sem_inc(const_steps, -build.reset())
            g.memset(junk[:, 0:1], 0.0).then_inc(consts, 1)
            pool.sem_inc(params_free, 1)

            steps = Count()
            with pool.Fori(0, DEPTH) as l:
                pool.wait_ge(zc_ready, 1)
                pool.sem_inc(zc_ready, -1)
                g.tensor_tensor(conv_u[:], zc[:, 4:6, :], zc[:, 0:2, :], ALU.mult).then_inc(pool_steps, 1)
                pool.wait_ge(pool_steps, steps.next())
                for cc in range(2):
                    w = [mix_cols[:, 2 * k + cc:2 * k + cc + 1] for k in range(3)]
                    g.tensor_scalar(conv_o[:, cc, :], conv_u[:, cc, :], w[1], None, ALU.mult).then_inc(pool_steps, 1)
                    pool.wait_ge(pool_steps, steps.next())
                    g.tensor_scalar(conv_t[:, cc, 1:SEQ], conv_u[:, cc, 0:SEQ - 1], w[0], None, ALU.mult).then_inc(pool_steps, 1)
                    pool.wait_ge(pool_steps, steps.next())
                    g.tensor_tensor(conv_o[:, cc, 1:SEQ], conv_o[:, cc, 1:SEQ], conv_t[:, cc, 1:SEQ], ALU.add).then_inc(pool_steps, 1)
                    pool.wait_ge(pool_steps, steps.next())
                    g.tensor_scalar(conv_t[:, cc, 0:SEQ - 1], conv_u[:, cc, 1:SEQ], w[2], None, ALU.mult).then_inc(pool_steps, 1)
                    pool.wait_ge(pool_steps, steps.next())
                    g.tensor_tensor(conv_o[:, cc, 0:SEQ - 1], conv_o[:, cc, 0:SEQ - 1], conv_t[:, cc, 0:SEQ - 1], ALU.add).then_inc(pool_steps, 1)
                    pool.wait_ge(pool_steps, steps.next())
                g.tensor_tensor(mixT[:, 4:6, :], conv_o[:], zc[:, 2:4, :], ALU.mult).then_inc(pool_steps, 1)
                pool.wait_ge(pool_steps, steps.next())
                g.memset(pool_in[:], 0.0).then_inc(pool_steps, 1)
                pool.wait_ge(pool_steps, steps.next())
                g.tensor_copy(pool_in[:, :, PAD:PAD + SEQ], zc[:, 6:8, :]).then_inc(pool_steps, 1)
                pool.wait_ge(pool_steps, steps.next())
                src, lo, hi = pool_in, 0, PADDED
                for n, w in enumerate(WINDOWS):
                    left, right = (1, 0) if w == 2 else (w // 4, w // 4)
                    dst = pool_s[n % 2]
                    lo, hi = lo + left, hi - right
                    g.tensor_tensor(dst[:, :, lo:hi], src[:, :, lo - left:hi - left], src[:, :, lo + right:hi + right], ALU.add).then_inc(pool_steps, 1)
                    pool.wait_ge(pool_steps, steps.next())
                    src = dst
                    rows, cc = slice(HEAD * (n % 2), HEAD * (n % 2) + HEAD), n // 2
                    g.tensor_tensor(pooled[rows, cc, :], src[rows, cc, PAD:PAD + SEQ], window_count[rows, cc, :], ALU.mult).then_inc(pool_steps, 1)
                    pool.wait_ge(pool_steps, steps.next())
                pool.sem_inc(pool_steps, -steps.reset())
                g.tensor_tensor(pooled[:], pooled[:], zc[:, 6:8, :], ALU.subtract).then_inc(pooled_ready, 1)

                with pool.Fori(0, UNITS // 2) as n2:
                    for p in range(2):
                        pool.wait_ge(expert_ready, 1)
                        pool.sem_inc(expert_ready, -1)
                        for half in range(TOPK // GRP):
                            for j in range(GRP):
                                k = half * GRP + j
                                pool.wait_ge(u_free, 1)
                                pool.sem_inc(u_free, -1)
                                g.indirect_dma_start(u_ring[:, k % U_SLOTS, :], None, A["peer_u"],
                                                     bass.IndirectOffsetOnAxis(expert[:, p, k:k + 1], 0)).then_inc(u_in[k % U_SLOTS], 16)
                            for j in range(GRP):
                                k = half * GRP + j
                                pool.wait_ge(v_free, 1)
                                pool.sem_inc(v_free, -1)
                                g.indirect_dma_start(v_ring[:, k, :], None, A["peer_v"],
                                                     bass.IndirectOffsetOnAxis(expert[:, p, k:k + 1], 0)).then_inc(v_in[k], 16)

            pool.wait_ge(block1_done, 1)
            pool.sem_inc(block1_done, -1)
            g.memset(w_gates[0], 0.0).then_inc(pool_steps, 1)
            pool.wait_ge(pool_steps, steps.next())
            g.memset(w_gates[1], 0.0).then_inc(pool_steps, 1)
            pool.wait_ge(pool_steps, steps.next())
            g.memset(rec_in[:, :, 0:CONV_K - 1], 0.0).then_inc(pool_steps, 1)
            pool.wait_ge(pool_steps, steps.next())
            pool.sem_inc(rnn_zeroed, 1)
            for which, name in enumerate(("rg_w_a_2", "rg_w_x_2")):
                src = A[name][0].rearrange("(s b) i d -> b i s d", b=SUPER)
                for b in range(SUPER):
                    lo = b * LRU
                    while lo < (b + 1) * LRU:
                        hi = min((b + 1) * LRU, (lo // RC + 1) * RC)
                        pool.dma_start(w_gates[which][lo % RC:lo % RC + hi - lo, :, lo // RC, b * LRU:(b + 1) * LRU],
                                       src[b, lo - b * LRU:hi - b * LRU]).then_inc(rnn_w_in, 16)
                        lo = hi
            pool.sem_inc(pool_steps, -steps.reset())
            pool.wait_ge(rnn_over, 1)
            pool.sem_inc(rnn_over, -1)
            g.memset(qTz2, 0.0).then_inc(pool_steps, 1)
            pool.wait_ge(pool_steps, steps.next())
            g.memset(c_pad, 0.0).then_inc(pool_steps, 1)
            pool.wait_ge(pool_steps, steps.next())
            g.memset(head_pick, 1.0).then_inc(pool_steps, 1)
            pool.wait_ge(pool_steps, steps.next())
            g.affine_select(out=head_pick, in_=head_pick, compare_op=ALU.is_equal, fill=0.0, base=0,
                            pattern=[[-1, HEADS2], [0, P]], channel_multiplier=1).then_inc(heads_zeroed, 1)
            pool.sem_inc(pool_steps, -steps.reset())

        @block.scalar
        def _(act):
            a = nc.scalar
            steps = Count()
            act.wait_ge(consts, 1)
            act.sem_inc(job_taken, 4)
            act.wait_ge(c_turned, 1)
            act.sem_inc(c_turned, -1)
            a.activation(c_act[:], ps[:, 0, 0:KC], ACT.Silu).then_inc(c_act_ready, 1)
            act.wait_ge(angle_ready, 1)
            act.sem_inc(angle_ready, -1)
            a.activation(sine[:], angle[:, 2], ACT.Sin)
            a.activation(cosine[:], angle[:, 3], ACT.Sin).then_inc(rope_ready, 1)

            def mean_square(source, ready, give):
                for t in range(TILES):
                    if ready is not None:
                        act.wait_ge(ready, 1)
                        act.sem_inc(ready, -1)
                    a.activation(junk, source(t), ACT.Square, accum_out=mean_sq[:, t:t + 1]).then_inc(act_steps, 1)
                    act.wait_ge(act_steps, steps.next())
                a.activation(rms[:], mean_sq[:], ACT.Sqrt, bias=eps[:], scale=1.0 / D).then_inc(give, 1)
                act.sem_inc(act_steps, -steps.reset())

            def norm_x():
                mean_square(lambda t: x[:, t, :], x_ready, rms_ready)

            def acc_rows(t):
                return ps[:, 2 * t:2 * t + 2, :].rearrange("p b n -> p (b n)")

            def norm_acc():
                act.wait_ge(rows_done, 1)
                act.sem_inc(rows_done, -1)
                act.sem_inc(slot_free, 1)
                mean_square(acc_rows, None, rms2_ready)

            def evacuate_hT():
                for t in range(TILES):
                    for half in range(2):
                        act.wait_ge(hT_turned, 1)
                        act.sem_inc(hT_turned, -1)
                        a.activation(hT[:, 4 * half:4 * half + 4, t * P:(t + 1) * P],
                                     ps[:, WORK + 2 * t + half, :].rearrange("p (k t) -> p k t", t=P), ACT.Copy).then_inc(hT_ready, 1)

            def bank(j):
                return WORK + j % 4

            def softmax_exps(n_units, S, sinks):
                units = attention_units(not sinks)
                for u in range(n_units):
                    b = u % 2
                    keys = SEQ if sinks else P * (units[u][0] + 1)
                    act.wait_ge(scores_ready, 1)
                    act.sem_inc(scores_ready, -1)
                    if sinks:
                        a.activation(sink_e[:, b, :], sink_d[:, b, :], ACT.Exp)
                    for i in range(GROUP):
                        ins = a.activation(S[:, b, i, 0:keys], S[:, b, i, 0:keys], ACT.Exp, bias=neg_max[:, b, i:i + 1],
                                           accum_out=row_sum[:, b, i:i + 1])
                    ins.then_inc(probs_ready, 1)
                    fan(act, sums_ready)
                    turned = pT if sinks else pT2
                    for half in range(2):
                        act.wait_ge(p_turned, 1)
                        act.sem_inc(p_turned, -1)
                        a.activation(turned[:, 4 * half:4 * half + 4, :], ps[:, half, :].rearrange("p (i t) -> p i t", t=P),
                                     ACT.Copy).then_inc(pT_ready, 1)

            with act.Fori(0, DEPTH) as l:
                norm_x()
                act.wait_ge(params_turned, 1)
                act.sem_inc(params_turned, -1)
                a.activation(mix_cols[:], ps[:, 0, 0:8], ACT.Copy)
                a.activation(keysT[:].rearrange("p s k -> p (s k)"), ps[:, 1, 0:2 * KEYS], ACT.Copy)
                with act.Fori(0, 3) as i:
                    for u in range(4):
                        act.wait_ge(job_done, 1)
                        act.sem_inc(job_done, -1)
                        act.sem_inc(slot_free, 1)
                        a.activation(mod.rearrange("p s d -> p (s d)")[:, bass.ds(i * (4 * N) + u * N, N)], ps[:, bank(u), :],
                                     ACT.Copy).then_inc(job_taken, 1)
                fan(act, mod_ready)
                evacuate_hT()
                for t in range(TILES):
                    act.wait_ge(job_done, 1)
                    act.sem_inc(job_done, -1)
                    a.activation(qk[:, t, 0:Q_HEADS, :].rearrange("p (c g) d -> p g c d", g=KV_HEADS),
                                 ps[:, bank(t), :].rearrange("p (g c d) -> p g c d", g=KV_HEADS, d=HEAD), ACT.Copy).then_inc(job_taken, 1)
                act.sem_inc(slot_free, 1)
                for t in range(TILES):
                    act.wait_ge(job_done, 1)
                    act.sem_inc(job_done, -1)
                    a.activation(qk[:, t, Q_HEADS:QK, :].rearrange("p h d -> p (h d)"), ps[:, bank(2 + t), 0:KV_W], ACT.Copy)
                    a.activation(v_tok[:, t, :], ps[:, bank(2 + t), KV_W:2 * KV_W], ACT.Copy).then_inc(job_taken, 1)
                act.sem_inc(slot_free, 1)
                fan(act, qk_ready)
                for j in range(8):
                    act.wait_ge(job_done, 1)
                    act.sem_inc(job_done, -1)
                    if j % 4 == 3:
                        act.sem_inc(slot_free, 1)
                    a.activation(zc[:, j, :], ps[:, bank(j), 0:SEQ], ACT.Copy).then_inc(job_taken, 1)
                fan(act, zc_ready)
                act.wait_ge(head_sq_ready, 1)
                act.sem_inc(head_sq_ready, -1)
                a.activation(head_rms[:], head_sq[:], ACT.Sqrt, bias=eps[:], scale=1.0 / HEAD).then_inc(head_rms_ready, 1)
                for t in range(TILES):
                    act.wait_ge(qk_turned, 1)
                    act.sem_inc(qk_turned, -1)
                    for s in range(KV_HEADS):
                        rows = slice(HEAD * s, HEAD * s + HEAD)
                        a.activation(qTz[rows, GROUP * s:GROUP * s + GROUP, t * P:(t + 1) * P],
                                     ps[rows, WORK + t, :].rearrange("p (c t) -> p c t", t=P), ACT.Copy, scale=HEAD ** -0.5)
                act.wait_ge(qk_turned, 1)
                act.sem_inc(qk_turned, -1)
                a.activation(kT, ps[:, WORK + 2, 0:SEQ], ACT.Copy).then_inc(qkT_ready, 1)
                softmax_exps(TILES * KV_HEADS, scores, True)
                act.wait_ge(pool_done, 1)
                act.sem_inc(pool_done, -1)
                for cc in range(2):
                    a.activation(mixT[:, 6 + cc, :], ps[:, WORK + 2, cc * SEQ:(cc + 1) * SEQ], ACT.Copy, scale=mix_cols[:, 6 + cc:7 + cc])
                for t in range(TILES):
                    act.wait_ge(attn_turned, 1)
                    act.sem_inc(attn_turned, -1)
                    a.activation(mixT[:, 0:4, t * P:(t + 1) * P], ps[:, WORK + t, :].rearrange("p (c t) -> p c t", t=P),
                                 ACT.Copy).then_inc(mixT_ready, 1)
                norm_x()
                evacuate_hT()
                for j in range(16):
                    act.wait_ge(job_done, 1)
                    act.sem_inc(job_done, -1)
                    a.activation(qpT[:, j, :], ps[:, bank(j), 0:SEQ], ACT.Copy).then_inc(job_taken, 1)
                for j in range(8):
                    act.wait_ge(key_s_done, 1)
                    act.sem_inc(key_s_done, -1)
                    a.activation(key_s[:, 2 * j:2 * j + 2, :, :].rearrange("p n h k -> p (n h k)"), ps[:, j, :], ACT.Copy).then_inc(key_s_ready, 1)

                def gate_exp(p):
                    act.wait_ge(top_ready, 1)
                    act.sem_inc(top_ready, -1)
                    a.activation(gate_e[:, p, :], top[:, p, :], ACT.Exp, bias=neg_top[:, p, :], accum_out=gate_sum[:, p, :]).then_inc(gate_ready, 1)

                def gelu(half):
                    act.wait_ge(dots_ready, 1)
                    act.sem_inc(dots_ready, -1)
                    a.activation(acts[:, half, :], dots[:, half, :], ACT.Gelu).then_inc(acts_ready, 1)

                gate_exp(0)
                with act.Fori(0, UNITS // 2 - 1) as n2:
                    for p in range(2):
                        gelu(0)
                        gate_exp(1 - p)
                        gelu(1)
                gelu(0)
                gate_exp(1)
                gelu(1)
                gelu(0)
                gelu(1)

            def feed_forward():
                norm_x()
                evacuate_hT()
                with act.Fori(0, FF_CHUNKS // 2) as i:
                    for b in range(2):
                        act.wait_ge(gu_done, 1)
                        act.sem_inc(gu_done, -1)
                        a.activation(silu_g[:, b, :], ps[:, WORK + b, 0:SEQ], ACT.Silu).then_inc(silu_ready, 1)
                norm_acc()

            feed_forward()
            norm_x()
            evacuate_hT()
            act.wait_ge(rnn_turned, 1)
            act.sem_inc(rnn_turned, -1)
            a.activation(rnn_cols[:].rearrange("p k c -> p (k c)"), ps[0:RC, 0, 0:8 * R_CHUNKS], ACT.Copy).then_inc(rnn_cols_ready, 1)
            job = 0
            for j in range(R_CHUNKS):
                act.wait_ge(job_done, 1)
                act.sem_inc(job_done, -1)
                if j % 4 == 3:
                    act.sem_inc(slot_free, 1)
                a.activation(gate_g[:, j, :], ps[0:RC, bank(job), 0:SEQ], ACT.Gelu_apprx_tanh).then_inc(job_taken, 1)
                job += 1
            act.wait_ge(lam_abs, 1)
            act.sem_inc(lam_abs, -1)
            a.activation(decay[:, 1, :], decay[:, 0, :], ACT.Exp, scale=-1.0).then_inc(lam_exp, 1)
            for j in range(R_CHUNKS):
                act.wait_ge(job_done, 1)
                act.sem_inc(job_done, -1)
                if j % 4 == 3:
                    act.sem_inc(slot_free, 1)
                a.activation(rec_in[:, j, CONV_K - 1:], ps[0:RC, bank(job), 0:SEQ], ACT.Copy).then_inc(job_taken, 1)
                job += 1
                if j % 3 == 2:
                    fan(act, rec_in_ready)
            for s in range(SUPER):
                for dst, row in ((gate_r, 5), (gate_i, 6)):
                    for jj in range(3):
                        j = 3 * s + jj
                        act.wait_ge(job_done, 1)
                        act.sem_inc(job_done, -1)
                        a.activation(dst[:, j, :], ps[0:RC, bank(job), 0:SEQ], ACT.Sigmoid, bias=rnn_cols[:, row, j:j + 1]).then_inc(job_taken, 1)
                        job += 1
            act.wait_ge(decay_ready, 1)
            act.sem_inc(decay_ready, -1)
            act.wait_ge(job_taken, 4)
            for j in range(R_CHUNKS):
                a.activation(decay_a[:, j, :], gate_r[:, j, :], ACT.Exp, scale=decay_neg[:, j:j + 1]).then_inc(act_steps, 1)
            steps.value += R_CHUNKS
            act.wait_ge(act_steps, steps.value)
            for s in range(SUPER):
                for j in range(3 * s, 3 * s + 3):
                    ins = a.activation(gate_r[:, j, :], gate_r[:, j, :], ACT.Tanh, scale=decay_pos[:, j:j + 1])
                ins.then_inc(gates_ready, 1)
            act.sem_inc(act_steps, -steps.reset())
            for s in range(SUPER):
                act.wait_ge(root_in, 1)
                act.sem_inc(root_in, -1)
                part = gate_r[:, 3 * s:3 * s + 3, :]
                a.activation(part, part, ACT.Sqrt).then_inc(root_ready, 1)
            norm_acc()
            feed_forward()
            norm_x()
            evacuate_hT()
            for j in range(8):
                act.wait_ge(job_done, 1)
                act.sem_inc(job_done, -1)
                if j % 4 == 3:
                    act.sem_inc(slot_free, 1)
                a.activation(kT2[:, j, :], ps[:, bank(j), 0:SEQ], ACT.Copy).then_inc(job_taken, 1)
            for b in range(2):
                for t in range(TILES):
                    act.wait_ge(job_done, 1)
                    act.sem_inc(job_done, -1)
                    if t == 1:
                        act.sem_inc(slot_free, 1)
                    a.activation(v2[:, t, b * N:(b + 1) * N], ps[:, bank(2 * b + t), :], ACT.Copy).then_inc(job_taken, 1)
            act.wait_ge(job_done, 1)
            act.sem_inc(job_done, -1)
            a.activation(f_tok[:], ps[:, bank(0), 0:TILES * HEADS2], ACT.Copy).then_inc(job_taken, 1)
            fan(act, f_ready)
            act.wait_ge(f_abs, 1)
            act.sem_inc(f_abs, -1)
            a.activation(logs[:, 1, :], logs[:, 0, :], ACT.Exp, scale=-1.0).then_inc(f_exp, 1)
            act.wait_ge(c_summed, 1)
            act.sem_inc(c_summed, -1)
            a.activation(c_tok[:], ps[:, 0, 0:TILES * HEADS2], ACT.Copy)
            act.wait_ge(heads_zeroed, 1)
            a.activation(c_pad[:, :, 0:HEADS2], ps[:, 0, 0:TILES * HEADS2].rearrange("p (t h) -> p t h", t=TILES), ACT.Copy,
                         scale=-1.0).then_inc(c_ready, 1)
            act.wait_ge(c_back, 1)
            act.sem_inc(c_back, -1)
            a.activation(neg_cT, ps[:, 1, 0:SEQ], ACT.Copy).then_inc(neg_cT_ready, 1)
            feed_forward()
            norm_x()
            evacuate_hT()
            for j in range(8):
                act.wait_ge(job_done, 1)
                act.sem_inc(job_done, -1)
                if j % 4 == 3:
                    act.sem_inc(slot_free, 1)
                for s in range(2):
                    rows = slice(HEAD * s, HEAD * s + HEAD)
                    ins = a.activation(qTz2[rows, 2 * j + s, :], ps[rows, bank(j), 0:SEQ], ACT.Copy, scale=HEAD ** -0.5)
                ins.then_inc(job_taken, 1)
            softmax_exps(TILES * HEADS2 // GROUP, scores2, False)
            evacuate_hT()
            norm_acc()
            feed_forward()

        @block.tensor
        def _(pe):
            mm = nc.tensor.matmul
            pe.sem_inc(slot_free, SLOTS)
            pe.wait_ge(consts, 1)
            pe.wait_ge(c_loaded, 16)
            pe.sem_inc(c_loaded, -16)
            nc.tensor.transpose(ps[:, 0, 0:KC], c_rows[:], ident[0:KC, 0:KC]).then_inc(c_turned, 1)
            pe.wait_ge(pos_float, 1)
            pe.sem_inc(pos_float, -1)
            nc.tensor.transpose(ps[:, 1, 0:TILES], pos_f[:], ident[0:TILES, 0:TILES]).then_inc(pos_turned, 1)
            pe.wait_ge(c_wide_ready, 1)
            pe.sem_inc(c_wide_ready, -1)

            def bank(j):
                return WORK + j % 4

            def turn_h():
                for t in range(TILES):
                    pe.wait_ge(h_ready, 1)
                    pe.sem_inc(h_ready, -1)
                    for half in range(2):
                        for k in range(4):
                            ins = nc.tensor.transpose(ps[:, WORK + 2 * t + half, k * P:(k + 1) * P],
                                                      h[:, t, (4 * half + k) * P:(4 * half + k + 1) * P], ident[:])
                        ins.then_inc(hT_turned, 1)
                pe.wait_ge(hT_ready, 4)
                pe.sem_inc(hT_ready, -4)

            def weights(n, dmas=1):
                pe.wait_ge(slot_in[n % SLOTS], 16 * dmas)
                pe.sem_inc(slot_in[n % SLOTS], -16 * dmas)
                return ring[:, n % SLOTS, :]

            def channel_job(j, w, width, col, m):
                pe.wait_ge(job_taken, 1)
                pe.sem_inc(job_taken, -1)
                wk = w[:, 0:KC * width].rearrange("p (k n) -> p k n", k=KC)
                for k in range(KC):
                    ins = mm(ps[0:m, bank(j), 0:SEQ], wk[:, k, col:col + m], hT[:, k, :], start=(k == 0), stop=(k == KC - 1))
                ins.then_inc(job_done, 1)

            def token_job(j, w, width, t):
                pe.wait_ge(job_taken, 1)
                pe.sem_inc(job_taken, -1)
                wk = w[:, 0:KC * width].rearrange("p (k n) -> p k n", k=KC)
                for k in range(KC):
                    ins = mm(ps[:, bank(j), 0:width], hT[:, k, t * P:(t + 1) * P], wk[:, k, :], start=(k == 0), stop=(k == KC - 1))
                ins.then_inc(job_done, 1)

            def accumulate_rows(source, w, start, stop):
                for t in range(TILES):
                    for c in range(2):
                        ins = mm(ps[:, 2 * t + c, :], source[:, t * P:(t + 1) * P], w[:, c * N:(c + 1) * N], start=start, stop=stop)
                return ins

            def row_product(n, count, sources, rows):
                per = len(sources) // count
                for u in range(count):
                    w = weights(n + u)[0:rows].rearrange("p (k n) -> p k n", n=D)
                    for k in range(per):
                        i = u * per + k
                        ins = accumulate_rows(sources[i], w[:, k, :], i == 0, i == len(sources) - 1)
                    ins.then_inc(slot_free if u < count - 1 else rows_done, 1)

            def attend(second):
                units = attention_units(second)
                queries, keys_of, turned = (qTz2, lambda i: kT2[:, i // 2, :], pT2) if second else (qTz, lambda i: kT, pT)
                S = scores2 if second else scores

                def score(u):
                    t, heads = units[u]
                    n = P * (t + 1) if second else SEQ
                    for i, head in enumerate(heads):
                        where = ps[:, WORK + 2 * (u % 2) + i // 2, (i % 2) * SEQ:(i % 2) * SEQ + n]
                        ins = mm(where, queries[:, head, t * P:(t + 1) * P], keys_of(head)[:, 0:n], start=True, stop=not second)
                        if second:
                            ins = mm(where, head_pick[:, head, :], neg_cT[:, 0:n], start=False, stop=True)
                    ins.then_inc(scores_done, 1)

                score(0)
                for u, (t, heads) in enumerate(units):
                    if u + 1 < len(units):
                        score(u + 1)
                    chunks = t + 1 if second else TILES
                    pe.wait_ge(probs_ready, 1)
                    pe.sem_inc(probs_ready, -1)
                    for half in range(2):
                        for i in range(2 * half, 2 * half + 2):
                            for k in range(TILES):
                                src = min(k, chunks - 1)
                                ins = nc.tensor.transpose(ps[:, half, ((2 * i + k) % 4) * P:((2 * i + k) % 4 + 1) * P],
                                                          S[:, u % 2, i, src * P:(src + 1) * P], ident[:])
                        ins.then_inc(p_turned, 1)
                    pe.wait_ge(pT_ready, 2)
                    pe.sem_inc(pT_ready, -2)
                    if u >= 2:
                        pe.wait_ge(attn_done, 1)
                        pe.sem_inc(attn_done, -1)
                    for i, head in enumerate(heads):
                        for k in range(chunks):
                            values = v2[:, k, head * HEAD:(head + 1) * HEAD] if second else \
                                v_tok[:, k, (head // GROUP) * HEAD:(head // GROUP + 1) * HEAD]
                            ins = mm(ps[:, 2 + u % 2, i * HEAD:(i + 1) * HEAD], turned[:, 2 * i + k, :], values,
                                     start=(k == 0), stop=(k == chunks - 1))
                    ins.then_inc(pv_done, 1)
                pe.wait_ge(attn_done, 2)
                pe.sem_inc(attn_done, -2)

            with pe.Fori(0, DEPTH) as l:
                pe.wait_ge(pe_params, 5 * 16)
                pe.sem_inc(pe_params, -5 * 16)
                nc.tensor.transpose(ps[:, 0, 0:8], mix_rows[:], ident[0:8, 0:8])
                for s in range(2):
                    ins = nc.tensor.transpose(ps[:, 1, s * KEYS:(s + 1) * KEYS], keys_raw[:, s, :], ident[:])
                ins.then_inc(params_turned, 1)
                pe.wait_ge(bias_in, 16)
                pe.sem_inc(bias_in, -16)
                with pe.Fori(0, 3) as i:
                    for u in range(4):
                        w = weights(u).rearrange("p (k n) -> p k n", k=KC)
                        pe.wait_ge(job_taken, 1)
                        pe.sem_inc(job_taken, -1)
                        mm(ps[:, bank(u), :], ident[0:4, u:u + 1].to_broadcast([4, P]), ada_bias[:, bass.ds(i * N, N)], start=True, stop=False)
                        for k in range(KC):
                            ins = mm(ps[:, bank(u), :], c_wide[:, k, :], w[:, k, :], start=False, stop=(k == KC - 1))
                        ins.then_inc(job_done, 1)
                turn_h()
                w = weights(0)
                for t in range(TILES):
                    token_job(t, w, N, t)
                w = weights(1)
                for t in range(TILES):
                    token_job(2 + t, w, 2 * KV_W, t)
                for b in range(2):
                    w = weights(2 + b)
                    for c in range(4):
                        channel_job(4 * b + c, w, N, c * P, P)
                pe.wait_ge(qk_done, 1)
                pe.sem_inc(qk_done, -1)
                pe.wait_ge(job_taken, 4)
                for t in range(TILES):
                    for c in range(4):
                        ins = nc.tensor.transpose(ps[:, WORK + t, c * P:(c + 1) * P],
                                                  qk[:, t, 2 * c:2 * c + 2, :].rearrange("p h d -> p (h d)"), ident[:])
                    ins.then_inc(qk_turned, 1)
                for t in range(TILES):
                    ins = nc.tensor.transpose(ps[:, WORK + 2, t * P:(t + 1) * P],
                                              qk[:, t, Q_HEADS:QK, :].rearrange("p h d -> p (h d)"), ident[:])
                ins.then_inc(qk_turned, 1)
                pe.wait_ge(qkT_ready, 1)
                pe.sem_inc(qkT_ready, -1)
                attend(False)
                pe.wait_ge(pooled_ready, 1)
                pe.sem_inc(pooled_ready, -1)
                for cc in range(2):
                    ins = mm(ps[:, WORK + 2, cc * SEQ:(cc + 1) * SEQ], pool_w[:, cc, :], pooled[:, cc, :], start=True, stop=True)
                ins.then_inc(pool_done, 1)
                for t in range(TILES):
                    for c in range(4):
                        ins = nc.tensor.transpose(ps[:, WORK + t, c * P:(c + 1) * P], attn[:, t, c * P:(c + 1) * P], ident[:])
                    ins.then_inc(attn_turned, 1)
                pe.wait_ge(mixT_ready, TILES)
                pe.sem_inc(mixT_ready, -TILES)
                row_product(0, 4, [mixT[:, k, :] for k in range(KC)], P)
                turn_h()
                for b in range(4):
                    w = weights(b)
                    for c in range(4):
                        channel_job(4 * b + c, w, N, c * P, P)
                pe.wait_ge(job_taken, 4)
                for t in range(TILES):
                    for j in range(4):
                        for i in range(4):
                            c = 4 * j + i
                            ins = mm(ps[:, 4 * t + j, i * KEYS:(i + 1) * KEYS], qpT[:, c, t * P:(t + 1) * P], keysT[:, c % 2, :],
                                     start=True, stop=True)
                        ins.then_inc(key_s_done, 1)
                pe.wait_ge(diag_ready, 1)
                for b in range(4):
                    mm(ps[:, b, :], zeros[:], h[:, 0, 0:N], start=True, stop=False, skip_group_check=True)
                for t in range(TILES):
                    with pe.Fori(0, EXPERT_HEADS // 2) as i:
                        for p in range(2):
                            for k in range(TOPK):
                                pe.wait_ge(diag_ready, 1)
                                pe.sem_inc(diag_ready, -1)
                                pe.wait_ge(v_in[k], (l * UNITS + (i * 2 + (t * EXPERT_HEADS + p + 1))) * 16)
                                for c in range(2):
                                    ins = mm(ps[:, 2 * t + c, :], diag[:, k, :], v_ring[:, k, c * N:(c + 1) * N],
                                             start=False, stop=False, skip_group_check=True)
                                ins.then_inc(v_free, 1)
                                if k % GRP == GRP - 1:
                                    fan(pe, diag_free)
                fan(pe, y_ready)

            def feed_forward(f):
                turn_h()
                n0 = first[f"ff{f}"]

                def gate_up(n, b):
                    w = weights(n, 3).rearrange("p (k m) -> p k m", m=P)
                    for g in range(2):
                        for k in range(KC):
                            ins = mm(ps[:, WORK + b, g * SEQ:(g + 1) * SEQ], w[:, g * KC + k, :], hT[:, k, :], start=(k == 0), stop=(k == KC - 1))
                    ins.then_inc(gu_done, 1)

                def down(n, b, start=False, stop=False):
                    pe.wait_ge(ff_ready, 1)
                    pe.sem_inc(ff_ready, -1)
                    ins = accumulate_rows(ff_a[:, b, :], ring[:, n % SLOTS, 2 * KC * P:2 * KC * P + D], start, stop)
                    ins.then_inc(rows_done if stop else slot_free, 1)

                gate_up(n0, 0)
                for j in range(1, PEEL):
                    gate_up(n0 + j, j % 2)
                    down(n0 + j - 1, (j - 1) % 2, start=(j == 1))
                with pe.Fori(0, TURNS) as i:
                    for u in range(SLOTS):
                        gate_up(n0 + PEEL + u, (PEEL + u) % 2)
                        down(n0 + PEEL + u - 1, (PEEL + u - 1) % 2)
                down(n0 + FF_CHUNKS - 1, (FF_CHUNKS - 1) % 2, stop=True)

            feed_forward(0)
            turn_h()
            pe.wait_ge(rnn_rows_in, 5 * 16)
            pe.sem_inc(rnn_rows_in, -5 * 16)
            nc.tensor.transpose(ps[0:RC, 0, 0:8 * R_CHUNKS], rnn_rows[:], ident[0:8 * R_CHUNKS, 0:8 * R_CHUNKS]).then_inc(rnn_turned, 1)
            job = 0
            for b in range(6):
                w = weights(first["rnn_in"] + b)
                for c in range(4):
                    channel_job(job, w, 4 * RC, c * RC, RC)
                    job += 1
            pe.wait_ge(rnn_w_in, 2 * 6 * 16)
            for s in range(SUPER):
                pe.wait_ge(rec_ready, 1)
                pe.sem_inc(rec_ready, -1)
                for which in range(2):
                    for jj in range(3):
                        pe.wait_ge(job_taken, 1)
                        pe.sem_inc(job_taken, -1)
                        near = [i for i in range(3) if abs(i - jj) <= 1]
                        for i in near:
                            ins = mm(ps[0:RC, bank(job), 0:SEQ], w_gates[which][:, s, i, jj * RC:(jj + 1) * RC], rec[:, 3 * s + i, :],
                                     start=(i == near[0]), stop=(i == near[-1]))
                        ins.then_inc(job_done, 1)
                        job += 1
            pe.wait_ge(rnn_out_ready, 1)
            pe.sem_inc(rnn_out_ready, -1)
            row_product(first["rnn_out"], 3, [gate_g[:, j, :] for j in range(R_CHUNKS)], RC)
            feed_forward(1)
            turn_h()
            for b in range(2):
                w = weights(first["kv"] + b)
                for c in range(4):
                    channel_job(4 * b + c, w, N, c * P, P)
            for b in range(2):
                w = weights(first["kv"] + 2 + b)
                for t in range(TILES):
                    token_job(2 * b + t, w, N, t)
            pe.wait_ge(wf_in, 32)
            pe.sem_inc(wf_in, -32)
            pe.wait_ge(job_taken, 1)
            pe.sem_inc(job_taken, -1)
            for t in range(TILES):
                where = ps[:, bank(0), t * HEADS2:(t + 1) * HEADS2]
                for k in range(KC):
                    mm(where, hT[:, k, t * P:(t + 1) * P], wf[:, k, :], start=(k == 0), stop=False)
                ins = mm(where, ones[0:1, :], bf[:], start=False, stop=True)
            ins.then_inc(job_done, 1)
            pe.wait_ge(log_f_ready, 1)
            pe.sem_inc(log_f_ready, -1)
            mm(ps[:, 0, 0:HEADS2], upto[:], log_f[:, 0:HEADS2], start=True, stop=True)
            mm(ps[:, 0, HEADS2:2 * HEADS2], ones[:], log_f[:, 0:HEADS2], start=True, stop=False)
            mm(ps[:, 0, HEADS2:2 * HEADS2], upto[:], log_f[:, HEADS2:2 * HEADS2], start=False, stop=True).then_inc(c_summed, 1)
            pe.wait_ge(c_ready, 1)
            pe.sem_inc(c_ready, -1)
            for t in range(TILES):
                ins = nc.tensor.transpose(ps[:, 1, t * P:(t + 1) * P], c_pad[:, t, :], ident[:])
            ins.then_inc(c_back, 1)
            pe.wait_ge(neg_cT_ready, 1)
            pe.sem_inc(neg_cT_ready, -1)
            feed_forward(2)
            turn_h()
            for b in range(2):
                w = weights(first["q"] + b)
                for c in range(4):
                    channel_job(4 * b + c, w, N, c * P, P)
            pe.wait_ge(job_taken, 4)
            attend(True)
            turn_h()
            row_product(first["o"], 2, [hT[:, k, :] for k in range(KC)], P)
            feed_forward(3)

        @block.vector
        def _(dve):
            v = nc.vector
            steps = Count()
            dve.wait_ge(consts, 1)
            dve.sem_inc(pre_free, 1)
            dve.sem_inc(post_free, 1)
            dve.sem_inc(u_free, U_SLOTS)
            dve.sem_inc(v_free, V_SLOTS)
            dve.sem_inc(diag_free, 2)
            dve.wait_ge(pos_loaded, 16)
            dve.sem_inc(pos_loaded, -16)
            v.tensor_copy(pos_f[:], pos_i[:]).then_inc(pos_float, 1)
            v.reciprocal(window_count[:], window_count[:]).then_inc(dve_steps, 1)
            dve.wait_ge(dve_steps, steps.next())
            dve.wait_ge(pos_turned, 1)
            dve.sem_inc(pos_turned, -1)
            v.tensor_copy(pos[:], ps[:, 1, 0:TILES]).then_inc(dve_steps, 1)
            dve.wait_ge(dve_steps, steps.next())
            two_pi = 2.0 * np.pi
            part1 = 6.28125
            part2 = float(np.float32(np.round((two_pi - part1) * 2.0 ** 21) / 2.0 ** 21))
            part3 = float(np.float32(two_pi - part1 - part2))
            near = 1.5 * 2.0 ** 23
            pi = float(np.nextafter(np.float32(np.pi), np.float32(0.0)))
            half = ROPE // 2
            for t in range(TILES):
                v.tensor_scalar(angle[:, 0, t, :], inv_freq[:], pos[:, t:t + 1], None, ALU.mult).then_inc(dve_steps, 1)
                dve.wait_ge(dve_steps, steps.next())
            v.tensor_scalar(angle[:, 1], angle[:, 0], float(1.0 / two_pi), None, ALU.mult).then_inc(dve_steps, 1)
            dve.wait_ge(dve_steps, steps.next())
            v.tensor_scalar(angle[:, 1], angle[:, 1], near, None, ALU.add).then_inc(dve_steps, 1)
            dve.wait_ge(dve_steps, steps.next())
            v.tensor_scalar(angle[:, 1], angle[:, 1], near, None, ALU.subtract).then_inc(dve_steps, 1)
            dve.wait_ge(dve_steps, steps.next())
            for part in (part1, part2, part3):
                v.scalar_tensor_tensor(angle[:, 0], angle[:, 1], -part, angle[:, 0], ALU.mult, ALU.add).then_inc(dve_steps, 1)
                dve.wait_ge(dve_steps, steps.next())
            v.tensor_scalar(angle[:, 2], angle[:, 0], pi, -pi, ALU.min, ALU.max).then_inc(dve_steps, 1)
            dve.wait_ge(dve_steps, steps.next())
            v.tensor_scalar(angle[:, 3], angle[:, 2], float(np.pi / 2), None, ALU.add).then_inc(dve_steps, 1)
            dve.wait_ge(dve_steps, steps.next())
            v.tensor_scalar(angle[:, 1], angle[:, 3], pi, None, ALU.is_gt).then_inc(dve_steps, 1)
            dve.wait_ge(dve_steps, steps.next())
            v.scalar_tensor_tensor(angle[:, 3], angle[:, 1], -two_pi, angle[:, 3], ALU.mult, ALU.add).then_inc(dve_steps, 1)
            dve.wait_ge(dve_steps, steps.next())
            v.tensor_scalar(angle[:, 3], angle[:, 3], pi, -pi, ALU.min, ALU.max).then_inc(angle_ready, 1)
            dve.wait_ge(c_act_ready, 1)
            dve.sem_inc(c_act_ready, -1)
            v.tensor_copy(c_wide[:], c_act[:].unsqueeze(2).to_broadcast([P, KC, P])).then_inc(c_wide_ready, 1)
            dve.wait_ge(rope_ready, 1)
            dve.sem_inc(rope_ready, -1)
            dve.wait_ge(x_loaded, 16)
            dve.sem_inc(x_loaded, -16)
            dve.sem_inc(x_ready, TILES)
            dve.sem_inc(dve_steps, -steps.reset())

            def normalise(scale, shift):
                dve.wait_ge(rms_ready, 1)
                dve.sem_inc(rms_ready, -1)
                v.reciprocal(rstd[:], rms[:]).then_inc(dve_steps, 1)
                dve.wait_ge(dve_steps, steps.next())
                for t in range(TILES):
                    ins = v.scalar_tensor_tensor(h[:, t, :], x[:, t, :], rstd[:, t:t + 1], scale, ALU.mult, ALU.mult)
                    if shift is not None:
                        ins.then_inc(dve_steps, 1)
                        dve.wait_ge(dve_steps, steps.next())
                        ins = v.tensor_tensor(h[:, t, :], h[:, t, :], shift, ALU.add)
                    ins.then_inc(h_ready, 1)

            def acc_rows(t):
                return ps[:, 2 * t:2 * t + 2, :].rearrange("p b n -> p (b n)")

            def add_gated(segment):
                for t in range(TILES):
                    v.tensor_tensor(h[:, t, :], acc_rows(t), mod[:, segment, :], ALU.mult).then_inc(dve_steps, 1)
                    dve.wait_ge(dve_steps, steps.next())
                    v.tensor_tensor(x[:, t, :], x[:, t, :], h[:, t, :], ALU.add).then_inc(x_ready, 1)

            def add_normed(weight, give):
                dve.wait_ge(rms2_ready, 1)
                dve.sem_inc(rms2_ready, -1)
                v.reciprocal(rstd[:], rms[:]).then_inc(dve_steps, 1)
                dve.wait_ge(dve_steps, steps.next())
                dve.wait_ge(post_in, 16)
                dve.sem_inc(post_in, -16)
                for t in range(TILES):
                    v.scalar_tensor_tensor(h[:, t, :], acc_rows(t), rstd[:, t:t + 1], gain_post[:], ALU.mult, ALU.mult).then_inc(dve_steps, 1)
                    dve.wait_ge(dve_steps, steps.next())
                    v.scalar_tensor_tensor(x[:, t, :], h[:, t, :], weight, x[:, t, :], ALU.mult, ALU.add).then_inc(give, 1)
                dve.sem_inc(post_free, 1)
                dve.sem_inc(dve_steps, -steps.reset())

            def pre_norm():
                dve.wait_ge(pre_in, 16)
                dve.sem_inc(pre_in, -16)
                normalise(gain_pre[:], None)
                fan(dve, pre_free)
                dve.sem_inc(dve_steps, -steps.reset())

            def softmax_rows(second):
                units = attention_units(second)
                S = scores2 if second else scores

                def rows(u):
                    t, heads = units[u]
                    b = u % 2
                    n = P * (t + 1) if second else SEQ
                    dve.wait_ge(scores_done, 1)
                    dve.sem_inc(scores_done, -1)
                    if second:
                        mask = window[:, 0, SEQ - n:SEQ]
                        for i, head in enumerate(heads):
                            ins = v.scalar_tensor_tensor(S[:, b, i, 0:n], ps[:, WORK + 2 * b + i // 2, (i % 2) * SEQ:(i % 2) * SEQ + n],
                                                         c_tok[:, t * HEADS2 + head:t * HEADS2 + head + 1], mask, ALU.add, ALU.add)
                    else:
                        for pair in range(2):
                            ins = v.tensor_tensor(S[:, b, 2 * pair:2 * pair + 2, :],
                                                  ps[:, WORK + 2 * b + pair, :].rearrange("p (i t) -> p i t", t=SEQ),
                                                  window[:, t:t + 1, :].to_broadcast([P, 2, SEQ]), ALU.add)
                    ins.then_inc(dve_steps, 1)
                    dve.wait_ge(dve_steps, steps.next())
                    v.tensor_reduce(row_max[:, b, :], S[:, b, :, 0:n], AX_X, ALU.max).then_inc(dve_steps, 1)
                    dve.wait_ge(dve_steps, steps.next())
                    if not second:
                        sinks = sink[:, heads[0]:heads[0] + GROUP]
                        v.tensor_tensor(row_max[:, b, :], row_max[:, b, :], sinks, ALU.max).then_inc(dve_steps, 1)
                        dve.wait_ge(dve_steps, steps.next())
                        v.tensor_tensor(sink_d[:, b, :], sinks, row_max[:, b, :], ALU.subtract).then_inc(dve_steps, 1)
                        dve.wait_ge(dve_steps, steps.next())
                    v.tensor_scalar(neg_max[:, b, :], row_max[:, b, :], -1.0, None, ALU.mult).then_inc(scores_ready, 1)

                def close(u):
                    t, heads = units[u]
                    b = u % 2
                    dve.wait_ge(sums_ready, 1)
                    dve.sem_inc(sums_ready, -1)
                    if not second:
                        v.tensor_tensor(row_sum[:, b, :], row_sum[:, b, :], sink_e[:, b, :], ALU.add).then_inc(dve_steps, 1)
                        dve.wait_ge(dve_steps, steps.next())
                    v.reciprocal(row_inv[:, b, :], row_sum[:, b, :]).then_inc(dve_steps, 1)
                    dve.wait_ge(dve_steps, steps.next())
                    dve.wait_ge(pv_done, 1)
                    dve.sem_inc(pv_done, -1)
                    dst = (h if second else attn)[:, t, heads[0] * HEAD:(heads[0] + GROUP) * HEAD]
                    v.tensor_tensor(dst.rearrange("p (i d) -> p i d", d=HEAD),
                                    ps[:, 2 + b, 0:GROUP * HEAD].rearrange("p (i d) -> p i d", d=HEAD),
                                    row_inv[:, b, :].unsqueeze(2).to_broadcast([P, GROUP, HEAD]), ALU.mult).then_inc(attn_done, 1)

                for u in range(len(units)):
                    rows(u)
                    if u >= 1:
                        close(u - 1)
                close(len(units) - 1)
                dve.sem_inc(dve_steps, -steps.reset())

            with dve.Fori(0, DEPTH) as l:
                v.tensor_scalar(expert_base[:], expert_base[:], float(EXPERTS), None, ALU.add).then_inc(dve_steps, 1)
                dve.wait_ge(dve_steps, steps.next())
                dve.wait_ge(mod_ready, 1)
                dve.sem_inc(mod_ready, -1)
                dve.wait_ge(pre_in, 16)
                dve.sem_inc(pre_in, -16)
                v.scalar_tensor_tensor(mod[:, 1, :], mod[:, 1, :], 1.0, gain_pre[:], ALU.add, ALU.mult).then_inc(dve_steps, 1)
                dve.wait_ge(dve_steps, steps.next())
                dve.sem_inc(pre_free, 1)
                normalise(mod[:, 1, :], mod[:, 0, :])
                dve.wait_ge(post_in, 16)
                dve.sem_inc(post_in, -16)
                v.scalar_tensor_tensor(mod[:, 4, :], mod[:, 4, :], 1.0, gain_post[:], ALU.add, ALU.mult).then_inc(dve_steps, 1)
                dve.wait_ge(dve_steps, steps.next())
                dve.sem_inc(post_free, 1)
                dve.wait_ge(dve_params, 3 * 16)
                dve.sem_inc(dve_params, -3 * 16)
                dve.wait_ge(qk_ready, 1)
                dve.sem_inc(qk_ready, -1)
                v.tensor_tensor(qk_sq[:], qk[:], qk[:], ALU.mult).then_inc(dve_steps, 1)
                dve.wait_ge(dve_steps, steps.next())
                v.tensor_reduce(head_sq[:], qk_sq[:], AX_X, ALU.add).then_inc(head_sq_ready, 1)
                dve.wait_ge(head_rms_ready, 1)
                dve.sem_inc(head_rms_ready, -1)
                v.reciprocal(head_rms[:], head_rms[:]).then_inc(dve_steps, 1)
                dve.wait_ge(dve_steps, steps.next())
                v.tensor_tensor(qk[:], qk[:], head_rms[:].unsqueeze(3).to_broadcast([P, TILES, QK, HEAD]), ALU.mult).then_inc(dve_steps, 1)
                dve.wait_ge(dve_steps, steps.next())
                for t in range(TILES):
                    v.tensor_tensor(qk[:, t], qk[:, t], qk_gain[:], ALU.mult).then_inc(dve_steps, 1)
                    dve.wait_ge(dve_steps, steps.next())
                low, high = qk[:, :, :, 0:half], qk[:, :, :, half:ROPE]
                cos = cosine[:].unsqueeze(2).to_broadcast([P, TILES, QK, half])
                sin = sine[:].unsqueeze(2).to_broadcast([P, TILES, QK, half])
                for n, (part, turn) in enumerate(((low, cos), (high, sin), (high, cos), (low, sin))):
                    v.tensor_tensor(rope_t[:, n], part, turn, ALU.mult).then_inc(dve_steps, 1)
                    dve.wait_ge(dve_steps, steps.next())
                v.tensor_tensor(low, rope_t[:, 0], rope_t[:, 1], ALU.subtract).then_inc(dve_steps, 1)
                dve.wait_ge(dve_steps, steps.next())
                v.tensor_tensor(high, rope_t[:, 2], rope_t[:, 3], ALU.add).then_inc(qk_done, 1)
                softmax_rows(False)
                dve.wait_ge(rows_done, 1)
                dve.sem_inc(rows_done, -1)
                dve.sem_inc(slot_free, 1)
                add_gated(2)
                normalise(mod[:, 4, :], mod[:, 3, :])
                dve.sem_inc(dve_steps, -steps.reset())

                def route(n, p):
                    v.tensor_copy(half_s[:].rearrange("p h k -> p (h k)"), key_s[:, bass.ds(n, 1), :, :].rearrange("p n h k -> p (n h k)")).then_inc(dve_steps, 1)
                    dve.wait_ge(dve_steps, steps.next())
                    for s in range(2):
                        v.max(best[:, s, 0:8], half_s[:, s, :]).then_inc(dve_steps, 1)
                        dve.wait_ge(dve_steps, steps.next())
                        v.max_index(best_i[:, s, 0:8], best[:, s, 0:8], half_s[:, s, :]).then_inc(dve_steps, 1)
                        dve.wait_ge(dve_steps, steps.next())
                        v.match_replace(half_r[:, s, :], best[:, s, 0:8], half_s[:, s, :], LEAST).then_inc(dve_steps, 1)
                        dve.wait_ge(dve_steps, steps.next())
                        v.max(best[:, s, 8:16], half_r[:, s, :]).then_inc(dve_steps, 1)
                        dve.wait_ge(dve_steps, steps.next())
                        v.max_index(best_i[:, s, 8:16], best[:, s, 8:16], half_r[:, s, :]).then_inc(dve_steps, 1)
                        dve.wait_ge(dve_steps, steps.next())
                    v.tensor_tensor(cand[:].rearrange("p (i j) -> p i j", i=TOPK), best[:, 0, :].unsqueeze(2).to_broadcast([P, TOPK, TOPK]),
                                    best[:, 1, :].unsqueeze(1).to_broadcast([P, TOPK, TOPK]), ALU.add).then_inc(dve_steps, 1)
                    dve.wait_ge(dve_steps, steps.next())
                    v.max(top[:, p, 0:8], cand[:]).then_inc(dve_steps, 1)
                    dve.wait_ge(dve_steps, steps.next())
                    v.max_index(place[:, 0:8], top[:, p, 0:8], cand[:]).then_inc(dve_steps, 1)
                    dve.wait_ge(dve_steps, steps.next())
                    v.match_replace(cand_r[:], top[:, p, 0:8], cand[:], LEAST).then_inc(dve_steps, 1)
                    dve.wait_ge(dve_steps, steps.next())
                    v.max(top[:, p, 8:16], cand_r[:]).then_inc(dve_steps, 1)
                    dve.wait_ge(dve_steps, steps.next())
                    v.max_index(place[:, 8:16], top[:, p, 8:16], cand_r[:]).then_inc(dve_steps, 1)
                    dve.wait_ge(dve_steps, steps.next())
                    v.tensor_scalar(neg_top[:, p, :], top[:, p, 0:1], -1.0, None, ALU.mult).then_inc(top_ready, 1)
                    v.tensor_scalar(place2[:, 0, :], place[:], 4, None, ALU.logical_shift_right).then_inc(dve_steps, 1)
                    dve.wait_ge(dve_steps, steps.next())
                    v.tensor_scalar(place2[:, 1, :], place[:], TOPK - 1, None, ALU.bitwise_and).then_inc(dve_steps, 1)
                    dve.wait_ge(dve_steps, steps.next())
                    v.tensor_copy(place_f[:], place2[:]).then_inc(dve_steps, 1)
                    dve.wait_ge(dve_steps, steps.next())
                    v.tensor_copy(best_f[:], best_i[:]).then_inc(dve_steps, 1)
                    dve.wait_ge(dve_steps, steps.next())
                    for s in range(2):
                        v.tensor_tensor(onehot[:], place_f[:, s, :].unsqueeze(2).to_broadcast([P, TOPK, TOPK]),
                                        iota16[:].unsqueeze(1).to_broadcast([P, TOPK, TOPK]), ALU.is_equal).then_inc(dve_steps, 1)
                        dve.wait_ge(dve_steps, steps.next())
                        v.tensor_tensor(onehot[:], onehot[:], best_f[:, s, :].unsqueeze(1).to_broadcast([P, TOPK, TOPK]), ALU.mult).then_inc(dve_steps, 1)
                        dve.wait_ge(dve_steps, steps.next())
                        v.tensor_reduce(chosen[:, s, :], onehot[:], AX_X, ALU.add).then_inc(dve_steps, 1)
                        dve.wait_ge(dve_steps, steps.next())
                    v.scalar_tensor_tensor(expert_f[:], chosen[:, 0, :], float(KEYS), chosen[:, 1, :], ALU.mult, ALU.add).then_inc(dve_steps, 1)
                    dve.wait_ge(dve_steps, steps.next())
                    v.tensor_scalar(expert[:, p, :], expert_f[:], expert_base[:], None, ALU.add).then_inc(expert_ready, 1)

                def unit(t, n, p, follow):
                    for g in range(2):
                        for j in range(GRP):
                            dve.wait_ge(u_in[j], (l * (2 * UNITS) + (n * 2 + (g + 1))) * 16)
                            v.tensor_tensor_reduce(out=junk, in0=u_ring[:, j, :], in1=h[:, t, :], scale=1.0, scalar=0.0,
                                                   op0=ALU.mult, op1=ALU.add, accum_out=dots[:, g, j:j + 1]).then_inc(dve_steps, 1)
                            dve.wait_ge(dve_steps, steps.next())
                            dve.sem_inc(u_free, 1)
                        dve.sem_inc(dots_ready, 1)
                        if g == 0:
                            dve.wait_ge(gate_ready, 1)
                            dve.sem_inc(gate_ready, -1)
                            v.reciprocal(gate_inv[:], gate_sum[:, p, :]).then_inc(dve_steps, 1)
                            dve.wait_ge(dve_steps, steps.next())
                            v.tensor_scalar(gate[:], gate_e[:, p, :], gate_inv[:], None, ALU.mult).then_inc(dve_steps, 1)
                            dve.wait_ge(dve_steps, steps.next())
                        dve.wait_ge(acts_ready, 1)
                        dve.sem_inc(acts_ready, -1)
                        if g == 0:
                            dve.wait_ge(diag_free, 1)
                            dve.sem_inc(diag_free, -1)
                        for j in range(GRP):
                            k = g * GRP + j
                            v.tensor_scalar(diag[:, k, :], ident[:], acts[:, g, j:j + 1], gate[:, k:k + 1], ALU.mult, ALU.mult).then_inc(diag_ready, 1)
                        if g == 0:
                            dve.wait_ge(diag_free, 1)
                            dve.sem_inc(diag_free, -1)
                            if follow:
                                route(n + 1, 1 - p)
                    dve.sem_inc(dve_steps, -steps.reset())

                dve.wait_ge(key_s_ready, 8)
                dve.sem_inc(key_s_ready, -8)
                route(0, 0)
                dve.sem_inc(dve_steps, -steps.reset())
                with dve.Fori(0, EXPERT_HEADS // 2) as i:
                    for p in range(2):
                        unit(0, i * 2 + p, p, True)
                with dve.Fori(0, EXPERT_HEADS // 2 - 1) as i:
                    for p in range(2):
                        unit(1, i * 2 + (EXPERT_HEADS + p), p, True)
                unit(1, UNITS - 2, 0, True)
                unit(1, UNITS - 1, 1, False)
                dve.wait_ge(y_ready, 1)
                dve.sem_inc(y_ready, -1)
                dve.sem_inc(slot_free, 4)
                add_gated(5)
                dve.sem_inc(params_free, 1)
                dve.sem_inc(dve_steps, -steps.reset())

            fan(dve, block1_done)

            def feed_forward(give=x_ready):
                pre_norm()
                with dve.Fori(0, FF_CHUNKS // 2) as i:
                    for b in range(2):
                        dve.wait_ge(silu_ready, 1)
                        dve.sem_inc(silu_ready, -1)
                        v.tensor_tensor(ff_a[:, b, :], silu_g[:, b, :], ps[:, WORK + b, SEQ:2 * SEQ], ALU.mult).then_inc(ff_ready, 1)
                add_normed(0.5, give)

            def log1p_series(t, total):
                v.tensor_scalar(t[2], t[1], 2.0, None, ALU.add).then_inc(dve_steps, 1)
                dve.wait_ge(dve_steps, steps.next())
                v.reciprocal(t[2], t[2]).then_inc(dve_steps, 1)
                dve.wait_ge(dve_steps, steps.next())
                v.tensor_tensor(t[3], t[1], t[2], ALU.mult).then_inc(dve_steps, 1)
                dve.wait_ge(dve_steps, steps.next())
                v.tensor_tensor(t[4], t[3], t[3], ALU.mult).then_inc(dve_steps, 1)
                dve.wait_ge(dve_steps, steps.next())
                v.tensor_scalar(t[5], t[4], 1.0 / (2 * total + 1), None, ALU.mult).then_inc(dve_steps, 1)
                dve.wait_ge(dve_steps, steps.next())
                for n in range(total - 1, 0, -1):
                    v.scalar_tensor_tensor(t[5], t[5], 1.0 / (2 * n + 1), t[4], ALU.add, ALU.mult).then_inc(dve_steps, 1)
                    dve.wait_ge(dve_steps, steps.next())
                v.scalar_tensor_tensor(t[5], t[5], 1.0, t[3], ALU.add, ALU.mult).then_inc(dve_steps, 1)
                dve.wait_ge(dve_steps, steps.next())
                v.tensor_scalar(t[5], t[5], 2.0, None, ALU.mult).then_inc(dve_steps, 1)
                dve.wait_ge(dve_steps, steps.next())

            feed_forward()
            pre_norm()
            dve.wait_ge(rnn_cols_ready, 1)
            dve.sem_inc(rnn_cols_ready, -1)
            lam = rnn_cols[:, 7, :]
            v.scalar_tensor_tensor(decay[:, 0, :], lam, -1.0, lam, ALU.mult, ALU.max).then_inc(lam_abs, 1)
            dve.wait_ge(lam_exp, 1)
            dve.sem_inc(lam_exp, -1)
            log1p_series([decay[:, k, :] for k in range(6)], 8)
            v.tensor_scalar(decay[:, 0, :], lam, -1.0, 0.0, ALU.mult, ALU.max).then_inc(dve_steps, 1)
            dve.wait_ge(dve_steps, steps.next())
            v.tensor_tensor(decay[:, 0, :], decay[:, 0, :], decay[:, 5, :], ALU.add).then_inc(dve_steps, 1)
            dve.wait_ge(dve_steps, steps.next())
            v.tensor_scalar(decay_neg[:], decay[:, 0, :], -8.0, None, ALU.mult).then_inc(dve_steps, 1)
            dve.wait_ge(dve_steps, steps.next())
            v.tensor_scalar(decay_pos[:], decay[:, 0, :], 8.0, None, ALU.mult).then_inc(decay_ready, 1)
            dve.wait_ge(rnn_zeroed, 1)
            dve.sem_inc(rnn_zeroed, -1)
            for s in range(SUPER):
                dve.wait_ge(rec_in_ready, 1)
                dve.sem_inc(rec_in_ready, -1)
                chunks = range(3 * s, 3 * s + 3)
                for j in chunks:
                    ins = v.tensor_scalar(rec[:, j, :], rec_in[:, j, CONV_K - 1:], rnn_cols[:, 3, j:j + 1], rnn_cols[:, 4, j:j + 1], ALU.mult, ALU.add)
                for k in range(CONV_K - 1):
                    ins.then_inc(dve_steps, 1)
                    dve.wait_ge(dve_steps, steps.next())
                    for j in chunks:
                        ins = v.scalar_tensor_tensor(rec[:, j, :], rec_in[:, j, k:k + SEQ], rnn_cols[:, k, j:j + 1], rec[:, j, :], ALU.mult, ALU.add)
                ins.then_inc(rec_ready, 1)
            for s in range(SUPER):
                c = slice(3 * s, 3 * s + 3)
                dve.wait_ge(gates_ready, 1)
                dve.sem_inc(gates_ready, -1)
                v.tensor_tensor(gate_i[:, c], gate_i[:, c], rec[:, c], ALU.mult).then_inc(dve_steps, 1)
                dve.wait_ge(dve_steps, steps.next())
                v.tensor_tensor(rec[:, c], decay_a[:, c], decay_a[:, c], ALU.mult).then_inc(dve_steps, 1)
                dve.wait_ge(dve_steps, steps.next())
                v.scalar_tensor_tensor(gate_r[:, c], rec[:, c], 1.0, gate_r[:, c], ALU.add, ALU.mult).then_inc(root_in, 1)
            for s in range(SUPER):
                c = slice(3 * s, 3 * s + 3)
                dve.wait_ge(root_ready, 1)
                dve.sem_inc(root_ready, -1)
                v.tensor_tensor(gate_i[:, c], gate_i[:, c], gate_r[:, c], ALU.mult).then_inc(dve_steps, 1)
                dve.wait_ge(dve_steps, steps.next())
                for j in range(3 * s, 3 * s + 3):
                    ins = v.tensor_tensor_scan(rec[:, j, :], decay_a[:, j, :], gate_i[:, j, :], 0.0, ALU.mult, ALU.add)
                ins.then_inc(dve_steps, 1)
                dve.wait_ge(dve_steps, steps.next())
                ins = v.tensor_tensor(gate_g[:, c], gate_g[:, c], rec[:, c], ALU.mult)
            ins.then_inc(rnn_out_ready, 1)
            add_normed(1.0, x_ready)
            fan(dve, rnn_over)
            feed_forward()
            pre_norm()
            dve.wait_ge(f_ready, 1)
            dve.sem_inc(f_ready, -1)
            v.scalar_tensor_tensor(logs[:, 0, :], f_tok[:], -1.0, f_tok[:], ALU.mult, ALU.max).then_inc(f_abs, 1)
            dve.wait_ge(f_exp, 1)
            dve.sem_inc(f_exp, -1)
            log1p_series([logs[:, k, :] for k in range(6)], 8)
            v.scalar_tensor_tensor(log_f[:], f_tok[:], 0.0, logs[:, 5, :], ALU.min, ALU.subtract).then_inc(log_f_ready, 1)
            dve.sem_inc(x_ready, TILES)
            dve.sem_inc(dve_steps, -steps.reset())
            feed_forward()
            pre_norm()
            softmax_rows(True)
            dve.sem_inc(h_ready, TILES)
            add_normed(1.0, x_ready)
            feed_forward(x_final)


INPUTS = [
    "x", "c", "positions", "norm1_g", "norm2_g", "w_ada", "b_ada", "w_in", "q_norm_g", "k_norm_g", "attn_sink",
    "conv_w", "pool_w", "pool_scale", "w_out", "peer_wq", "peer_keys", "peer_u", "peer_v", "ffn1_pre_g_2",
    "ffn1_w_gate_2", "ffn1_w_up_2", "ffn1_w_down_2", "ffn1_post_g_2", "mix_pre_g_2", "mix_post_g_2",
    "ffn2_pre_g_2", "ffn2_w_gate_2", "ffn2_w_up_2", "ffn2_w_down_2", "ffn2_post_g_2", "rg_w_in_2",
    "rg_conv_w_2", "rg_conv_b_2", "rg_w_a_2", "rg_b_a_2", "rg_w_x_2", "rg_b_x_2", "rg_lambda_2", "rg_w_out_2",
    "kv_norm_g_2", "w_kv_2", "w_fgate_2", "b_fgate_2", "attn_w_q_2", "attn_w_o_2",
]


def kernel(**inputs):
    import concourse.bacc as bacc
    from concourse.bass_utils import run_bass_kernel_spmd

    nc = bacc.Bacc("TRN2", target_bir_lowering=False, num_devices=1)
    arrays, views = {}, {}
    for name in INPUTS:
        a = np.ascontiguousarray(inputs[name])
        if name in ("peer_u", "peer_v"):
            a = a.reshape(-1, a.shape[-1])
        arrays["in_" + name] = a
        views[name] = nc.dram_tensor("in_" + name, a.shape, mybir.dt.from_np(a.dtype), kind="ExternalInput").ap()
    out = nc.dram_tensor("out", (1, SEQ, D), F32, kind="ExternalOutput").ap()
    program(nc, views, out)
    return run_bass_kernel_spmd(nc, [arrays], core_ids=[0]).results[0]["out"]
```

```python
from contextlib import ExitStack

import numpy as np

import concourse.bass as bass
from concourse import mybir

ALU = mybir.AluOpType
ACT = mybir.ActivationFunctionType
F32 = mybir.dt.float32
F32R = mybir.dt.float32r
I32 = mybir.dt.int32
U32 = mybir.dt.uint32
AX_X = mybir.AxisListType.X

P = 128
SEQ = 256
D = 1024
KC = D // P
TILES = SEQ // P
DEPTH = 2
EPS = 1e-6
MASKED = -1e30
LEAST = -3.0e38

HEAD = 64
Q_HEADS = 8
KV_HEADS = 2
GROUP = Q_HEADS // KV_HEADS
ROPE = HEAD // 4
ROPE_THETA = 500000.0
WINDOWS = (2, 4, 8, 16)
PAD = WINDOWS[-1]
PADDED = SEQ + 2 * PAD
ATTN_W = Q_HEADS * HEAD
KV_W = KV_HEADS * HEAD
EXPERT_HEADS = 8
KEYS = 128
EXPERTS = KEYS * KEYS
TOPK = 16
UNITS = TILES * EXPERT_HEADS
U_SLOTS = 8
V_SLOTS = 16
GRP = 8

D_FF = 2816
FF_CHUNKS = D_FF // P
D_RNN = 1344
RC = 112
R_CHUNKS = D_RNN // RC
LRU = 84
SUPER = 4
CONV_K = 4
HEADS2 = 16

SLOTS = 4
SLOT = 4096
N = 512


def program(nc, A, out):
    with ExitStack() as ctx:
        def sb(name, shape, dt=F32):
            return ctx.enter_context(nc.sbuf_tensor(name, shape, dt))

        def sem(name):
            return ctx.enter_context(nc.semaphore(name))

        ps = ctx.enter_context(nc.psum_tensor("ps", [P, 8, N], F32))
        WORK = 4

        x = sb("x", [P, TILES, D])
        h_ext = sb("h_ext", [P, TILES * D + D])
        h = h_ext[:, 0:TILES * D].rearrange("p (t d) -> p t d", t=TILES)
        junk = h_ext[:, TILES * D:]
        gain_pre = sb("gain_pre", [P, D])
        gain_post = sb("gain_post", [P, D])
        ident = sb("ident", [P, P])
        zeros = sb("zeros", [P, P])
        ones = sb("ones", [P, P])
        upto = sb("upto", [P, P])
        window = sb("window_mask", [P, TILES, SEQ])
        eps = sb("eps", [P, 1])
        iota16 = sb("iota16", [P, TOPK])
        window_count = sb("window_count", [P, 2, SEQ])
        c_rows = sb("c_rows", [KC, P])
        c_act = sb("c_act", [P, KC])
        c_hi = sb("c_hi", [P, KC], F32R)
        c_lo = sb("c_lo", [P, KC], F32R)
        pos_i = sb("pos_i", [TILES, P], I32)
        pos_f = sb("pos_f", [TILES, P])
        pos = sb("pos", [P, TILES])
        inv_freq = sb("inv_freq", [P, ROPE // 2])
        angle = sb("angle", [P, 4, TILES, ROPE // 2])
        cosine = sb("cosine", [P, TILES, ROPE // 2])
        sine = sb("sine", [P, TILES, ROPE // 2])
        mix_rows = sb("mix_rows", [8, P])
        mix_cols = sb("mix_cols", [P, 8])
        pool_w = sb("pool_w", [P, 2, P])
        keys_raw = sb("keys_raw", [P, 2, KEYS])
        keysT = sb("keysT", [P, 2, KEYS])
        sink = sb("sink", [P, Q_HEADS])
        expert_base = sb("expert_base", [P, 1])
        mean_sq = sb("mean_sq", [P, TILES])
        rms = sb("rms", [P, TILES])
        root_table = sb("root_table", [P, 1])
        rstd = sb("rstd", [P, TILES])
        head_sq = sb("head_sq", [P, TILES, Q_HEADS + KV_HEADS])
        head_rms = sb("head_rms", [P, TILES, Q_HEADS + KV_HEADS])
        row_max = sb("row_max", [P, 2, GROUP])
        neg_max = sb("neg_max", [P, 2, GROUP])
        sink_d = sb("sink_d", [P, 2, GROUP])
        sink_e = sb("sink_e", [P, 2, GROUP])
        row_sum = sb("row_sum", [P, 2, GROUP])
        row_inv = sb("row_inv", [P, 2, GROUP])
        best = sb("best", [P, 2, TOPK])
        best_i = sb("best_i", [P, 2, TOPK], U32)
        best_f = sb("best_f", [P, 2, TOPK])
        place = sb("place", [P, TOPK], U32)
        place2 = sb("place2", [P, 2, TOPK], U32)
        place_f = sb("place_f", [P, 2, TOPK])
        chosen = sb("chosen", [P, 2, TOPK])
        expert_f = sb("expert_f", [P, TOPK])
        expert = sb("expert", [P, 2, TOPK], U32)
        top = sb("top", [P, 2, TOPK])
        neg_top = sb("neg_top", [P, 2, 1])
        gate_e = sb("gate_e", [P, 2, TOPK])
        gate_sum = sb("gate_sum", [P, 2, 1])
        gate_inv = sb("gate_inv", [P, 1])
        gate = sb("gate", [P, TOPK])
        dots = sb("dots", [P, 2, GRP])
        acts = sb("acts", [P, 2, GRP])
        rnn_rows = sb("rnn_rows", [8 * R_CHUNKS, RC])
        rnn_cols = sb("rnn_cols", [RC, 8, R_CHUNKS])
        decay = sb("decay", [RC, 6, R_CHUNKS])
        decay_neg = sb("decay_neg", [RC, R_CHUNKS])
        decay_pos = sb("decay_pos", [RC, R_CHUNKS])
        wf = sb("wf", [P, KC, HEADS2])
        bf = sb("bf", [1, HEADS2])
        f_tok = sb("f_tok", [P, TILES * HEADS2])
        logs = sb("logs", [P, 6, TILES * HEADS2])
        log_f = sb("log_f", [P, TILES * HEADS2])
        c_tok = sb("c_tok", [P, TILES * HEADS2])

        ARENA = 21824
        AT_HT = SLOTS * SLOT
        AT_ARENA = AT_HT + KC * SEQ

        def overlay(name, at, shape, dt=F32):
            with ExitStack() as scope:
                if at:
                    scope.enter_context(nc.sbuf_tensor("below_" + name, [P, at], F32))
                return scope.enter_context(nc.sbuf_tensor(name, shape, dt))

        ring = overlay("weight_ring", 0, [P, SLOTS, SLOT])
        ring_lo = overlay("ring_lo", 0, [P, SLOTS, SLOT], F32R)
        hT = overlay("hT", AT_HT, [P, KC, SEQ])
        hT_hi = overlay("hT_hi", AT_HT, [P, KC, SEQ], F32R)
        arena = overlay("arena", AT_ARENA, [P, ARENA])

        class Carve:

            def __init__(self, start=0):
                self.at = start

            def __call__(self, size, pattern=None, **kw):
                part = arena[:, self.at:self.at + size]
                self.at += size
                assert self.at <= ARENA, self.at
                return part.rearrange(pattern, **kw) if pattern else part

        c1 = Carve()
        mod = c1(6 * D, "p (s d) -> p s d", s=6)
        qTz = c1(Q_HEADS * SEQ, "p (h t) -> p h t", h=Q_HEADS)
        shared = c1.at
        QK = Q_HEADS + KV_HEADS
        qk_gain = c1(QK * HEAD, "p (h d) -> p h d", h=QK)
        qk = c1(TILES * QK * HEAD, "p (t h d) -> p t h d", t=TILES, h=QK)
        v_tok = c1(TILES * KV_W, "p (t d) -> p t d", t=TILES)
        zc = c1(8 * SEQ, "p (c t) -> p c t", c=8)
        kT = c1(SEQ)
        pT = c1(2 * GROUP * P, "p (i t) -> p i t", t=P)
        attn = c1(TILES * ATTN_W, "p (t d) -> p t d", t=TILES)
        conv_u = c1(2 * SEQ, "p (c t) -> p c t", c=2)
        conv_o = c1(2 * SEQ, "p (c t) -> p c t", c=2)
        conv_t = c1(2 * SEQ, "p (c t) -> p c t", c=2)
        pool_in = c1(2 * PADDED, "p (c t) -> p c t", c=2)
        pool_s = [c1(2 * PADDED, "p (c t) -> p c t", c=2) for _ in range(2)]
        pooled = c1(2 * SEQ, "p (c t) -> p c t", c=2)
        mixT = hT
        ROPE_N = 4 * TILES * QK * ROPE // 2
        qk_sq = h_ext[:, ROPE_N:ROPE_N + TILES * QK * HEAD].rearrange("p (t h d) -> p t h d", t=TILES, h=QK)
        rope_t = h_ext[:, 0:4 * TILES * QK * ROPE // 2].rearrange("p (n t h d) -> p n t h d", n=4, t=TILES, h=QK)
        scores = h_ext[:, 0:2 * GROUP * SEQ].rearrange("p (b i t) -> p b i t", b=2, i=GROUP)
        c2 = Carve(shared)
        qpT = arena[:, shared:shared + 16 * SEQ].rearrange("p (c t) -> p c t", c=16)
        diag = c2(2 * GRP * P, "p (s t) -> p s t", t=P)
        c2 = Carve(shared + 16 * SEQ)
        u_ring = c2(U_SLOTS * D, "p (s d) -> p s d", s=U_SLOTS)
        half_s = c2(2 * KEYS, "p (h k) -> p h k", h=2)
        half_r = c2(2 * KEYS, "p (h k) -> p h k", h=2)
        cand = c2(TOPK * TOPK)
        cand_r = c2(TOPK * TOPK)
        onehot = c2(TOPK * TOPK, "p (k j) -> p k j", k=TOPK)
        key_s = arena[:, 0:UNITS * 2 * KEYS].rearrange("p (n h k) -> p n h k", n=UNITS, h=2)
        v_ring = ring[:, :, :].rearrange("p s (b d) -> p (s b) d", d=D)
        ada_bias = hT[0:4, :, :].rearrange("p c t -> p (c t)")
        ADA_N = 384
        BLK = 256
        ROWS = KC * BLK // D
        ada_hi = overlay("ada_hi", AT_ARENA + ARENA - SLOTS * KC * ADA_N, [P, SLOTS, KC * ADA_N], F32R)
        in_hi = overlay("in_hi", AT_ARENA + ARENA - SLOTS * KC * BLK, [P, SLOTS, KC * BLK], F32R)
        hT_lo1 = overlay("hT_lo1", AT_ARENA, [P, KC, SEQ], F32R)
        STAYS = 2 * TILES * D + 2 * SEQ
        FF_SLOT = 2 * KC * P + D
        AT_FF = STAYS + KC * SEQ
        AT_W = AT_FF + 6 * SEQ
        hT_lo = overlay("hT_lo", AT_ARENA + STAYS, [P, KC, SEQ], F32R)
        silu_g = arena[:, AT_FF:AT_FF + 2 * SEQ].rearrange("p (b t) -> p b t", b=2)
        ff_hi = overlay("ff_hi", AT_ARENA + AT_FF + 2 * SEQ, [P, 2, SEQ], F32R)
        ff_lo = overlay("ff_lo", AT_ARENA + AT_FF + 4 * SEQ, [P, 2, SEQ], F32R)
        w_hi = overlay("w_hi", AT_ARENA + AT_W, [P, SLOTS, FF_SLOT], F32R)
        assert AT_W + SLOTS * FF_SLOT <= ARENA
        c3 = Carve()
        gate_g = c3(R_CHUNKS * SEQ, "p (c t) -> p c t", c=R_CHUNKS)[0:RC]
        rec_width = SEQ + CONV_K - 1
        rec_at = c3.at
        rec_in = c3(R_CHUNKS * rec_width, "p (c t) -> p c t", c=R_CHUNKS)[0:RC]
        gate_i = arena[0:RC, rec_at:rec_at + R_CHUNKS * SEQ].rearrange("p (c t) -> p c t", c=R_CHUNKS)
        rec = c3(R_CHUNKS * SEQ, "p (c t) -> p c t", c=R_CHUNKS)[0:RC]
        gate_r = c3(R_CHUNKS * SEQ, "p (c t) -> p c t", c=R_CHUNKS)[0:RC]
        wide = 3 * RC
        w_gates = [c3(SUPER * 3 * wide, "p (s i d) -> p s i d", s=SUPER, i=3)[0:RC] for _ in range(2)]
        decay_a = h_ext[0:RC, :].rearrange("p (c t) -> p c t", c=R_CHUNKS)
        c4 = Carve()
        kT2 = c4(8 * SEQ, "p (c t) -> p c t", c=8)
        v2 = c4(TILES * D, "p (t d) -> p t d", t=TILES)
        c_pad = c4(TILES * P, "p (t j) -> p t j", t=TILES)
        neg_cT = c4(SEQ)
        qTz2 = arena[:, AT_W:AT_W + SLOTS * FF_SLOT].rearrange("p (s m) -> p s m", s=SLOTS)[:, :, KC * BLK:KC * BLK + GROUP * SEQ] \
            .rearrange("p s (h t) -> p s h t", h=GROUP)
        scores2 = hT[:].rearrange("p c t -> p (c t)").rearrange("p (b i t) -> p b i t", b=2, i=GROUP)
        pT2 = junk.rearrange("p (i t) -> p i t", t=P)

        consts, tables = sem("consts"), sem("tables")
        const_steps = sem("const_steps")
        x_loaded = sem("x_loaded")
        c_loaded = sem("c_loaded")
        pos_loaded = sem("pos_loaded")
        pos_float = sem("pos_float")
        pos_turned = sem("pos_turned")
        angle_ready = sem("angle_ready")
        rope_ready = sem("rope_ready")
        c_turned = sem("c_turned")
        c_act_ready = sem("c_act_ready")
        c_split = sem("c_split")
        slot_in = [sem(f"slot_in{i}") for i in range(SLOTS)]
        plain_in = [sem(f"plain_in{i}") for i in range(SLOTS)]
        slot_free = sem("slot_free")
        pre_in, pre_free = sem("pre_in"), sem("pre_free")
        post_in, post_free = sem("post_in"), sem("post_free")
        pe_params, dve_params, params_free = sem("pe_params"), sem("dve_params"), sem("params_free")
        bias_in = sem("bias_in")
        params_turned = sem("params_turned")
        x_ready = sem("x_ready")
        rms_ready = sem("rms_ready")
        h_ready = sem("h_ready")
        hT_turned = sem("hT_turned")
        hT_ready = sem("hT_ready")
        job_done, job_taken = sem("job_done"), sem("job_taken")
        mod_ready = sem("mod_ready")
        qk_ready = sem("qk_ready")
        head_sq_ready, head_rms_ready = sem("head_sq_ready"), sem("head_rms_ready")
        zc_ready = sem("zc_ready")
        qk_done = sem("qk_done")
        qk_turned = sem("qk_turned")
        qkT_ready = sem("qkT_ready")
        scores_done = sem("scores_done")
        scores_ready = sem("scores_ready")
        probs_ready = sem("probs_ready")
        sums_ready = sem("sums_ready")
        p_turned, pT_ready = sem("p_turned"), sem("pT_ready")
        pv_done, attn_done = sem("pv_done"), sem("attn_done")
        pooled_ready, pool_done = sem("pooled_ready"), sem("pool_done")
        attn_turned, mixT_ready = sem("attn_turned"), sem("mixT_ready")
        rows_done = sem("rows_done")
        rms2_ready = sem("rms2_ready")
        key_s_done, key_s_ready = sem("key_s_done"), sem("key_s_ready")
        expert_ready = sem("expert_ready")
        top_ready, gate_ready = sem("top_ready"), sem("gate_ready")
        u_in = [sem(f"u_in{i}") for i in range(U_SLOTS)]
        u_free = sem("u_free")
        v_in = [sem(f"v_in{i}") for i in range(V_SLOTS)]
        v_free = sem("v_free")
        dots_ready, acts_ready = sem("dots_ready"), sem("acts_ready")
        diag_ready, diag_free = sem("diag_ready"), sem("diag_free")
        y_ready, acc_read = sem("y_ready"), sem("acc_read")
        ff0_over, ff2_over = sem("ff0_over"), sem("ff2_over")
        hT_split = sem("hT_split")
        w_hi_ready, w_split = sem("w_hi_ready"), sem("w_split")
        gu_done, silu_ready, ff_ready = sem("gu_done"), sem("silu_ready"), sem("ff_ready")
        rnn_rows_in, rnn_turned, rnn_cols_ready = sem("rnn_rows_in"), sem("rnn_turned"), sem("rnn_cols_ready")
        rnn_zeroed, rnn_w_in = sem("rnn_zeroed"), sem("rnn_w_in")
        lam_abs, lam_exp, decay_ready = sem("lam_abs"), sem("lam_exp"), sem("decay_ready")
        rec_in_ready, rec_ready = sem("rec_in_ready"), sem("rec_ready")
        gates_ready, root_in, root_ready = sem("gates_ready"), sem("root_in"), sem("root_ready")
        rnn_out_ready = sem("rnn_out_ready")
        rnn_over = sem("rnn_over")
        wf_in = sem("wf_in")
        c_pad_zeroed, heads_zeroed = sem("c_pad_zeroed"), sem("heads_zeroed")
        f_ready, f_abs, f_exp, log_f_ready = sem("f_ready"), sem("f_abs"), sem("f_exp"), sem("log_f_ready")
        c_summed, c_ready, c_back, neg_cT_ready = sem("c_summed"), sem("c_ready"), sem("c_back"), sem("neg_cT_ready")
        x_final = sem("x_final")
        out_stored = sem("out_stored")
        act_steps, dve_steps, pool_steps = sem("act_steps"), sem("dve_steps"), sem("pool_steps")

        def fan(eng, s):
            eng.drain().then_inc(s, 1)

        class Count:

            def __init__(self):
                self.value = 0

            def next(self):
                self.value += 1
                return self.value

            def reset(self):
                value, self.value = self.value, 0
                assert value
                return value

        FF_NAMES = [("ffn1", 0), ("ffn2", 0), ("ffn1", 1), ("ffn2", 1)]
        first = {}
        at = 0
        for name, count in (("ff0", FF_CHUNKS), ("rnn_in", 6), ("rnn_out", 3), ("ff1", FF_CHUNKS), ("kv", 8),
                            ("ff2", FF_CHUNKS), ("q", 4), ("o", 4), ("ff3", FF_CHUNKS)):
            first[name] = at
            at += count
        PEEL = FF_CHUNKS % SLOTS
        TURNS = FF_CHUNKS // SLOTS

        IN_CUT = [0, BLK, ATTN_W, ATTN_W + KV_W] + [ATTN_W + 2 * KV_W + BLK * u for u in range(5)]

        def attention_units(second):
            return [(t, list(range(GROUP * g, GROUP * g + GROUP)))
                    for t in range(TILES) for g in range((HEADS2 if second else Q_HEADS) // GROUP)]

        block = ctx.enter_context(nc.Block())

        @block.sync
        def _(sp):
            sp.dma_start(c_rows[:], A["c"].rearrange("o (k p) -> (o k) p", p=P)).then_inc(c_loaded, 16)
            sp.dma_start(pos_i[:], A["positions"].rearrange("o (t p) -> (o t) p", p=P)).then_inc(pos_loaded, 16)

            def load(n, parts, given=slot_in):
                sp.wait_ge(slot_free, 1)
                sp.sem_inc(slot_free, -1)
                for off, rows, k, m, src in parts:
                    sp.dma_start(ring[0:rows, n % SLOTS, off:off + k * m].rearrange("p (k m) -> p k m", k=k), src).then_inc(given[n % SLOTS], 16)

            with sp.Fori(0, DEPTH) as l:
                def of(name):
                    return A[name][bass.ds(l, 1)].rearrange("o a b -> (o a) b")

                sp.wait_ge(params_free, 1)
                sp.sem_inc(params_free, -1)
                sp.dma_start(mix_rows[0:6, :], A["conv_w"][bass.ds(l, 1)].rearrange("o k (c p) -> (o k c) p", p=P)).then_inc(pe_params, 16)
                sp.dma_start(mix_rows[6:8, :], A["pool_scale"][bass.ds(l, 1)].rearrange("o (c p) -> (o c) p", p=P)).then_inc(pe_params, 16)
                sp.dma_start(keys_raw[:], A["peer_keys"][bass.ds(l, 1)].rearrange("o s k d -> k (o s) d")).then_inc(pe_params, 16)
                groups = A["pool_w"][bass.ds(l, 1)].rearrange("o (c s) i e -> s i (o c) e", s=2)
                for s in range(2):
                    sp.dma_start(pool_w[HEAD * s:HEAD * s + HEAD, :, HEAD * s:HEAD * s + HEAD], groups[s]).then_inc(pe_params, 16)
                sp.dma_start(ada_bias[:, 0:6 * D // 4].rearrange("p (i n) -> p i n", n=ADA_N),
                             A["b_ada"][bass.ds(l, 1)].rearrange("o (i u n) -> (o u) i n", u=4, n=ADA_N)).then_inc(bias_in, 16)
                sp.wait_ge(pre_free, 1)
                sp.sem_inc(pre_free, -1)
                sp.dma_start(gain_pre[:], A["norm1_g"][bass.ds(l, 1)].to_broadcast([P, D])).then_inc(pre_in, 16)
                sp.wait_ge(post_free, 1)
                sp.sem_inc(post_free, -1)
                sp.dma_start(gain_post[:], A["norm2_g"][bass.ds(l, 1)].to_broadcast([P, D])).then_inc(post_in, 16)
                w_ada = of("w_ada").rearrange("(k p) n -> p k n", p=P)
                with sp.Fori(0, 6 * D // (4 * ADA_N)) as i:
                    for u in range(4):
                        load(u, [(0, P, KC, ADA_N, w_ada[:, :, bass.ds(i * (4 * ADA_N) + u * ADA_N, ADA_N)])])
                sp.dma_start(qk_gain[:, 0:Q_HEADS, :], A["q_norm_g"][bass.ds(l, 1)].unsqueeze(1).to_broadcast([P, Q_HEADS, HEAD])).then_inc(dve_params, 16)
                sp.dma_start(qk_gain[:, Q_HEADS:QK, :], A["k_norm_g"][bass.ds(l, 1)].unsqueeze(1).to_broadcast([P, KV_HEADS, HEAD])).then_inc(dve_params, 16)
                sp.dma_start(sink[:], A["attn_sink"][bass.ds(l, 1)].to_broadcast([P, Q_HEADS])).then_inc(dve_params, 16)
                w_in = of("w_in").rearrange("(k p) n -> p k n", p=P)
                for u in range(8):
                    load(u, [(0, P, KC, IN_CUT[u + 1] - IN_CUT[u], w_in[:, :, IN_CUT[u]:IN_CUT[u + 1]])])
                w_out = of("w_out").rearrange("(k p) n -> p k n", p=P)
                for u in range(4):
                    load(u, [(0, P, 2, D, w_out[:, 2 * u:2 * u + 2, :])], plain_in)
                w_q = of("peer_wq").rearrange("(k p) n -> p k n", p=P)
                for u in range(8):
                    load(u, [(0, P, KC, BLK, w_q[:, :, u * BLK:(u + 1) * BLK])])

            def gain(name, layer, pre):
                src = A[name][layer:layer + 1, :] if layer is not None else A[name].unsqueeze(0)
                sp.wait_ge(pre_free if pre else post_free, 1)
                sp.sem_inc(pre_free if pre else post_free, -1)
                sp.dma_start((gain_pre if pre else gain_post)[:], src.to_broadcast([P, D])).then_inc(pre_in if pre else post_in, 16)

            def feed_forward(f):
                name, layer = FF_NAMES[f]
                w_g = A[name + "_w_gate_2"][layer].rearrange("(k p) n -> p k n", p=P)
                w_u = A[name + "_w_up_2"][layer].rearrange("(k p) n -> p k n", p=P)
                w_d = A[name + "_w_down_2"][layer].rearrange("(j p) n -> p j n", p=P)
                gain(name + "_pre_g_2", layer, True)

                def chunk(n, j):
                    load(n, [(0, P, KC, P, w_g[:, :, bass.ds(j * P, P)]),
                             (KC * P, P, KC, P, w_u[:, :, bass.ds(j * P, P)]),
                             (2 * KC * P, P, 1, D, w_d[:, bass.ds(j, 1), :])])

                n0 = first[f"ff{f}"]
                for j in range(PEEL):
                    chunk(n0 + j, j)
                with sp.Fori(0, TURNS) as i:
                    for u in range(SLOTS):
                        chunk(n0 + PEEL + u, i * SLOTS + (PEEL + u))
                gain(name + "_post_g_2", layer, False)

            feed_forward(0)
            rows = [("rg_conv_w_2", 0, CONV_K), ("rg_conv_b_2", 4, 1), ("rg_b_a_2", 5, 1), ("rg_b_x_2", 6, 1), ("rg_lambda_2", 7, 1)]
            for name, row, count in rows:
                src = A[name][0] if count > 1 else A[name]
                sp.dma_start(rnn_rows[row * R_CHUNKS:(row + count) * R_CHUNKS, :], src.rearrange("k (c p) -> (k c) p", p=RC)).then_inc(rnn_rows_in, 16)
            gain("mix_pre_g_2", 0, True)
            w = A["rg_w_in_2"][0].rearrange("(k p) n -> p k n", p=P)
            for u in range(6):
                load(first["rnn_in"] + u, [(0, P, KC, 4 * RC, w[:, :, u * 4 * RC:(u + 1) * 4 * RC])], plain_in)
            gain("mix_post_g_2", 0, False)
            w = A["rg_w_out_2"][0].rearrange("(c p) n -> p c n", p=RC)
            for u in range(3):
                load(first["rnn_out"] + u, [(0, RC, 4, D, w[:, 4 * u:4 * u + 4, :])], plain_in)
            feed_forward(1)
            sp.dma_start(wf[:], A["w_fgate_2"].rearrange("(k p) n -> p k n", p=P)).then_inc(wf_in, 16)
            sp.dma_start(bf[:], A["b_fgate_2"].unsqueeze(0)).then_inc(wf_in, 16)
            gain("kv_norm_g_2", None, True)
            w = A["w_kv_2"].rearrange("(k p) n -> p k n", p=P)
            for u in range(8):
                load(first["kv"] + u, [(0, P, KC, BLK, w[:, :, u * BLK:(u + 1) * BLK])])
            feed_forward(2)
            gain("mix_pre_g_2", 1, True)
            w = A["attn_w_q_2"][0].rearrange("(k p) n -> p k n", p=P)
            for u in range(4):
                load(first["q"] + u, [(0, P, KC, BLK, w[:, :, u * BLK:(u + 1) * BLK])])
            gain("mix_post_g_2", 1, False)
            w = A["attn_w_o_2"][0].rearrange("(k p) n -> p k n", p=P)
            for u in range(4):
                load(first["o"] + u, [(0, P, ROWS, D, w[:, ROWS * u:ROWS * u + ROWS, :])])
            feed_forward(3)
            sp.wait_ge(x_final, TILES)
            sp.sem_inc(x_final, -TILES)
            sp.dma_start(out.rearrange("o (t p) d -> p (o t) d", p=P), x[:]).then_inc(out_stored, 16)
            sp.wait_ge(out_stored, 16)

        @block.gpsimd
        def _(pool):
            g = nc.gpsimd
            build = Count()

            g.memset(zeros[:], 0.0).then_inc(const_steps, 1)
            pool.wait_ge(const_steps, build.next())
            g.memset(ones[:], 1.0).then_inc(const_steps, 1)
            pool.wait_ge(const_steps, build.next())
            g.affine_select(out=ident[:], in_=zeros[:], compare_op=ALU.not_equal, fill=1.0, base=0,
                            pattern=[[-1, P]], channel_multiplier=1).then_inc(const_steps, 1)
            pool.wait_ge(const_steps, build.next())
            g.affine_select(out=upto[:], in_=ones[:], compare_op=ALU.is_ge, fill=0.0, base=0,
                            pattern=[[1, P]], channel_multiplier=-1).then_inc(const_steps, 1)
            pool.wait_ge(const_steps, build.next())
            for i in range(ROPE // 2):
                g.memset(inv_freq[:, i:i + 1], float(ROPE_THETA ** (-2.0 * i / ROPE))).then_inc(const_steps, 1)
                pool.wait_ge(const_steps, build.next())
            g.memset(eps[:], EPS).then_inc(const_steps, 1)
            pool.wait_ge(const_steps, build.next())
            g.memset(pool_w[:], 0.0).then_inc(const_steps, 1)
            pool.wait_ge(const_steps, build.next())
            pool.sem_inc(consts, 1)
            pool.sem_inc(params_free, 1)
            g.memset(window[:], 0.0).then_inc(const_steps, 1)
            pool.wait_ge(const_steps, build.next())
            g.affine_select(out=window[:, 0, P:SEQ], in_=window[:, 0, P:SEQ], compare_op=ALU.is_ge, fill=MASKED,
                            base=0, pattern=[[-1, P]], channel_multiplier=1).then_inc(const_steps, 1)
            pool.wait_ge(const_steps, build.next())
            g.affine_select(out=window[:, 1, 0:P], in_=window[:, 1, 0:P], compare_op=ALU.is_ge, fill=MASKED,
                            base=0, pattern=[[1, P]], channel_multiplier=-1).then_inc(const_steps, 1)
            pool.wait_ge(const_steps, build.next())
            g.iota(iota16[:], pattern=[[1, TOPK]], base=0, channel_multiplier=0, allow_small_or_imprecise_dtypes=True).then_inc(const_steps, 1)
            pool.wait_ge(const_steps, build.next())
            g.iota(pool_in[:, 0, 0:SEQ], pattern=[[1, SEQ]], base=0, channel_multiplier=0, allow_small_or_imprecise_dtypes=True).then_inc(const_steps, 1)
            pool.wait_ge(const_steps, build.next())
            for n, w in enumerate(WINDOWS):
                rows, cc = slice(HEAD * (n % 2), HEAD * (n % 2) + HEAD), n // 2
                g.tensor_scalar(pool_s[0][rows, cc, 0:SEQ], pool_in[rows, 0, 0:SEQ], float(w // 2), float(SEQ), ALU.add, ALU.min).then_inc(const_steps, 1)
                pool.wait_ge(const_steps, build.next())
                g.tensor_scalar(pool_s[1][rows, cc, 0:SEQ], pool_in[rows, 0, 0:SEQ], float(-(w // 2)), 0.0, ALU.add, ALU.max).then_inc(const_steps, 1)
                pool.wait_ge(const_steps, build.next())
            g.tensor_tensor(window_count[:], pool_s[0][:, :, 0:SEQ], pool_s[1][:, :, 0:SEQ], ALU.subtract).then_inc(const_steps, 1)
            pool.wait_ge(const_steps, build.next())
            g.memset(qTz[:], 0.0).then_inc(const_steps, 1)
            pool.wait_ge(const_steps, build.next())
            g.memset(expert_base[:], float(-EXPERTS)).then_inc(const_steps, 1)
            pool.wait_ge(const_steps, build.next())
            pool.sem_inc(const_steps, -build.reset())
            pool.sem_inc(tables, 1)
            pool.dma_start(x[:], A["x"].rearrange("o (t p) d -> p (o t) d", p=P)).then_inc(x_loaded, 16)

            steps = Count()
            with pool.Fori(0, DEPTH) as l:
                pool.wait_ge(zc_ready, 1)
                pool.sem_inc(zc_ready, -1)
                g.tensor_tensor(conv_u[:], zc[:, 4:6, :], zc[:, 0:2, :], ALU.mult).then_inc(pool_steps, 1)
                pool.wait_ge(pool_steps, steps.next())
                for cc in range(2):
                    w = [mix_cols[:, 2 * k + cc:2 * k + cc + 1] for k in range(3)]
                    g.tensor_scalar(conv_o[:, cc, :], conv_u[:, cc, :], w[1], None, ALU.mult).then_inc(pool_steps, 1)
                    pool.wait_ge(pool_steps, steps.next())
                    g.tensor_scalar(conv_t[:, cc, 1:SEQ], conv_u[:, cc, 0:SEQ - 1], w[0], None, ALU.mult).then_inc(pool_steps, 1)
                    pool.wait_ge(pool_steps, steps.next())
                    g.tensor_tensor(conv_o[:, cc, 1:SEQ], conv_o[:, cc, 1:SEQ], conv_t[:, cc, 1:SEQ], ALU.add).then_inc(pool_steps, 1)
                    pool.wait_ge(pool_steps, steps.next())
                    g.tensor_scalar(conv_t[:, cc, 0:SEQ - 1], conv_u[:, cc, 1:SEQ], w[2], None, ALU.mult).then_inc(pool_steps, 1)
                    pool.wait_ge(pool_steps, steps.next())
                    g.tensor_tensor(conv_o[:, cc, 0:SEQ - 1], conv_o[:, cc, 0:SEQ - 1], conv_t[:, cc, 0:SEQ - 1], ALU.add).then_inc(pool_steps, 1)
                    pool.wait_ge(pool_steps, steps.next())
                g.tensor_tensor(mixT[:, 4:6, :], conv_o[:], zc[:, 2:4, :], ALU.mult).then_inc(pool_steps, 1)
                pool.wait_ge(pool_steps, steps.next())
                g.memset(pool_in[:], 0.0).then_inc(pool_steps, 1)
                pool.wait_ge(pool_steps, steps.next())
                g.tensor_copy(pool_in[:, :, PAD:PAD + SEQ], zc[:, 6:8, :]).then_inc(pool_steps, 1)
                pool.wait_ge(pool_steps, steps.next())
                src, lo, hi = pool_in, 0, PADDED
                for n, w in enumerate(WINDOWS):
                    left, right = (1, 0) if w == 2 else (w // 4, w // 4)
                    dst = pool_s[n % 2]
                    lo, hi = lo + left, hi - right
                    g.tensor_tensor(dst[:, :, lo:hi], src[:, :, lo - left:hi - left], src[:, :, lo + right:hi + right], ALU.add).then_inc(pool_steps, 1)
                    pool.wait_ge(pool_steps, steps.next())
                    src = dst
                    rows, cc = slice(HEAD * (n % 2), HEAD * (n % 2) + HEAD), n // 2
                    g.tensor_tensor(pooled[rows, cc, :], src[rows, cc, PAD:PAD + SEQ], window_count[rows, cc, :], ALU.mult).then_inc(pool_steps, 1)
                    pool.wait_ge(pool_steps, steps.next())
                pool.sem_inc(pool_steps, -steps.reset())
                g.tensor_tensor(pooled[:], pooled[:], zc[:, 6:8, :], ALU.subtract).then_inc(pooled_ready, 1)

                with pool.Fori(0, UNITS // 2) as n2:
                    for p in range(2):
                        pool.wait_ge(expert_ready, 1)
                        pool.sem_inc(expert_ready, -1)
                        for half in range(TOPK // GRP):
                            for j in range(GRP):
                                k = half * GRP + j
                                pool.wait_ge(u_free, 1)
                                pool.sem_inc(u_free, -1)
                                g.indirect_dma_start(u_ring[:, k % U_SLOTS, :], None, A["peer_u"],
                                                     bass.IndirectOffsetOnAxis(expert[:, p, k:k + 1], 0)).then_inc(u_in[k % U_SLOTS], 16)
                            for j in range(GRP):
                                k = half * GRP + j
                                pool.wait_ge(v_free, 1)
                                pool.sem_inc(v_free, -1)
                                g.indirect_dma_start(v_ring[:, k, :], None, A["peer_v"],
                                                     bass.IndirectOffsetOnAxis(expert[:, p, k:k + 1], 0)).then_inc(v_in[k], 16)

            pool.wait_ge(ff0_over, 1)
            pool.sem_inc(ff0_over, -1)
            g.memset(w_gates[0], 0.0).then_inc(pool_steps, 1)
            pool.wait_ge(pool_steps, steps.next())
            g.memset(w_gates[1], 0.0).then_inc(pool_steps, 1)
            pool.wait_ge(pool_steps, steps.next())
            g.memset(rec_in[:, :, 0:CONV_K - 1], 0.0).then_inc(pool_steps, 1)
            pool.wait_ge(pool_steps, steps.next())
            pool.sem_inc(rnn_zeroed, 1)
            for which, name in enumerate(("rg_w_a_2", "rg_w_x_2")):
                src = A[name][0].rearrange("(s b) i d -> b i s d", b=SUPER)
                for b in range(SUPER):
                    lo = b * LRU
                    while lo < (b + 1) * LRU:
                        hi = min((b + 1) * LRU, (lo // RC + 1) * RC)
                        pool.dma_start(w_gates[which][lo % RC:lo % RC + hi - lo, :, lo // RC, b * LRU:(b + 1) * LRU],
                                       src[b, lo - b * LRU:hi - b * LRU]).then_inc(rnn_w_in, 16)
                        lo = hi
            pool.sem_inc(pool_steps, -steps.reset())
            pool.wait_ge(rnn_over, 1)
            pool.sem_inc(rnn_over, -1)
            g.memset(c_pad, 0.0).then_inc(c_pad_zeroed, 1)
            pool.wait_ge(ff2_over, 1)
            pool.sem_inc(ff2_over, -1)
            g.memset(qTz2, 0.0).then_inc(heads_zeroed, 1)

        @block.scalar
        def _(act):
            a = nc.scalar
            steps = Count()
            act.wait_ge(consts, 1)
            act.sem_inc(job_taken, 4)
            act.wait_ge(c_turned, 1)
            act.sem_inc(c_turned, -1)
            a.activation(c_act[:], ps[:, 0, 0:KC], ACT.Silu).then_inc(c_act_ready, 1)

            def mean_square(source, t, give):
                a.activation(junk, source, ACT.Square, accum_out=mean_sq[:, t:t + 1]).then_inc(act_steps, 1)
                act.wait_ge(act_steps, steps.next())
                a.activation(rms[:, t:t + 1], mean_sq[:, t:t + 1], ACT.Sqrt, bias=eps[:], scale=1.0 / D).then_inc(give, 1)

            def norm_x():
                for t in range(TILES):
                    act.wait_ge(x_ready, 1)
                    act.sem_inc(x_ready, -1)
                    mean_square(x[:, t, :], t, rms_ready)
                act.sem_inc(act_steps, -steps.reset())

            def acc_rows(t):
                return ps[:, 2 * t:2 * t + 2, :].rearrange("p b n -> p (b n)")

            def norm_acc():
                a.activation(root_table[:], eps[:], ACT.Sqrt).then_inc(act_steps, 1)
                act.wait_ge(act_steps, steps.next())
                for t in range(TILES):
                    act.wait_ge(rows_done, 1)
                    act.sem_inc(rows_done, -1)
                    if t == TILES - 1:
                        act.sem_inc(slot_free, 1)
                    mean_square(acc_rows(t), t, rms2_ready)
                act.sem_inc(act_steps, -steps.reset())

            def evacuate_hT(target):
                for t in range(TILES):
                    for half in range(2):
                        act.wait_ge(hT_turned, 1)
                        act.sem_inc(hT_turned, -1)
                        a.activation(target[:, 4 * half:4 * half + 4, t * P:(t + 1) * P],
                                     ps[:, WORK + 2 * t + half, :].rearrange("p (k t) -> p k t", t=P), ACT.Copy).then_inc(hT_ready, 1)

            def high(n, hi, width, dmas=1):
                slot = n % SLOTS
                act.wait_ge(slot_in[slot], dmas * 16)
                act.sem_inc(slot_in[slot], -dmas * 16)
                a.activation(hi[:, slot, 0:width], ring[:, slot, 0:width], ACT.Copy).then_inc(w_hi_ready, 1)

            def bank(j):
                return WORK + j % 4

            def softmax_exps(n_units, S, sinks):
                units = attention_units(not sinks)
                for u in range(n_units):
                    b = u % 2
                    keys = SEQ if sinks else P * (units[u][0] + 1)
                    act.wait_ge(scores_ready, 1)
                    act.sem_inc(scores_ready, -1)
                    if sinks:
                        a.activation(sink_e[:, b, :], sink_d[:, b, :], ACT.Exp)
                    for i in range(GROUP):
                        ins = a.activation(S[:, b, i, 0:keys], S[:, b, i, 0:keys], ACT.Exp, bias=neg_max[:, b, i:i + 1],
                                           accum_out=row_sum[:, b, i:i + 1])
                    ins.then_inc(probs_ready, 1)
                    fan(act, sums_ready)
                    turned = pT if sinks else pT2
                    for half in range(2):
                        act.wait_ge(p_turned, 1)
                        act.sem_inc(p_turned, -1)
                        a.activation(turned[:, 4 * half:4 * half + 4, :], ps[:, half, :].rearrange("p (i t) -> p i t", t=P),
                                     ACT.Copy).then_inc(pT_ready, 1)

            act.wait_ge(angle_ready, 1)
            act.sem_inc(angle_ready, -1)
            a.activation(sine[:], angle[:, 2], ACT.Sin)
            a.activation(cosine[:], angle[:, 3], ACT.Sin).then_inc(rope_ready, 1)
            act.sem_inc(x_ready, TILES)
            with act.Fori(0, DEPTH) as l:
                act.wait_ge(x_ready, TILES)
                high(0, ada_hi, KC * ADA_N)
                high(1, ada_hi, KC * ADA_N)
                act.wait_ge(params_turned, 1)
                act.sem_inc(params_turned, -1)
                a.activation(mix_cols[:], ps[:, 0, 0:8], ACT.Copy)
                a.activation(keysT[:].rearrange("p s k -> p (s k)"), ps[:, 1, 0:2 * KEYS], ACT.Copy)

                def mod_block(i, u):
                    act.wait_ge(job_done, 1)
                    act.sem_inc(job_done, -1)
                    act.sem_inc(slot_free, 1)
                    a.activation(mod.rearrange("p s d -> p (s d)")[:, bass.ds(i * (4 * ADA_N) + u * ADA_N, ADA_N)], ps[:, bank(u), 0:ADA_N],
                                 ACT.Copy).then_inc(job_taken, 1)

                ADA_TURNS = 6 * D // (4 * ADA_N)
                with act.Fori(0, ADA_TURNS - 1) as i:
                    for u in range(4):
                        mod_block(i, u)
                        high(u + 2, ada_hi, KC * ADA_N)
                for u in range(4):
                    mod_block(ADA_TURNS - 1, u)
                    if u < 2:
                        high(u + 2, ada_hi, KC * ADA_N)
                    else:
                        high(u - 2, in_hi, KC * BLK)
                fan(act, mod_ready)
                act.wait_ge(x_loaded, 16)
                norm_x()
                evacuate_hT(hT_hi)
                job = 0
                for b in range(8):
                    for t in range(2):
                        act.wait_ge(job_done, 1)
                        act.sem_inc(job_done, -1)
                        if t == 1:
                            act.sem_inc(slot_free, 1)
                        if b < 2:
                            dst = qk[:, t, 0:Q_HEADS, :].rearrange("p (c g) d -> p g c d", g=KV_HEADS)[:, b]
                            src = ps[:, bank(job), 0:BLK].rearrange("p (c d) -> p c d", d=HEAD)
                        elif b == 2:
                            dst, src = qk[:, t, Q_HEADS:QK, :].rearrange("p h d -> p (h d)"), ps[:, bank(job), 0:KV_W]
                        elif b == 3:
                            dst, src = v_tok[:, t, :], ps[:, bank(job), 0:KV_W]
                        else:
                            dst, src = zc[:, 2 * (b - 4) + t, :], ps[:, bank(job), 0:SEQ]
                        a.activation(dst, src, ACT.Copy).then_inc(job_taken, 1)
                        job += 1
                    if b == 2:
                        fan(act, qk_ready)
                    if b + 2 < 8:
                        high(b + 2, in_hi, KC * (IN_CUT[b + 3] - IN_CUT[b + 2]))
                    if b == 3:
                        act.wait_ge(head_sq_ready, 1)
                        act.sem_inc(head_sq_ready, -1)
                        a.activation(head_rms[:], head_sq[:], ACT.Sqrt, bias=eps[:], scale=1.0 / HEAD).then_inc(head_rms_ready, 1)
                fan(act, zc_ready)
                for t in range(TILES):
                    act.wait_ge(qk_turned, 1)
                    act.sem_inc(qk_turned, -1)
                    for s in range(KV_HEADS):
                        rows = slice(HEAD * s, HEAD * s + HEAD)
                        a.activation(qTz[rows, GROUP * s:GROUP * s + GROUP, t * P:(t + 1) * P],
                                     ps[rows, WORK + t, :].rearrange("p (c t) -> p c t", t=P), ACT.Copy, scale=HEAD ** -0.5)
                act.wait_ge(qk_turned, 1)
                act.sem_inc(qk_turned, -1)
                a.activation(kT, ps[:, WORK + 2, 0:SEQ], ACT.Copy).then_inc(qkT_ready, 1)
                softmax_exps(TILES * KV_HEADS, scores, True)
                act.wait_ge(pool_done, 1)
                act.sem_inc(pool_done, -1)
                for cc in range(2):
                    a.activation(mixT[:, 6 + cc, :], ps[:, WORK + 2, cc * SEQ:(cc + 1) * SEQ], ACT.Copy, scale=mix_cols[:, 6 + cc:7 + cc])
                for t in range(TILES):
                    act.wait_ge(attn_turned, 1)
                    act.sem_inc(attn_turned, -1)
                    a.activation(mixT[:, 0:4, t * P:(t + 1) * P], ps[:, WORK + t, :].rearrange("p (c t) -> p c t", t=P),
                                 ACT.Copy).then_inc(mixT_ready, 1)
                high(0, in_hi, KC * BLK)
                high(1, in_hi, KC * BLK)
                norm_x()
                evacuate_hT(hT_hi)
                for j in range(16):
                    act.wait_ge(job_done, 1)
                    act.sem_inc(job_done, -1)
                    if j % 2 == 1 and j // 2 < 8 - SLOTS:
                        act.sem_inc(slot_free, 1)
                    a.activation(qpT[:, j, :], ps[:, bank(j), 0:SEQ], ACT.Copy).then_inc(job_taken, 1)
                    if j % 2 == 1 and j // 2 + 2 < 8:
                        high(j // 2 + 2, in_hi, KC * BLK)
                for j in range(8):
                    act.wait_ge(key_s_done, 1)
                    act.sem_inc(key_s_done, -1)
                    a.activation(key_s[:, 2 * j:2 * j + 2, :, :].rearrange("p n h k -> p (n h k)"), ps[:, j, :], ACT.Copy).then_inc(key_s_ready, 1)

                def gate_exp(p):
                    act.wait_ge(top_ready, 1)
                    act.sem_inc(top_ready, -1)
                    a.activation(gate_e[:, p, :], top[:, p, :], ACT.Exp, bias=neg_top[:, p, :], accum_out=gate_sum[:, p, :]).then_inc(gate_ready, 1)

                def gelu(half):
                    act.wait_ge(dots_ready, 1)
                    act.sem_inc(dots_ready, -1)
                    a.activation(acts[:, half, :], dots[:, half, :], ACT.Gelu).then_inc(acts_ready, 1)

                gate_exp(0)
                with act.Fori(0, UNITS // 2 - 1) as n2:
                    for p in range(2):
                        gelu(0)
                        gate_exp(1 - p)
                        gelu(1)
                gelu(0)
                gate_exp(1)
                gelu(1)
                gelu(0)
                gelu(1)

            def high_ff(n):
                high(n, w_hi, FF_SLOT, 3)

            def high_block(n):
                high(n, w_hi, KC * BLK)

            def feed_forward(f, ahead):
                n0 = first[f"ff{f}"]

                def silu(b):
                    act.wait_ge(gu_done, 1)
                    act.sem_inc(gu_done, -1)
                    a.activation(silu_g[:, b, :], ps[:, WORK + b, 0:SEQ], ACT.Silu).then_inc(silu_ready, 1)

                norm_x()
                if f < 2:
                    high_ff(n0)
                evacuate_hT(hT_hi)
                if f < 2:
                    high_ff(n0 + 1)
                with act.Fori(0, (FF_CHUNKS - 2) // SLOTS) as i:
                    for u in range(SLOTS):
                        silu(u % 2)
                        high_ff(n0 + 2 + u)
                for u in range(2):
                    silu(u)
                    if ahead is not None:
                        ahead(n0 + FF_CHUNKS + u)
                norm_acc()

            feed_forward(0, None)
            norm_x()
            evacuate_hT(hT)
            act.wait_ge(rnn_turned, 1)
            act.sem_inc(rnn_turned, -1)
            a.activation(rnn_cols[:].rearrange("p k c -> p (k c)"), ps[0:RC, 0, 0:8 * R_CHUNKS], ACT.Copy).then_inc(rnn_cols_ready, 1)
            job = 0
            for j in range(R_CHUNKS):
                act.wait_ge(job_done, 1)
                act.sem_inc(job_done, -1)
                if j % 4 == 3:
                    act.sem_inc(slot_free, 1)
                a.activation(gate_g[:, j, :], ps[0:RC, bank(job), 0:SEQ], ACT.Gelu_apprx_tanh).then_inc(job_taken, 1)
                job += 1
            act.wait_ge(lam_abs, 1)
            act.sem_inc(lam_abs, -1)
            a.activation(decay[:, 1, :], decay[:, 0, :], ACT.Exp, scale=-1.0).then_inc(lam_exp, 1)
            for j in range(R_CHUNKS):
                act.wait_ge(job_done, 1)
                act.sem_inc(job_done, -1)
                if j % 4 == 3:
                    act.sem_inc(slot_free, 1)
                a.activation(rec_in[:, j, CONV_K - 1:], ps[0:RC, bank(job), 0:SEQ], ACT.Copy).then_inc(job_taken, 1)
                job += 1
                if j % 3 == 2:
                    fan(act, rec_in_ready)
            for s in range(SUPER):
                for dst, row in ((gate_r, 5), (gate_i, 6)):
                    for jj in range(3):
                        j = 3 * s + jj
                        act.wait_ge(job_done, 1)
                        act.sem_inc(job_done, -1)
                        a.activation(dst[:, j, :], ps[0:RC, bank(job), 0:SEQ], ACT.Sigmoid, bias=rnn_cols[:, row, j:j + 1]).then_inc(job_taken, 1)
                        job += 1
            act.wait_ge(decay_ready, 1)
            act.sem_inc(decay_ready, -1)
            act.wait_ge(job_taken, 4)
            for j in range(R_CHUNKS):
                a.activation(decay_a[:, j, :], gate_r[:, j, :], ACT.Exp, scale=decay_neg[:, j:j + 1]).then_inc(act_steps, 1)
            steps.value += R_CHUNKS
            act.wait_ge(act_steps, steps.value)
            for s in range(SUPER):
                for j in range(3 * s, 3 * s + 3):
                    ins = a.activation(gate_r[:, j, :], gate_r[:, j, :], ACT.Tanh, scale=decay_pos[:, j:j + 1])
                ins.then_inc(gates_ready, 1)
            act.sem_inc(act_steps, -steps.reset())
            for s in range(SUPER):
                act.wait_ge(root_in, 1)
                act.sem_inc(root_in, -1)
                part = gate_r[:, 3 * s:3 * s + 3, :]
                a.activation(part, part, ACT.Sqrt).then_inc(root_ready, 1)
            norm_acc()
            feed_forward(1, high_block)
            norm_x()
            evacuate_hT(hT_hi)
            act.wait_ge(job_done, 1)
            act.sem_inc(job_done, -1)
            a.activation(f_tok[:], ps[:, bank(0), 0:TILES * HEADS2], ACT.Copy).then_inc(f_ready, 1)
            fan(act, job_taken)
            act.wait_ge(f_abs, 1)
            act.sem_inc(f_abs, -1)
            a.activation(logs[:, 1, :], logs[:, 0, :], ACT.Exp, scale=-1.0).then_inc(f_exp, 1)
            n0 = first["kv"]
            for j in range(16):
                act.wait_ge(job_done, 1)
                act.sem_inc(job_done, -1)
                if j % 2 == 1:
                    act.sem_inc(slot_free, 1)
                b = j // 2
                dst = kT2[:, j, :] if b < 4 else v2[:, j % 2, (b - 4) * BLK:(b - 3) * BLK]
                a.activation(dst, ps[:, bank(j + 1), 0:BLK], ACT.Copy).then_inc(job_taken, 1)
                if j % 2 == 1:
                    if b + 2 < 8:
                        high_block(n0 + b + 2)
                    else:
                        high_ff(n0 + b + 2)
            act.wait_ge(c_summed, 1)
            act.sem_inc(c_summed, -1)
            a.activation(c_tok[:], ps[:, 0, 0:TILES * HEADS2], ACT.Copy)
            act.wait_ge(c_pad_zeroed, 1)
            a.activation(c_pad[:, :, 0:HEADS2], ps[:, 0, 0:TILES * HEADS2].rearrange("p (t h) -> p t h", t=TILES), ACT.Copy,
                         scale=-1.0).then_inc(c_ready, 1)
            act.wait_ge(c_back, 1)
            act.sem_inc(c_back, -1)
            a.activation(neg_cT, ps[:, 1, 0:SEQ], ACT.Copy).then_inc(neg_cT_ready, 1)
            feed_forward(2, high_block)
            norm_x()
            evacuate_hT(hT_hi)
            act.wait_ge(heads_zeroed, 1)
            act.sem_inc(heads_zeroed, -1)
            n0 = first["q"]
            for j in range(8):
                act.wait_ge(job_done, 1)
                act.sem_inc(job_done, -1)
                if j % 2 == 1:
                    act.sem_inc(slot_free, 1)
                for s in range(2):
                    rows, head = slice(HEAD * s, HEAD * s + HEAD), 2 * j + s
                    ins = a.activation(qTz2[rows, head // GROUP, head % GROUP, :], ps[rows, bank(j), 0:SEQ], ACT.Copy, scale=HEAD ** -0.5)
                ins.then_inc(job_taken, 1)
                if j % 2 == 1:
                    high_block(n0 + j // 2 + 2)
            softmax_exps(TILES * HEADS2 // GROUP, scores2, False)
            evacuate_hT(hT_hi)
            n0 = first["o"]
            for u in range(2):
                high_block(n0 + 2 + u)
            for u in range(2):
                high_ff(n0 + 4 + u)
            norm_acc()
            feed_forward(3, None)

        @block.tensor
        def _(pe):
            mm = nc.tensor.matmul
            pe.sem_inc(slot_free, SLOTS)
            pe.wait_ge(consts, 1)
            pe.wait_ge(c_loaded, 16)
            pe.sem_inc(c_loaded, -16)
            nc.tensor.transpose(ps[:, 0, 0:KC], c_rows[:], ident[0:KC, 0:KC]).then_inc(c_turned, 1)
            pe.wait_ge(pos_float, 1)
            pe.sem_inc(pos_float, -1)
            nc.tensor.transpose(ps[:, 3, 0:TILES], pos_f[:], ident[0:TILES, 0:TILES]).then_inc(pos_turned, 1)
            pe.wait_ge(c_split, 1)
            pe.sem_inc(c_split, -1)

            def bank(j):
                return WORK + j % 4

            def turn_h(ready=hT_ready):
                for t in range(TILES):
                    pe.wait_ge(h_ready, 1)
                    pe.sem_inc(h_ready, -1)
                    for half in range(2):
                        for k in range(4):
                            ins = nc.tensor.transpose(ps[:, WORK + 2 * t + half, k * P:(k + 1) * P],
                                                      h[:, t, (4 * half + k) * P:(4 * half + k + 1) * P], ident[:])
                        ins.then_inc(hT_turned, 1)
                pe.wait_ge(ready, 4)
                pe.sem_inc(ready, -4)

            def weights(n):
                pe.wait_ge(plain_in[n % SLOTS], 16)
                pe.sem_inc(plain_in[n % SLOTS], -16)
                return ring[:, n % SLOTS, :]

            def three_passes(where, pairs):
                for k, (w_high, w_low, s_high, s_low) in enumerate(pairs):
                    mm(where, w_high, s_high, start=(k == 0), stop=False)
                    mm(where, w_high, s_low, start=False, stop=False)
                    ins = mm(where, w_low, s_high, start=False, stop=(k == len(pairs) - 1))
                return ins

            def split_weights(n, hi, width):
                pe.wait_ge(w_split, 1)
                pe.sem_inc(w_split, -1)
                return [part[:, n % SLOTS, 0:KC * width].rearrange("p (k n) -> p k n", k=KC) for part in (hi, ring_lo)]

            def channel_job(j, w, col, low):
                pe.wait_ge(job_taken, 1)
                pe.sem_inc(job_taken, -1)
                cols = slice(col, col + P)
                three_passes(ps[:, bank(j), 0:SEQ], [(w[0][:, k, cols], w[1][:, k, cols], hT_hi[:, k, :], low[:, k, :])
                                                     for k in range(KC)]).then_inc(job_done, 1)

            def token_job(j, w, width, t, low):
                pe.wait_ge(job_taken, 1)
                pe.sem_inc(job_taken, -1)
                tokens = slice(t * P, (t + 1) * P)
                three_passes(ps[:, bank(j), 0:width], [(hT_hi[:, k, tokens], low[:, k, tokens], w[0][:, k, :], w[1][:, k, :])
                                                       for k in range(KC)]).then_inc(job_done, 1)

            def plain_channel_job(j, w, width, col, m):
                pe.wait_ge(job_taken, 1)
                pe.sem_inc(job_taken, -1)
                wk = w[:, 0:KC * width].rearrange("p (k n) -> p k n", k=KC)
                for k in range(KC):
                    ins = mm(ps[0:m, bank(j), 0:SEQ], wk[:, k, col:col + m], hT[:, k, :], start=(k == 0), stop=(k == KC - 1))
                ins.then_inc(job_done, 1)

            def accumulate_rows(parts, start, stop, n_slot=None):
                for t in range(TILES):
                    for i, (source, w) in enumerate(parts):
                        for c in range(2):
                            ins = mm(ps[:, 2 * t + c, :], source[:, t * P:(t + 1) * P], w[:, c * N:(c + 1) * N],
                                     start=start and i == 0, stop=stop and i == len(parts) - 1)
                    if stop:
                        ins.then_inc(rows_done, 1)
                return ins

            def row_product(n, count, sources, rows):
                per = len(sources) // count
                for u in range(count):
                    w = weights(n + u)[0:rows].rearrange("p (k n) -> p k n", n=D)
                    for k in range(per):
                        i = u * per + k
                        ins = accumulate_rows([(sources[i], w[:, k, :])], i == 0, i == len(sources) - 1)
                    if u < count - 1:
                        ins.then_inc(slot_free, 1)

            def attend(second):
                units = attention_units(second)
                keys_of, turned = (lambda i: kT2[:, i // 2, :], pT2) if second else (lambda i: kT, pT)
                S = scores2 if second else scores

                def score(u):
                    t, heads = units[u]
                    n = P * (t + 1) if second else SEQ
                    for i, head in enumerate(heads):
                        where = ps[:, WORK + 2 * (u % 2) + i // 2, (i % 2) * SEQ:(i % 2) * SEQ + n]
                        query = qTz2[:, head // GROUP, head % GROUP, :] if second else qTz[:, head, :]
                        ins = mm(where, query[:, t * P:(t + 1) * P], keys_of(head)[:, 0:n], start=True, stop=not second)
                        if second:
                            ins = mm(where, ident[:, head:head + 1].to_broadcast([P, P]), neg_cT[:, 0:n], start=False, stop=True)
                    ins.then_inc(scores_done, 1)

                score(0)
                for u, (t, heads) in enumerate(units):
                    if u + 1 < len(units):
                        score(u + 1)
                    chunks = t + 1 if second else TILES
                    pe.wait_ge(probs_ready, 1)
                    pe.sem_inc(probs_ready, -1)
                    for half in range(2):
                        for i in range(2 * half, 2 * half + 2):
                            for k in range(TILES):
                                src = min(k, chunks - 1)
                                ins = nc.tensor.transpose(ps[:, half, ((2 * i + k) % 4) * P:((2 * i + k) % 4 + 1) * P],
                                                          S[:, u % 2, i, src * P:(src + 1) * P], ident[:])
                        ins.then_inc(p_turned, 1)
                    pe.wait_ge(pT_ready, 2)
                    pe.sem_inc(pT_ready, -2)
                    if u >= 2:
                        pe.wait_ge(attn_done, 1)
                        pe.sem_inc(attn_done, -1)
                    for i, head in enumerate(heads):
                        for k in range(chunks):
                            values = v2[:, k, head * HEAD:(head + 1) * HEAD] if second else \
                                v_tok[:, k, (head // GROUP) * HEAD:(head // GROUP + 1) * HEAD]
                            ins = mm(ps[:, 2 + u % 2, i * HEAD:(i + 1) * HEAD], turned[:, 2 * i + k, :], values,
                                     start=(k == 0), stop=(k == chunks - 1))
                    ins.then_inc(pv_done, 1)
                pe.wait_ge(attn_done, 2)
                pe.sem_inc(attn_done, -2)

            with pe.Fori(0, DEPTH) as l:
                pe.wait_ge(pe_params, 5 * 16)
                pe.sem_inc(pe_params, -5 * 16)
                pe.wait_ge(acc_read, 1)
                pe.sem_inc(acc_read, -1)
                nc.tensor.transpose(ps[:, 0, 0:8], mix_rows[:], ident[0:8, 0:8])
                for s in range(2):
                    ins = nc.tensor.transpose(ps[:, 1, s * KEYS:(s + 1) * KEYS], keys_raw[:, s, :], ident[:])
                ins.then_inc(params_turned, 1)
                pe.wait_ge(bias_in, 16)
                pe.sem_inc(bias_in, -16)
                with pe.Fori(0, 6 * D // (4 * ADA_N)) as i:
                    for u in range(4):
                        w = split_weights(u, ada_hi, ADA_N)
                        pe.wait_ge(job_taken, 1)
                        pe.sem_inc(job_taken, -1)
                        where = ps[:, bank(u), 0:ADA_N]
                        mm(where, ident[0:4, u:u + 1].to_broadcast([4, P]), ada_bias[:, bass.ds(i * ADA_N, ADA_N)], start=True, stop=False)
                        for k in range(KC):
                            c_high, c_low = [part[:, k:k + 1].to_broadcast([P, P]) for part in (c_hi, c_lo)]
                            mm(where, c_high, w[0][:, k, :], start=False, stop=False)
                            mm(where, c_high, w[1][:, k, :], start=False, stop=False)
                            ins = mm(where, c_low, w[0][:, k, :], start=False, stop=(k == KC - 1))
                        ins.then_inc(job_done, 1)
                turn_h(hT_split)
                job = 0
                for b in range(8):
                    width = IN_CUT[b + 1] - IN_CUT[b]
                    w = split_weights(b, in_hi, width)
                    for t in range(2):
                        if b < 4:
                            token_job(job, w, width, t, hT_lo1)
                        else:
                            channel_job(job, w, t * P, hT_lo1)
                        job += 1
                pe.wait_ge(qk_done, 1)
                pe.sem_inc(qk_done, -1)
                pe.wait_ge(job_taken, 4)
                for t in range(TILES):
                    for c in range(4):
                        ins = nc.tensor.transpose(ps[:, WORK + t, c * P:(c + 1) * P],
                                                  qk[:, t, 2 * c:2 * c + 2, :].rearrange("p h d -> p (h d)"), ident[:])
                    ins.then_inc(qk_turned, 1)
                for t in range(TILES):
                    ins = nc.tensor.transpose(ps[:, WORK + 2, t * P:(t + 1) * P],
                                              qk[:, t, Q_HEADS:QK, :].rearrange("p h d -> p (h d)"), ident[:])
                ins.then_inc(qk_turned, 1)
                pe.wait_ge(qkT_ready, 1)
                pe.sem_inc(qkT_ready, -1)
                attend(False)
                pe.wait_ge(pooled_ready, 1)
                pe.sem_inc(pooled_ready, -1)
                for cc in range(2):
                    ins = mm(ps[:, WORK + 2, cc * SEQ:(cc + 1) * SEQ], pool_w[:, cc, :], pooled[:, cc, :], start=True, stop=True)
                ins.then_inc(pool_done, 1)
                for t in range(TILES):
                    for c in range(4):
                        ins = nc.tensor.transpose(ps[:, WORK + t, c * P:(c + 1) * P], attn[:, t, c * P:(c + 1) * P], ident[:])
                    ins.then_inc(attn_turned, 1)
                pe.wait_ge(mixT_ready, TILES)
                pe.sem_inc(mixT_ready, -TILES)
                row_product(0, 4, [mixT[:, k, :] for k in range(KC)], P)
                turn_h(hT_split)
                for b in range(8):
                    w = split_weights(b, in_hi, BLK)
                    for c in range(2):
                        channel_job(2 * b + c, w, c * P, hT_lo1)
                pe.wait_ge(job_taken, 4)
                for t in range(TILES):
                    for j in range(4):
                        for i in range(4):
                            c = 4 * j + i
                            ins = mm(ps[:, 4 * t + j, i * KEYS:(i + 1) * KEYS], qpT[:, c, t * P:(t + 1) * P], keysT[:, c % 2, :],
                                     start=True, stop=True)
                        ins.then_inc(key_s_done, 1)
                pe.wait_ge(diag_ready, 1)
                for b in range(4):
                    mm(ps[:, b, :], zeros[:], h[:, 0, 0:N], start=True, stop=False, skip_group_check=True)
                for t in range(TILES):
                    with pe.Fori(0, EXPERT_HEADS // 2) as i:
                        for p in range(2):
                            for k in range(TOPK):
                                pe.wait_ge(diag_ready, 1)
                                pe.sem_inc(diag_ready, -1)
                                pe.wait_ge(v_in[k], (l * UNITS + (i * 2 + (t * EXPERT_HEADS + p + 1))) * 16)
                                for c in range(2):
                                    ins = mm(ps[:, 2 * t + c, :], diag[:, k, :], v_ring[:, k, c * N:(c + 1) * N],
                                             start=False, stop=False, skip_group_check=True)
                                ins.then_inc(v_free, 1)
                                if k % GRP == GRP - 1:
                                    fan(pe, diag_free)
                    fan(pe, y_ready)

            def feed_forward(f):
                turn_h(hT_split)
                n0 = first[f"ff{f}"]

                def gate_up(n, b):
                    pe.wait_ge(w_split, 1)
                    pe.sem_inc(w_split, -1)
                    hi = w_hi[:, n % SLOTS, :].rearrange("p (k m) -> p k m", m=P)
                    lo = ring_lo[:, n % SLOTS, 0:FF_SLOT].rearrange("p (k m) -> p k m", m=P)
                    for g in range(2):
                        ins = three_passes(ps[:, WORK + b, g * SEQ:(g + 1) * SEQ],
                                           [(hi[:, g * KC + k, :], lo[:, g * KC + k, :], hT_hi[:, k, :], hT_lo[:, k, :]) for k in range(KC)])
                    ins.then_inc(gu_done, 1)

                def down(n, b, start=False, stop=False):
                    pe.wait_ge(ff_ready, 1)
                    pe.sem_inc(ff_ready, -1)
                    hi, lo = w_hi[:, n % SLOTS, 2 * KC * P:], ring_lo[:, n % SLOTS, 2 * KC * P:FF_SLOT]
                    ins = accumulate_rows([(ff_hi[:, b, :], hi), (ff_hi[:, b, :], lo), (ff_lo[:, b, :], hi)], start, stop)
                    if not stop:
                        ins.then_inc(slot_free, 1)

                gate_up(n0, 0)
                for j in range(1, PEEL):
                    gate_up(n0 + j, j % 2)
                    down(n0 + j - 1, (j - 1) % 2, start=(j == 1))
                with pe.Fori(0, TURNS) as i:
                    for u in range(SLOTS):
                        gate_up(n0 + PEEL + u, (PEEL + u) % 2)
                        down(n0 + PEEL + u - 1, (PEEL + u - 1) % 2)
                down(n0 + FF_CHUNKS - 1, (FF_CHUNKS - 1) % 2, stop=True)

            feed_forward(0)
            turn_h()
            pe.wait_ge(rnn_rows_in, 5 * 16)
            pe.sem_inc(rnn_rows_in, -5 * 16)
            nc.tensor.transpose(ps[0:RC, 0, 0:8 * R_CHUNKS], rnn_rows[:], ident[0:8 * R_CHUNKS, 0:8 * R_CHUNKS]).then_inc(rnn_turned, 1)
            job = 0
            for b in range(6):
                w = weights(first["rnn_in"] + b)
                for c in range(4):
                    plain_channel_job(job, w, 4 * RC, c * RC, RC)
                    job += 1
            pe.wait_ge(rnn_w_in, 2 * 6 * 16)
            for s in range(SUPER):
                pe.wait_ge(rec_ready, 1)
                pe.sem_inc(rec_ready, -1)
                for which in range(2):
                    for jj in range(3):
                        pe.wait_ge(job_taken, 1)
                        pe.sem_inc(job_taken, -1)
                        near = [i for i in range(3) if abs(i - jj) <= 1]
                        for i in near:
                            ins = mm(ps[0:RC, bank(job), 0:SEQ], w_gates[which][:, s, i, jj * RC:(jj + 1) * RC], rec[:, 3 * s + i, :],
                                     start=(i == near[0]), stop=(i == near[-1]))
                        ins.then_inc(job_done, 1)
                        job += 1
            pe.wait_ge(rnn_out_ready, 1)
            pe.sem_inc(rnn_out_ready, -1)
            row_product(first["rnn_out"], 3, [gate_g[:, j, :] for j in range(R_CHUNKS)], RC)
            feed_forward(1)
            turn_h(hT_split)
            pe.wait_ge(wf_in, 32)
            pe.sem_inc(wf_in, -32)
            pe.wait_ge(job_taken, 1)
            pe.sem_inc(job_taken, -1)
            for t in range(TILES):
                where = ps[:, bank(0), t * HEADS2:(t + 1) * HEADS2]
                for k in range(KC):
                    for i, part in enumerate((hT_hi, hT_lo)):
                        mm(where, part[:, k, t * P:(t + 1) * P].bitcast(F32), wf[:, k, :], start=(k == 0 and i == 0), stop=False)
                ins = mm(where, ones[0:1, :], bf[:], start=False, stop=True)
            ins.then_inc(job_done, 1)
            for b in range(8):
                w = split_weights(first["kv"] + b, w_hi, BLK)
                for c in range(2):
                    if b < 4:
                        channel_job(2 * b + c + 1, w, c * P, hT_lo)
                    else:
                        token_job(2 * b + c + 1, w, BLK, c, hT_lo)
            pe.wait_ge(log_f_ready, 1)
            pe.sem_inc(log_f_ready, -1)
            mm(ps[:, 0, 0:HEADS2], upto[:], log_f[:, 0:HEADS2], start=True, stop=True)
            mm(ps[:, 0, HEADS2:2 * HEADS2], ones[:], log_f[:, 0:HEADS2], start=True, stop=False)
            mm(ps[:, 0, HEADS2:2 * HEADS2], upto[:], log_f[:, HEADS2:2 * HEADS2], start=False, stop=True).then_inc(c_summed, 1)
            pe.wait_ge(c_ready, 1)
            pe.sem_inc(c_ready, -1)
            for t in range(TILES):
                ins = nc.tensor.transpose(ps[:, 1, t * P:(t + 1) * P], c_pad[:, t, :], ident[:])
            ins.then_inc(c_back, 1)
            pe.wait_ge(neg_cT_ready, 1)
            pe.sem_inc(neg_cT_ready, -1)
            feed_forward(2)
            turn_h(hT_split)
            for b in range(4):
                w = split_weights(first["q"] + b, w_hi, BLK)
                for c in range(2):
                    channel_job(2 * b + c, w, c * P, hT_lo)
            pe.wait_ge(job_taken, 4)
            attend(True)
            turn_h(hT_split)
            for b in range(4):
                pe.wait_ge(w_split, 1)
                pe.sem_inc(w_split, -1)
                hi, lo = [part[:, (first["o"] + b) % SLOTS, 0:ROWS * D].rearrange("p (k n) -> p k n", n=D) for part in (w_hi, ring_lo)]
                for i in range(ROWS):
                    k = b * ROWS + i
                    ins = accumulate_rows([(hT_hi[:, k, :], hi[:, i, :]), (hT_hi[:, k, :], lo[:, i, :]), (hT_lo[:, k, :], hi[:, i, :])],
                                          k == 0, k == KC - 1)
                if b < 3:
                    ins.then_inc(slot_free, 1)
            feed_forward(3)

        @block.vector
        def _(dve):
            v = nc.vector
            steps = Count()
            dve.wait_ge(consts, 1)
            dve.sem_inc(pre_free, 1)
            dve.sem_inc(post_free, 1)
            dve.sem_inc(u_free, U_SLOTS)
            dve.sem_inc(v_free, V_SLOTS)
            dve.sem_inc(diag_free, 2)
            dve.sem_inc(acc_read, 1)
            dve.wait_ge(pos_loaded, 16)
            dve.sem_inc(pos_loaded, -16)
            v.tensor_copy(pos_f[:], pos_i[:]).then_inc(pos_float, 1)
            dve.wait_ge(c_act_ready, 1)
            dve.sem_inc(c_act_ready, -1)
            v.tensor_copy(c_hi[:], c_act[:]).then_inc(dve_steps, 1)
            dve.wait_ge(dve_steps, steps.next())
            v.tensor_tensor(c_lo[:], c_act[:], c_hi[:].bitcast(F32), ALU.subtract).then_inc(c_split, 1)
            dve.wait_ge(pos_turned, 1)
            dve.sem_inc(pos_turned, -1)
            v.tensor_copy(pos[:], ps[:, 3, 0:TILES]).then_inc(dve_steps, 1)
            dve.wait_ge(dve_steps, steps.next())
            two_pi = 2.0 * np.pi
            part1 = 6.28125
            part2 = float(np.float32(np.round((two_pi - part1) * 2.0 ** 21) / 2.0 ** 21))
            part3 = float(np.float32(two_pi - part1 - part2))
            near = 1.5 * 2.0 ** 23
            pi = float(np.nextafter(np.float32(np.pi), np.float32(0.0)))
            half = ROPE // 2
            for t in range(TILES):
                v.tensor_scalar(angle[:, 0, t, :], inv_freq[:], pos[:, t:t + 1], None, ALU.mult).then_inc(dve_steps, 1)
                dve.wait_ge(dve_steps, steps.next())
            v.tensor_scalar(angle[:, 1], angle[:, 0], float(1.0 / two_pi), None, ALU.mult).then_inc(dve_steps, 1)
            dve.wait_ge(dve_steps, steps.next())
            v.tensor_scalar(angle[:, 1], angle[:, 1], near, None, ALU.add).then_inc(dve_steps, 1)
            dve.wait_ge(dve_steps, steps.next())
            v.tensor_scalar(angle[:, 1], angle[:, 1], near, None, ALU.subtract).then_inc(dve_steps, 1)
            dve.wait_ge(dve_steps, steps.next())
            for part in (part1, part2, part3):
                v.scalar_tensor_tensor(angle[:, 0], angle[:, 1], -part, angle[:, 0], ALU.mult, ALU.add).then_inc(dve_steps, 1)
                dve.wait_ge(dve_steps, steps.next())
            v.tensor_scalar(angle[:, 2], angle[:, 0], pi, -pi, ALU.min, ALU.max).then_inc(dve_steps, 1)
            dve.wait_ge(dve_steps, steps.next())
            v.tensor_scalar(angle[:, 3], angle[:, 2], float(np.pi / 2), None, ALU.add).then_inc(dve_steps, 1)
            dve.wait_ge(dve_steps, steps.next())
            v.tensor_scalar(angle[:, 1], angle[:, 3], pi, None, ALU.is_gt).then_inc(dve_steps, 1)
            dve.wait_ge(dve_steps, steps.next())
            v.scalar_tensor_tensor(angle[:, 3], angle[:, 1], -two_pi, angle[:, 3], ALU.mult, ALU.add).then_inc(dve_steps, 1)
            dve.wait_ge(dve_steps, steps.next())
            v.tensor_scalar(angle[:, 3], angle[:, 3], pi, -pi, ALU.min, ALU.max).then_inc(angle_ready, 1)
            dve.wait_ge(tables, 1)
            v.reciprocal(window_count[:], window_count[:]).then_inc(dve_steps, 1)
            dve.wait_ge(dve_steps, steps.next())
            dve.sem_inc(dve_steps, -steps.reset())

            def normalise(scale, shift):
                for t in range(TILES):
                    dve.wait_ge(rms_ready, 1)
                    dve.sem_inc(rms_ready, -1)
                    v.reciprocal(rstd[:, t:t + 1], rms[:, t:t + 1]).then_inc(dve_steps, 1)
                    dve.wait_ge(dve_steps, steps.next())
                    ins = v.scalar_tensor_tensor(h[:, t, :], x[:, t, :], rstd[:, t:t + 1], scale, ALU.mult, ALU.mult)
                    if shift is not None:
                        ins.then_inc(dve_steps, 1)
                        dve.wait_ge(dve_steps, steps.next())
                        ins = v.tensor_tensor(h[:, t, :], h[:, t, :], shift, ALU.add)
                    ins.then_inc(h_ready, 1)

            def low(n, hi, width):
                slot = n % SLOTS
                dve.wait_ge(w_hi_ready, 1)
                dve.sem_inc(w_hi_ready, -1)
                v.tensor_tensor(ring_lo[:, slot, 0:width], ring[:, slot, 0:width], hi[:, slot, 0:width].bitcast(F32),
                                ALU.subtract).then_inc(w_split, 1)

            def split_hT(low_part):
                for t in range(TILES):
                    for k in range(2):
                        dve.wait_ge(hT_ready, 1)
                        dve.sem_inc(hT_ready, -1)
                        part = (slice(None), slice(4 * k, 4 * k + 4), slice(t * P, (t + 1) * P))
                        v.tensor_tensor(low_part[part], ps[:, WORK + 2 * t + k, :].rearrange("p (k t) -> p k t", t=P),
                                        hT_hi[part].bitcast(F32), ALU.subtract).then_inc(hT_split, 1)

            def acc_rows(t):
                return ps[:, 2 * t:2 * t + 2, :].rearrange("p b n -> p (b n)")

            def add_gated(t, segment):
                v.tensor_tensor(h[:, t, :], acc_rows(t), mod[:, segment, :], ALU.mult).then_inc(dve_steps, 1)
                dve.wait_ge(dve_steps, steps.next())
                v.tensor_tensor(x[:, t, :], x[:, t, :], h[:, t, :], ALU.add).then_inc(x_ready, 1)

            def add_normed(weight, give):
                dve.wait_ge(post_in, 16)
                dve.sem_inc(post_in, -16)
                for t in range(TILES):
                    dve.wait_ge(rms2_ready, 1)
                    dve.sem_inc(rms2_ready, -1)
                    v.reciprocal(rstd[:, t:t + 1], rms[:, t:t + 1]).then_inc(dve_steps, 1)
                    dve.wait_ge(dve_steps, steps.next())
                    v.scalar_tensor_tensor(h[:, t, :], acc_rows(t), rstd[:, t:t + 1], gain_post[:], ALU.mult, ALU.mult).then_inc(dve_steps, 1)
                    dve.wait_ge(dve_steps, steps.next())
                    v.scalar_tensor_tensor(x[:, t, :], h[:, t, :], weight, x[:, t, :], ALU.mult, ALU.add).then_inc(give, 1)
                dve.sem_inc(post_free, 1)
                dve.sem_inc(dve_steps, -steps.reset())

            def pre_norm():
                dve.wait_ge(pre_in, 16)
                dve.sem_inc(pre_in, -16)
                normalise(gain_pre[:], None)
                fan(dve, pre_free)
                dve.sem_inc(dve_steps, -steps.reset())

            def softmax_rows(second):
                units = attention_units(second)
                S = scores2 if second else scores

                def rows(u):
                    t, heads = units[u]
                    b = u % 2
                    n = P * (t + 1) if second else SEQ
                    dve.wait_ge(scores_done, 1)
                    dve.sem_inc(scores_done, -1)
                    if second:
                        mask = window[:, 0, SEQ - n:SEQ]
                        for i, head in enumerate(heads):
                            ins = v.scalar_tensor_tensor(S[:, b, i, 0:n], ps[:, WORK + 2 * b + i // 2, (i % 2) * SEQ:(i % 2) * SEQ + n],
                                                         c_tok[:, t * HEADS2 + head:t * HEADS2 + head + 1], mask, ALU.add, ALU.add)
                    else:
                        for pair in range(2):
                            ins = v.tensor_tensor(S[:, b, 2 * pair:2 * pair + 2, :],
                                                  ps[:, WORK + 2 * b + pair, :].rearrange("p (i t) -> p i t", t=SEQ),
                                                  window[:, t:t + 1, :].to_broadcast([P, 2, SEQ]), ALU.add)
                    ins.then_inc(dve_steps, 1)
                    dve.wait_ge(dve_steps, steps.next())
                    v.tensor_reduce(row_max[:, b, :], S[:, b, :, 0:n], AX_X, ALU.max).then_inc(dve_steps, 1)
                    dve.wait_ge(dve_steps, steps.next())
                    if not second:
                        sinks = sink[:, heads[0]:heads[0] + GROUP]
                        v.tensor_tensor(row_max[:, b, :], row_max[:, b, :], sinks, ALU.max).then_inc(dve_steps, 1)
                        dve.wait_ge(dve_steps, steps.next())
                        v.tensor_tensor(sink_d[:, b, :], sinks, row_max[:, b, :], ALU.subtract).then_inc(dve_steps, 1)
                        dve.wait_ge(dve_steps, steps.next())
                    v.tensor_scalar(neg_max[:, b, :], row_max[:, b, :], -1.0, None, ALU.mult).then_inc(scores_ready, 1)

                def close(u):
                    t, heads = units[u]
                    b = u % 2
                    dve.wait_ge(sums_ready, 1)
                    dve.sem_inc(sums_ready, -1)
                    if not second:
                        v.tensor_tensor(row_sum[:, b, :], row_sum[:, b, :], sink_e[:, b, :], ALU.add).then_inc(dve_steps, 1)
                        dve.wait_ge(dve_steps, steps.next())
                    v.reciprocal(row_inv[:, b, :], row_sum[:, b, :]).then_inc(dve_steps, 1)
                    dve.wait_ge(dve_steps, steps.next())
                    dve.wait_ge(pv_done, 1)
                    dve.sem_inc(pv_done, -1)
                    dst = (h if second else attn)[:, t, heads[0] * HEAD:(heads[0] + GROUP) * HEAD]
                    v.tensor_tensor(dst.rearrange("p (i d) -> p i d", d=HEAD),
                                    ps[:, 2 + b, 0:GROUP * HEAD].rearrange("p (i d) -> p i d", d=HEAD),
                                    row_inv[:, b, :].unsqueeze(2).to_broadcast([P, GROUP, HEAD]), ALU.mult).then_inc(attn_done, 1)

                for u in range(len(units)):
                    rows(u)
                    if u >= 1:
                        close(u - 1)
                close(len(units) - 1)
                dve.sem_inc(dve_steps, -steps.reset())

            with dve.Fori(0, DEPTH) as l:
                v.tensor_scalar(expert_base[:], expert_base[:], float(EXPERTS), None, ALU.add).then_inc(dve_steps, 1)
                dve.wait_ge(dve_steps, steps.next())
                with dve.Fori(0, 6 * D // (4 * ADA_N)) as i:
                    for u in range(4):
                        low(u, ada_hi, KC * ADA_N)
                for u in range(2):
                    low(u, in_hi, KC * BLK)
                dve.wait_ge(mod_ready, 1)
                dve.sem_inc(mod_ready, -1)
                dve.wait_ge(pre_in, 16)
                dve.sem_inc(pre_in, -16)
                v.scalar_tensor_tensor(mod[:, 1, :], mod[:, 1, :], 1.0, gain_pre[:], ALU.add, ALU.mult).then_inc(dve_steps, 1)
                dve.wait_ge(dve_steps, steps.next())
                dve.sem_inc(pre_free, 1)
                normalise(mod[:, 1, :], mod[:, 0, :])
                dve.wait_ge(post_in, 16)
                dve.sem_inc(post_in, -16)
                v.scalar_tensor_tensor(mod[:, 4, :], mod[:, 4, :], 1.0, gain_post[:], ALU.add, ALU.mult).then_inc(dve_steps, 1)
                dve.wait_ge(dve_steps, steps.next())
                dve.sem_inc(post_free, 1)
                split_hT(hT_lo1)

                def low_in(b):
                    low(b, in_hi, KC * (IN_CUT[b + 1] - IN_CUT[b]))

                for b in range(2, 5):
                    low_in(b)
                dve.wait_ge(dve_params, 3 * 16)
                dve.sem_inc(dve_params, -3 * 16)
                dve.wait_ge(qk_ready, 1)
                dve.sem_inc(qk_ready, -1)
                v.tensor_tensor(qk_sq[:], qk[:], qk[:], ALU.mult).then_inc(dve_steps, 1)
                dve.wait_ge(dve_steps, steps.next())
                v.tensor_reduce(head_sq[:], qk_sq[:], AX_X, ALU.add).then_inc(head_sq_ready, 1)
                low_in(5)
                dve.wait_ge(head_rms_ready, 1)
                dve.sem_inc(head_rms_ready, -1)
                v.reciprocal(head_rms[:], head_rms[:]).then_inc(dve_steps, 1)
                dve.wait_ge(dve_steps, steps.next())
                v.tensor_tensor(qk[:], qk[:], head_rms[:].unsqueeze(3).to_broadcast([P, TILES, QK, HEAD]), ALU.mult).then_inc(dve_steps, 1)
                dve.wait_ge(dve_steps, steps.next())
                low_in(6)
                for t in range(TILES):
                    v.tensor_tensor(qk[:, t], qk[:, t], qk_gain[:], ALU.mult).then_inc(dve_steps, 1)
                    dve.wait_ge(dve_steps, steps.next())
                low_in(7)
                dve.wait_ge(rope_ready, 1)
                first_half, second_half = qk[:, :, :, 0:half], qk[:, :, :, half:ROPE]
                cos = cosine[:].unsqueeze(2).to_broadcast([P, TILES, QK, half])
                sin = sine[:].unsqueeze(2).to_broadcast([P, TILES, QK, half])
                for n, (part, turn) in enumerate(((first_half, cos), (second_half, sin), (second_half, cos), (first_half, sin))):
                    v.tensor_tensor(rope_t[:, n], part, turn, ALU.mult).then_inc(dve_steps, 1)
                    dve.wait_ge(dve_steps, steps.next())
                v.tensor_tensor(first_half, rope_t[:, 0], rope_t[:, 1], ALU.subtract).then_inc(dve_steps, 1)
                dve.wait_ge(dve_steps, steps.next())
                v.tensor_tensor(second_half, rope_t[:, 2], rope_t[:, 3], ALU.add).then_inc(qk_done, 1)
                softmax_rows(False)
                for u in range(2):
                    low(u, in_hi, KC * BLK)
                for t in range(TILES):
                    dve.wait_ge(rows_done, 1)
                    dve.sem_inc(rows_done, -1)
                    if t == TILES - 1:
                        dve.sem_inc(slot_free, 1)
                    add_gated(t, 2)
                normalise(mod[:, 4, :], mod[:, 3, :])
                split_hT(hT_lo1)
                for u in range(2, 8):
                    low(u, in_hi, KC * BLK)
                dve.sem_inc(dve_steps, -steps.reset())

                def route(n, p):
                    v.tensor_copy(half_s[:].rearrange("p h k -> p (h k)"), key_s[:, bass.ds(n, 1), :, :].rearrange("p n h k -> p (n h k)")).then_inc(dve_steps, 1)
                    dve.wait_ge(dve_steps, steps.next())
                    for s in range(2):
                        v.max(best[:, s, 0:8], half_s[:, s, :]).then_inc(dve_steps, 1)
                        dve.wait_ge(dve_steps, steps.next())
                        v.max_index(best_i[:, s, 0:8], best[:, s, 0:8], half_s[:, s, :]).then_inc(dve_steps, 1)
                        dve.wait_ge(dve_steps, steps.next())
                        v.match_replace(half_r[:, s, :], best[:, s, 0:8], half_s[:, s, :], LEAST).then_inc(dve_steps, 1)
                        dve.wait_ge(dve_steps, steps.next())
                        v.max(best[:, s, 8:16], half_r[:, s, :]).then_inc(dve_steps, 1)
                        dve.wait_ge(dve_steps, steps.next())
                        v.max_index(best_i[:, s, 8:16], best[:, s, 8:16], half_r[:, s, :]).then_inc(dve_steps, 1)
                        dve.wait_ge(dve_steps, steps.next())
                    v.tensor_tensor(cand[:].rearrange("p (i j) -> p i j", i=TOPK), best[:, 0, :].unsqueeze(2).to_broadcast([P, TOPK, TOPK]),
                                    best[:, 1, :].unsqueeze(1).to_broadcast([P, TOPK, TOPK]), ALU.add).then_inc(dve_steps, 1)
                    dve.wait_ge(dve_steps, steps.next())
                    v.max(top[:, p, 0:8], cand[:]).then_inc(dve_steps, 1)
                    dve.wait_ge(dve_steps, steps.next())
                    v.max_index(place[:, 0:8], top[:, p, 0:8], cand[:]).then_inc(dve_steps, 1)
                    dve.wait_ge(dve_steps, steps.next())
                    v.match_replace(cand_r[:], top[:, p, 0:8], cand[:], LEAST).then_inc(dve_steps, 1)
                    dve.wait_ge(dve_steps, steps.next())
                    v.max(top[:, p, 8:16], cand_r[:]).then_inc(dve_steps, 1)
                    dve.wait_ge(dve_steps, steps.next())
                    v.max_index(place[:, 8:16], top[:, p, 8:16], cand_r[:]).then_inc(dve_steps, 1)
                    dve.wait_ge(dve_steps, steps.next())
                    v.tensor_scalar(neg_top[:, p, :], top[:, p, 0:1], -1.0, None, ALU.mult).then_inc(top_ready, 1)
                    v.tensor_scalar(place2[:, 0, :], place[:], 4, None, ALU.logical_shift_right).then_inc(dve_steps, 1)
                    dve.wait_ge(dve_steps, steps.next())
                    v.tensor_scalar(place2[:, 1, :], place[:], TOPK - 1, None, ALU.bitwise_and).then_inc(dve_steps, 1)
                    dve.wait_ge(dve_steps, steps.next())
                    v.tensor_copy(place_f[:], place2[:]).then_inc(dve_steps, 1)
                    dve.wait_ge(dve_steps, steps.next())
                    v.tensor_copy(best_f[:], best_i[:]).then_inc(dve_steps, 1)
                    dve.wait_ge(dve_steps, steps.next())
                    for s in range(2):
                        v.tensor_tensor(onehot[:], place_f[:, s, :].unsqueeze(2).to_broadcast([P, TOPK, TOPK]),
                                        iota16[:].unsqueeze(1).to_broadcast([P, TOPK, TOPK]), ALU.is_equal).then_inc(dve_steps, 1)
                        dve.wait_ge(dve_steps, steps.next())
                        v.tensor_tensor(onehot[:], onehot[:], best_f[:, s, :].unsqueeze(1).to_broadcast([P, TOPK, TOPK]), ALU.mult).then_inc(dve_steps, 1)
                        dve.wait_ge(dve_steps, steps.next())
                        v.tensor_reduce(chosen[:, s, :], onehot[:], AX_X, ALU.add).then_inc(dve_steps, 1)
                        dve.wait_ge(dve_steps, steps.next())
                    v.scalar_tensor_tensor(expert_f[:], chosen[:, 0, :], float(KEYS), chosen[:, 1, :], ALU.mult, ALU.add).then_inc(dve_steps, 1)
                    dve.wait_ge(dve_steps, steps.next())
                    v.tensor_scalar(expert[:, p, :], expert_f[:], expert_base[:], None, ALU.add).then_inc(expert_ready, 1)

                def unit(t, n, p, follow):
                    for g in range(2):
                        for j in range(GRP):
                            dve.wait_ge(u_in[j], (l * (2 * UNITS) + (n * 2 + (g + 1))) * 16)
                            v.tensor_tensor_reduce(out=junk, in0=u_ring[:, j, :], in1=h[:, t, :], scale=1.0, scalar=0.0,
                                                   op0=ALU.mult, op1=ALU.add, accum_out=dots[:, g, j:j + 1]).then_inc(dve_steps, 1)
                            dve.wait_ge(dve_steps, steps.next())
                            dve.sem_inc(u_free, 1)
                        dve.sem_inc(dots_ready, 1)
                        if g == 0:
                            dve.wait_ge(gate_ready, 1)
                            dve.sem_inc(gate_ready, -1)
                            v.reciprocal(gate_inv[:], gate_sum[:, p, :]).then_inc(dve_steps, 1)
                            dve.wait_ge(dve_steps, steps.next())
                            v.tensor_scalar(gate[:], gate_e[:, p, :], gate_inv[:], None, ALU.mult).then_inc(dve_steps, 1)
                            dve.wait_ge(dve_steps, steps.next())
                        dve.wait_ge(acts_ready, 1)
                        dve.sem_inc(acts_ready, -1)
                        if g == 0:
                            dve.wait_ge(diag_free, 1)
                            dve.sem_inc(diag_free, -1)
                        for j in range(GRP):
                            k = g * GRP + j
                            v.tensor_scalar(diag[:, k, :], ident[:], acts[:, g, j:j + 1], gate[:, k:k + 1], ALU.mult, ALU.mult).then_inc(diag_ready, 1)
                        if g == 0:
                            dve.wait_ge(diag_free, 1)
                            dve.sem_inc(diag_free, -1)
                            if follow:
                                route(n + 1, 1 - p)
                    dve.sem_inc(dve_steps, -steps.reset())

                dve.wait_ge(key_s_ready, 1)
                dve.sem_inc(key_s_ready, -1)
                route(0, 0)
                dve.wait_ge(key_s_ready, 7)
                dve.sem_inc(key_s_ready, -7)
                dve.sem_inc(params_free, 1)
                dve.sem_inc(dve_steps, -steps.reset())
                with dve.Fori(0, EXPERT_HEADS // 2) as i:
                    for p in range(2):
                        unit(0, i * 2 + p, p, True)
                with dve.Fori(0, EXPERT_HEADS // 2 - 1) as i:
                    for p in range(2):
                        unit(1, i * 2 + (EXPERT_HEADS + p), p, True)
                dve.wait_ge(y_ready, 1)
                dve.sem_inc(y_ready, -1)
                add_gated(0, 5)
                dve.sem_inc(dve_steps, -steps.reset())
                unit(1, UNITS - 2, 0, True)
                unit(1, UNITS - 1, 1, False)
                dve.wait_ge(y_ready, 1)
                dve.sem_inc(y_ready, -1)
                dve.sem_inc(slot_free, 4)
                add_gated(1, 5)
                fan(dve, acc_read)
                dve.sem_inc(dve_steps, -steps.reset())

            def low_ff(n):
                low(n, w_hi, FF_SLOT)

            def low_block(n):
                low(n, w_hi, KC * BLK)

            def feed_forward(f, ahead, give=x_ready):
                n0 = first[f"ff{f}"]

                def gated(b):
                    dve.wait_ge(silu_ready, 1)
                    dve.sem_inc(silu_ready, -1)
                    v.tensor_tensor(silu_g[:, b, :], silu_g[:, b, :], ps[:, WORK + b, SEQ:2 * SEQ], ALU.mult).then_inc(dve_steps, 1)
                    dve.wait_ge(dve_steps, steps.next())
                    v.tensor_copy(ff_hi[:, b, :], silu_g[:, b, :]).then_inc(dve_steps, 1)
                    dve.wait_ge(dve_steps, steps.next())
                    v.tensor_tensor(ff_lo[:, b, :], silu_g[:, b, :], ff_hi[:, b, :].bitcast(F32), ALU.subtract).then_inc(ff_ready, 1)

                pre_norm()
                if f < 2:
                    low_ff(n0)
                split_hT(hT_lo)
                if f < 2:
                    low_ff(n0 + 1)
                with dve.Fori(0, (FF_CHUNKS - 2) // SLOTS) as i:
                    for u in range(SLOTS):
                        gated(u % 2)
                        low_ff(n0 + 2 + u)
                    dve.sem_inc(dve_steps, -steps.reset())
                for u in range(2):
                    gated(u)
                    if ahead is not None:
                        ahead(n0 + FF_CHUNKS + u)
                dve.sem_inc(dve_steps, -steps.reset())
                add_normed(0.5, give)

            def log1p_series(t, total):
                v.tensor_scalar(t[2], t[1], 2.0, None, ALU.add).then_inc(dve_steps, 1)
                dve.wait_ge(dve_steps, steps.next())
                v.reciprocal(t[2], t[2]).then_inc(dve_steps, 1)
                dve.wait_ge(dve_steps, steps.next())
                v.tensor_tensor(t[3], t[1], t[2], ALU.mult).then_inc(dve_steps, 1)
                dve.wait_ge(dve_steps, steps.next())
                v.tensor_tensor(t[4], t[3], t[3], ALU.mult).then_inc(dve_steps, 1)
                dve.wait_ge(dve_steps, steps.next())
                v.tensor_scalar(t[5], t[4], 1.0 / (2 * total + 1), None, ALU.mult).then_inc(dve_steps, 1)
                dve.wait_ge(dve_steps, steps.next())
                for n in range(total - 1, 0, -1):
                    v.scalar_tensor_tensor(t[5], t[5], 1.0 / (2 * n + 1), t[4], ALU.add, ALU.mult).then_inc(dve_steps, 1)
                    dve.wait_ge(dve_steps, steps.next())
                v.scalar_tensor_tensor(t[5], t[5], 1.0, t[3], ALU.add, ALU.mult).then_inc(dve_steps, 1)
                dve.wait_ge(dve_steps, steps.next())
                v.tensor_scalar(t[5], t[5], 2.0, None, ALU.mult).then_inc(dve_steps, 1)
                dve.wait_ge(dve_steps, steps.next())

            feed_forward(0, None)
            fan(dve, ff0_over)
            pre_norm()
            dve.wait_ge(rnn_cols_ready, 1)
            dve.sem_inc(rnn_cols_ready, -1)
            lam = rnn_cols[:, 7, :]
            v.scalar_tensor_tensor(decay[:, 0, :], lam, -1.0, lam, ALU.mult, ALU.max).then_inc(lam_abs, 1)
            dve.wait_ge(lam_exp, 1)
            dve.sem_inc(lam_exp, -1)
            log1p_series([decay[:, k, :] for k in range(6)], 8)
            v.tensor_scalar(decay[:, 0, :], lam, -1.0, 0.0, ALU.mult, ALU.max).then_inc(dve_steps, 1)
            dve.wait_ge(dve_steps, steps.next())
            v.tensor_tensor(decay[:, 0, :], decay[:, 0, :], decay[:, 5, :], ALU.add).then_inc(dve_steps, 1)
            dve.wait_ge(dve_steps, steps.next())
            v.tensor_scalar(decay_neg[:], decay[:, 0, :], -8.0, None, ALU.mult).then_inc(dve_steps, 1)
            dve.wait_ge(dve_steps, steps.next())
            v.tensor_scalar(decay_pos[:], decay[:, 0, :], 8.0, None, ALU.mult).then_inc(decay_ready, 1)
            dve.wait_ge(rnn_zeroed, 1)
            dve.sem_inc(rnn_zeroed, -1)
            for s in range(SUPER):
                dve.wait_ge(rec_in_ready, 1)
                dve.sem_inc(rec_in_ready, -1)
                chunks = range(3 * s, 3 * s + 3)
                for j in chunks:
                    ins = v.tensor_scalar(rec[:, j, :], rec_in[:, j, CONV_K - 1:], rnn_cols[:, 3, j:j + 1], rnn_cols[:, 4, j:j + 1], ALU.mult, ALU.add)
                for k in range(CONV_K - 1):
                    ins.then_inc(dve_steps, 1)
                    dve.wait_ge(dve_steps, steps.next())
                    for j in chunks:
                        ins = v.scalar_tensor_tensor(rec[:, j, :], rec_in[:, j, k:k + SEQ], rnn_cols[:, k, j:j + 1], rec[:, j, :], ALU.mult, ALU.add)
                ins.then_inc(rec_ready, 1)
            for s in range(SUPER):
                c = slice(3 * s, 3 * s + 3)
                dve.wait_ge(gates_ready, 1)
                dve.sem_inc(gates_ready, -1)
                v.tensor_tensor(gate_i[:, c], gate_i[:, c], rec[:, c], ALU.mult).then_inc(dve_steps, 1)
                dve.wait_ge(dve_steps, steps.next())
                v.tensor_tensor(rec[:, c], decay_a[:, c], decay_a[:, c], ALU.mult).then_inc(dve_steps, 1)
                dve.wait_ge(dve_steps, steps.next())
                v.scalar_tensor_tensor(gate_r[:, c], rec[:, c], 1.0, gate_r[:, c], ALU.add, ALU.mult).then_inc(root_in, 1)
            for s in range(SUPER):
                c = slice(3 * s, 3 * s + 3)
                dve.wait_ge(root_ready, 1)
                dve.sem_inc(root_ready, -1)
                v.tensor_tensor(gate_i[:, c], gate_i[:, c], gate_r[:, c], ALU.mult).then_inc(dve_steps, 1)
                dve.wait_ge(dve_steps, steps.next())
                for j in range(3 * s, 3 * s + 3):
                    ins = v.tensor_tensor_scan(rec[:, j, :], decay_a[:, j, :], gate_i[:, j, :], 0.0, ALU.mult, ALU.add)
                ins.then_inc(dve_steps, 1)
                dve.wait_ge(dve_steps, steps.next())
                ins = v.tensor_tensor(gate_g[:, c], gate_g[:, c], rec[:, c], ALU.mult)
            ins.then_inc(rnn_out_ready, 1)
            add_normed(1.0, x_ready)
            fan(dve, rnn_over)
            feed_forward(1, low_block)
            pre_norm()
            split_hT(hT_lo)
            dve.wait_ge(f_ready, 1)
            dve.sem_inc(f_ready, -1)
            v.scalar_tensor_tensor(logs[:, 0, :], f_tok[:], -1.0, f_tok[:], ALU.mult, ALU.max).then_inc(f_abs, 1)
            dve.wait_ge(f_exp, 1)
            dve.sem_inc(f_exp, -1)
            for u in range(2, 4):
                low_block(first["kv"] + u)
            log1p_series([logs[:, k, :] for k in range(6)], 8)
            v.scalar_tensor_tensor(log_f[:], f_tok[:], 0.0, logs[:, 5, :], ALU.min, ALU.subtract).then_inc(log_f_ready, 1)
            for u in range(4, 8):
                low_block(first["kv"] + u)
            for u in range(2):
                low_ff(first["ff2"] + u)
            dve.sem_inc(x_ready, TILES)
            dve.sem_inc(dve_steps, -steps.reset())
            feed_forward(2, low_block)
            fan(dve, ff2_over)
            pre_norm()
            split_hT(hT_lo)
            for u in range(2, 4):
                low_block(first["q"] + u)
            for u in range(2):
                low_block(first["o"] + u)
            softmax_rows(True)
            dve.sem_inc(h_ready, TILES)
            split_hT(hT_lo)
            for u in range(2, 4):
                low_block(first["o"] + u)
            for u in range(2):
                low_ff(first["ff3"] + u)
            add_normed(1.0, x_ready)
            feed_forward(3, None, x_final)


INPUTS = [
    "x", "c", "positions", "norm1_g", "norm2_g", "w_ada", "b_ada", "w_in", "q_norm_g", "k_norm_g", "attn_sink",
    "conv_w", "pool_w", "pool_scale", "w_out", "peer_wq", "peer_keys", "peer_u", "peer_v", "ffn1_pre_g_2",
    "ffn1_w_gate_2", "ffn1_w_up_2", "ffn1_w_down_2", "ffn1_post_g_2", "mix_pre_g_2", "mix_post_g_2",
    "ffn2_pre_g_2", "ffn2_w_gate_2", "ffn2_w_up_2", "ffn2_w_down_2", "ffn2_post_g_2", "rg_w_in_2",
    "rg_conv_w_2", "rg_conv_b_2", "rg_w_a_2", "rg_b_a_2", "rg_w_x_2", "rg_b_x_2", "rg_lambda_2", "rg_w_out_2",
    "kv_norm_g_2", "w_kv_2", "w_fgate_2", "b_fgate_2", "attn_w_q_2", "attn_w_o_2",
]


def kernel(**inputs):
    import concourse.bacc as bacc
    from concourse.bass_utils import run_bass_kernel_spmd

    nc = bacc.Bacc("TRN2", target_bir_lowering=False, num_devices=1)
    arrays, views = {}, {}
    for name in INPUTS:
        a = np.ascontiguousarray(inputs[name])
        if name in ("peer_u", "peer_v"):
            a = a.reshape(-1, a.shape[-1])
        arrays["in_" + name] = a
        views[name] = nc.dram_tensor("in_" + name, a.shape, mybir.dt.from_np(a.dtype), kind="ExternalInput").ap()
    out = nc.dram_tensor("out", (1, SEQ, D), F32, kind="ExternalOutput").ap()
    program(nc, views, out)
    return run_bass_kernel_spmd(nc, [arrays], core_ids=[0]).results[0]["out"]
```

```python
from contextlib import ExitStack

import numpy as np

import concourse.bass as bass
from concourse import mybir

ALU = mybir.AluOpType
ACT = mybir.ActivationFunctionType
F32 = mybir.dt.float32
F32R = mybir.dt.float32r
I32 = mybir.dt.int32
U32 = mybir.dt.uint32
AX_X = mybir.AxisListType.X

P = 128
SEQ = 256
D = 1024
KC = D // P
TILES = SEQ // P
DEPTH = 2
EPS = 1e-6
MASKED = -1e30
LEAST = -3.0e38

HEAD = 64
Q_HEADS = 8
KV_HEADS = 2
GROUP = Q_HEADS // KV_HEADS
ROPE = HEAD // 4
ROPE_THETA = 500000.0
WINDOWS = (2, 4, 8, 16)
PAD = WINDOWS[-1]
PADDED = SEQ + 2 * PAD
ATTN_W = Q_HEADS * HEAD
KV_W = KV_HEADS * HEAD
EXPERT_HEADS = 8
KEYS = 128
EXPERTS = KEYS * KEYS
TOPK = 16
UNITS = TILES * EXPERT_HEADS
U_SLOTS = 8
V_SLOTS = 16
GRP = 8

D_FF = 2816
FF_CHUNKS = D_FF // P
D_RNN = 1344
RC = 112
R_CHUNKS = D_RNN // RC
LRU = 84
SUPER = 4
CONV_K = 4
HEADS2 = 16

SLOTS = 4
SLOT = 4096
N = 512


def program(nc, A, out):
    with ExitStack() as ctx:
        def sb(name, shape, dt=F32):
            return ctx.enter_context(nc.sbuf_tensor(name, shape, dt))

        def sem(name):
            return ctx.enter_context(nc.semaphore(name))

        ps = ctx.enter_context(nc.psum_tensor("ps", [P, 8, N], F32))
        WORK = 4

        x = sb("x", [P, TILES, D])
        h_ext = sb("h_ext", [P, TILES * D + D])
        h = h_ext[:, 0:TILES * D].rearrange("p (t d) -> p t d", t=TILES)
        junk = h_ext[:, TILES * D:]
        gain_pre = sb("gain_pre", [P, D])
        gain_post = sb("gain_post", [P, D])
        ident = sb("ident", [P, P])
        zeros = sb("zeros", [P, P])
        ones = sb("ones", [P, P])
        upto = sb("upto", [P, P])
        window = sb("window_mask", [P, TILES, SEQ])
        eps = sb("eps", [P, 1])
        iota16 = sb("iota16", [P, TOPK])
        window_count = sb("window_count", [P, 2, SEQ])
        window_share = sb("window_share", [P, 2, SEQ])
        c_rows = sb("c_rows", [KC, P])
        c_act = sb("c_act", [P, KC])
        c_hi = sb("c_hi", [P, KC], F32R)
        c_lo = sb("c_lo", [P, KC], F32R)
        pos_i = sb("pos_i", [TILES, P], I32)
        pos_f = sb("pos_f", [TILES, P])
        pos = sb("pos", [P, TILES])
        inv_freq = sb("inv_freq", [P, ROPE // 2])
        angle = sb("angle", [P, 4, TILES, ROPE // 2])
        cosine = sb("cosine", [P, TILES, ROPE // 2])
        sine = sb("sine", [P, TILES, ROPE // 2])
        mix_rows = sb("mix_rows", [8, P])
        mix_cols = sb("mix_cols", [P, 8])
        pool_w = sb("pool_w", [P, 2, P])
        keys_raw = sb("keys_raw", [P, 2, KEYS])
        keysT = sb("keysT", [P, 2, KEYS])
        sink = sb("sink", [P, Q_HEADS])
        ada_bias = sb("ada_bias", [8, 2, 384])
        expert_base = sb("expert_base", [P, 1])
        mean_sq = sb("mean_sq", [P, TILES])
        rms = sb("rms", [P, TILES])
        table_use = sb("table_use", [P, 1])
        rstd = sb("rstd", [P, TILES])
        head_sq = sb("head_sq", [P, TILES, Q_HEADS + KV_HEADS])
        head_rms = sb("head_rms", [P, TILES, Q_HEADS + KV_HEADS])
        row_max = sb("row_max", [P, 2, GROUP])
        neg_max = sb("neg_max", [P, 2, GROUP])
        sink_d = sb("sink_d", [P, 2, GROUP])
        sink_e = sb("sink_e", [P, 4, GROUP])
        row_sum = sb("row_sum", [P, 4, GROUP])
        row_inv = sb("row_inv", [P, 2, GROUP])
        best = sb("best", [P, 2, TOPK])
        best_i = sb("best_i", [P, 2, TOPK], U32)
        best_f = sb("best_f", [P, 2, TOPK])
        place = sb("place", [P, TOPK], U32)
        place2 = sb("place2", [P, 2, TOPK], U32)
        place_f = sb("place_f", [P, 2, TOPK])
        chosen = sb("chosen", [P, 2, TOPK])
        expert_f = sb("expert_f", [P, TOPK])
        expert = sb("expert", [P, 2, TOPK], U32)
        top = sb("top", [P, 2, TOPK])
        neg_top = sb("neg_top", [P, 2, 1])
        gate_e = sb("gate_e", [P, 2, TOPK])
        gate_sum = sb("gate_sum", [P, 2, 1])
        gate_inv = sb("gate_inv", [P, 1])
        gate = sb("gate", [P, TOPK])
        dots = sb("dots", [P, 2, GRP])
        acts = sb("acts", [P, 2, GRP])
        rnn_rows = sb("rnn_rows", [8 * R_CHUNKS, RC])
        rnn_cols = sb("rnn_cols", [RC, 8, R_CHUNKS])
        decay = sb("decay", [RC, 6, R_CHUNKS])
        decay_neg = sb("decay_neg", [RC, R_CHUNKS])
        decay_pos = sb("decay_pos", [RC, R_CHUNKS])
        wf = sb("wf", [P, KC, HEADS2])
        bf = sb("bf", [1, HEADS2])
        f_tok = sb("f_tok", [P, TILES * HEADS2])
        logs = sb("logs", [P, 6, TILES * HEADS2])
        log_f = sb("log_f", [P, TILES * HEADS2])
        c_tok = sb("c_tok", [P, TILES * HEADS2])

        ARENA = 21824
        AT_HT = SLOTS * SLOT
        AT_ARENA = AT_HT + KC * SEQ

        def overlay(name, at, shape, dt=F32):
            with ExitStack() as scope:
                if at:
                    scope.enter_context(nc.sbuf_tensor("below_" + name, [P, at], F32))
                return scope.enter_context(nc.sbuf_tensor(name, shape, dt))

        ring = overlay("weight_ring", 0, [P, SLOTS, SLOT])
        ring_lo = overlay("ring_lo", 0, [P, SLOTS, SLOT], F32R)
        hT = overlay("hT", AT_HT, [P, KC, SEQ])
        hT_hi = overlay("hT_hi", AT_HT, [P, KC, SEQ], F32R)
        arena = overlay("arena", AT_ARENA, [P, ARENA])

        class Carve:

            def __init__(self, start=0):
                self.at = start

            def __call__(self, size, pattern=None, **kw):
                part = arena[:, self.at:self.at + size]
                self.at += size
                assert self.at <= ARENA, self.at
                return part.rearrange(pattern, **kw) if pattern else part

        c1 = Carve()
        mod = c1(6 * D, "p (s d) -> p s d", s=6)
        qTz = c1(Q_HEADS * SEQ, "p (h t) -> p h t", h=Q_HEADS)
        shared = c1.at
        QK = Q_HEADS + KV_HEADS
        qk_gain = c1(QK * HEAD, "p (h d) -> p h d", h=QK)
        qk = c1(TILES * QK * HEAD, "p (t h d) -> p t h d", t=TILES, h=QK)
        v_tok = c1(TILES * KV_W, "p (t d) -> p t d", t=TILES)
        zc = c1(8 * SEQ, "p (c t) -> p c t", c=8)
        kT = c1(SEQ)
        pT = c1(2 * GROUP * P, "p (i t) -> p i t", t=P)
        attn = c1(TILES * ATTN_W, "p (t d) -> p t d", t=TILES)
        conv_u = c1(2 * SEQ, "p (c t) -> p c t", c=2)
        conv_o = c1(2 * SEQ, "p (c t) -> p c t", c=2)
        conv_t = c1(2 * SEQ, "p (c t) -> p c t", c=2)
        pool_in = c1(2 * PADDED, "p (c t) -> p c t", c=2)
        pool_s = [c1(2 * PADDED, "p (c t) -> p c t", c=2) for _ in range(2)]
        pooled = c1(2 * SEQ, "p (c t) -> p c t", c=2)
        mixT = hT
        ROPE_N = 4 * TILES * QK * ROPE // 2
        qk_sq = h_ext[:, ROPE_N:ROPE_N + TILES * QK * HEAD].rearrange("p (t h d) -> p t h d", t=TILES, h=QK)
        rope_t = h_ext[:, 0:4 * TILES * QK * ROPE // 2].rearrange("p (n t h d) -> p n t h d", n=4, t=TILES, h=QK)
        scores = h_ext[:, 0:2 * GROUP * SEQ].rearrange("p (b i t) -> p b i t", b=2, i=GROUP)
        c2 = Carve(shared)
        qpT = c2(4 * SEQ, "p (b c t) -> p b c t", b=2, c=2)
        half_s = c2(2 * KEYS, "p (h k) -> p h k", h=2)
        half_r = c2(2 * KEYS, "p (h k) -> p h k", h=2)
        cand = c2(TOPK * TOPK)
        cand_r = c2(TOPK * TOPK)
        onehot = c2(TOPK * TOPK, "p (k j) -> p k j", k=TOPK)
        AT_QUERY_LO = c2.at
        diag = c2(2 * GRP * P, "p (s t) -> p s t", t=P)
        u_ring = c2(U_SLOTS * D, "p (s d) -> p s d", s=U_SLOTS)
        key_s = arena[:, 0:UNITS * 2 * KEYS].rearrange("p (n h k) -> p n h k", n=UNITS, h=2)
        v_ring = ring[:, :, :].rearrange("p s (b d) -> p (s b) d", d=D)
        ADA_N = 384
        ADA_TURNS = 6 * D // (SLOTS * ADA_N)
        BLK = 256
        ROWS = KC * BLK // D
        ada_hi = [overlay(f"ada_hi{u}", AT_ARENA + ARENA - (SLOTS - (u + 1) % SLOTS) * KC * ADA_N, [P, KC * ADA_N], F32R) for u in range(SLOTS)]
        IN_HI = ARENA - SLOTS * KC * BLK
        in_hi = [overlay(f"in_hi{u}", AT_ARENA + IN_HI + u * KC * BLK, [P, KC * BLK], F32R) for u in range(SLOTS)]
        U_AT = c2.at - U_SLOTS * D
        u_opened_by = [EXPERT_HEADS - SLOTS + max(0, (U_AT + (k + 1) * D - 1 - IN_HI) // (KC * BLK)) for k in range(U_SLOTS)]
        hT_lo1 = overlay("hT_lo1", AT_ARENA, [P, KC, SEQ], F32R)
        query_lo = overlay("query_lo", AT_ARENA + AT_QUERY_LO, [P, KC, SEQ], F32R)
        STAYS = 2 * TILES * D + 2 * SEQ
        FF_SLOT = 2 * KC * P + D
        AT_FF = STAYS + KC * SEQ
        AT_W = AT_FF + 6 * SEQ
        hT_lo = overlay("hT_lo", AT_ARENA + STAYS, [P, KC, SEQ], F32R)
        silu_g = arena[:, AT_FF:AT_FF + 2 * SEQ].rearrange("p (b t) -> p b t", b=2)
        ff_hi = overlay("ff_hi", AT_ARENA + AT_FF + 2 * SEQ, [P, 2, SEQ], F32R)
        ff_lo = overlay("ff_lo", AT_ARENA + AT_FF + 4 * SEQ, [P, 2, SEQ], F32R)
        w_hi = overlay("w_hi", AT_ARENA + AT_W, [P, SLOTS, FF_SLOT], F32R)
        w_hi_slots = [w_hi[:, u, :] for u in range(SLOTS)]
        assert AT_W + SLOTS * FF_SLOT <= ARENA
        c3 = Carve()
        gate_g = c3(R_CHUNKS * SEQ, "p (c t) -> p c t", c=R_CHUNKS)[0:RC]
        rec_width = SEQ + CONV_K - 1
        rec_at = c3.at
        rec_in = c3(R_CHUNKS * rec_width, "p (c t) -> p c t", c=R_CHUNKS)[0:RC]
        gate_i = arena[0:RC, rec_at:rec_at + R_CHUNKS * SEQ].rearrange("p (c t) -> p c t", c=R_CHUNKS)
        rec = c3(R_CHUNKS * SEQ, "p (c t) -> p c t", c=R_CHUNKS)[0:RC]
        gate_r = c3(R_CHUNKS * SEQ, "p (c t) -> p c t", c=R_CHUNKS)[0:RC]
        wide = 3 * RC
        w_gates = [c3(SUPER * 3 * wide, "p (s i d) -> p s i d", s=SUPER, i=3)[0:RC] for _ in range(2)]
        RNN_IN = KC * 2 * RC
        rnn_hi = ring_lo[:, :, RNN_IN:2 * RNN_IN]
        hT_lo_r = ring_lo[:, :, 2 * RNN_IN:2 * RNN_IN + KC * SEQ // SLOTS].rearrange("p s (k t) -> p s k t", t=SEQ)
        assert 2 * RNN_IN + KC * SEQ // SLOTS <= SLOT and 2 * RNN_IN >= FF_SLOT
        out_hi = overlay("out_hi", AT_ARENA + rec_at + R_CHUNKS * rec_width + R_CHUNKS * SEQ, [P, R_CHUNKS, SEQ], F32R)
        out_lo = overlay("out_lo", AT_ARENA + rec_at, [P, R_CHUNKS, SEQ], F32R)
        decay_a = h_ext[0:RC, :].rearrange("p (c t) -> p c t", c=R_CHUNKS)
        c4 = Carve()
        kT2 = c4(8 * SEQ, "p (c t) -> p c t", c=8)
        v2 = c4(TILES * D, "p (t d) -> p t d", t=TILES)
        c_pad = c4(TILES * P, "p (t j) -> p t j", t=TILES)
        neg_cT = c4(SEQ)
        qTz2 = arena[:, AT_W:AT_W + SLOTS * FF_SLOT].rearrange("p (s m) -> p s m", s=SLOTS)[:, :, KC * BLK:KC * BLK + GROUP * SEQ] \
            .rearrange("p s (h t) -> p s h t", h=GROUP)
        scores2 = hT[:].rearrange("p c t -> p (c t)").rearrange("p (b i t) -> p b i t", b=2, i=GROUP)
        pT2 = junk.rearrange("p (i t) -> p i t", t=P)

        consts, tables = sem("consts"), sem("tables")
        const_steps = sem("const_steps")
        x_loaded = sem("x_loaded")
        share_ready = sem("share_ready")
        c_loaded = sem("c_loaded")
        pos_loaded = sem("pos_loaded")
        pos_float = sem("pos_float")
        pos_turned = sem("pos_turned")
        angle_ready = sem("angle_ready")
        rope_ready = sem("rope_ready")
        c_turned = sem("c_turned")
        c_act_ready = sem("c_act_ready")
        c_split = sem("c_split")
        slot_in = [sem(f"slot_in{i}") for i in range(SLOTS)]
        plain_in = [sem(f"plain_in{i}") for i in range(SLOTS)]
        slot_free = [sem(f"slot_free{i}") for i in range(SLOTS)]
        pre_in, pre_free = sem("pre_in"), sem("pre_free")
        post_in, post_free = sem("post_in"), sem("post_free")
        pe_params, dve_params, params_free = sem("pe_params"), sem("dve_params"), sem("params_free")
        bias_in = sem("bias_in")
        params_turned = sem("params_turned")
        x_ready = sem("x_ready")
        rms_ready = sem("rms_ready")
        h_ready = sem("h_ready")
        hT_turned = sem("hT_turned")
        hT_ready = sem("hT_ready")
        job_done, job_taken = sem("job_done"), sem("job_taken")
        mod_ready = sem("mod_ready")
        qk_ready = sem("qk_ready")
        head_sq_ready, head_rms_ready = sem("head_sq_ready"), sem("head_rms_ready")
        zc_ready = sem("zc_ready")
        qk_done = sem("qk_done")
        qk_turned = sem("qk_turned")
        qkT_ready = sem("qkT_ready")
        scores_done = sem("scores_done")
        scores_ready = sem("scores_ready")
        probs_ready = sem("probs_ready")
        sums_ready = sem("sums_ready")
        p_turned, pT_ready = sem("p_turned"), sem("pT_ready")
        pv_done, attn_done = sem("pv_done"), sem("attn_done")
        pooled_ready, pool_done = sem("pooled_ready"), sem("pool_done")
        attn_turned, mixT_ready = sem("attn_turned"), sem("mixT_ready")
        rows_done = sem("rows_done")
        rms2_ready = sem("rms2_ready")
        key_s_ready = sem("key_s_ready")
        expert_ready = sem("expert_ready")
        top_ready, gate_ready = sem("top_ready"), sem("gate_ready")
        u_in = [sem(f"u_in{i}") for i in range(U_SLOTS)]
        u_free = sem("u_free")
        v_in = [sem(f"v_in{i}") for i in range(V_SLOTS)]
        v_free = sem("v_free")
        queries_ready, experts_open = sem("queries_ready"), sem("experts_open")
        dots_ready, acts_ready = sem("dots_ready"), sem("acts_ready")
        diag_ready, diag_free = sem("diag_ready"), sem("diag_free")
        y_ready, acc_read = sem("y_ready"), sem("acc_read")
        ff0_over, ff2_over = sem("ff0_over"), sem("ff2_over")
        hT_split = sem("hT_split")
        w_hi_ready, w_split = sem("w_hi_ready"), sem("w_split")
        gu_done, silu_ready, ff_ready = sem("gu_done"), sem("silu_ready"), sem("ff_ready")
        rnn_rows_in, rnn_turned, rnn_cols_ready = sem("rnn_rows_in"), sem("rnn_turned"), sem("rnn_cols_ready")
        rnn_zeroed, rnn_w_in = sem("rnn_zeroed"), sem("rnn_w_in")
        lam_abs, lam_exp, decay_ready = sem("lam_abs"), sem("lam_exp"), sem("decay_ready")
        rec_in_ready, rec_ready = sem("rec_in_ready"), sem("rec_ready")
        gates_ready, root_in, root_ready = sem("gates_ready"), sem("root_in"), sem("root_ready")
        gelu_ready, rnn_out_ready = sem("gelu_ready"), sem("rnn_out_ready")
        rnn_over = sem("rnn_over")
        wf_in = sem("wf_in")
        c_pad_zeroed, heads_zeroed = sem("c_pad_zeroed"), sem("heads_zeroed")
        f_ready, f_abs, f_exp, log_f_ready = sem("f_ready"), sem("f_abs"), sem("f_exp"), sem("log_f_ready")
        c_summed, c_ready, c_back, neg_cT_ready = sem("c_summed"), sem("c_ready"), sem("c_back"), sem("neg_cT_ready")
        x_final = sem("x_final")
        out_stored = sem("out_stored")
        act_steps, dve_steps, pool_steps = sem("act_steps"), sem("dve_steps"), sem("pool_steps")

        def fan(eng, s):
            eng.drain().then_inc(s, 1)

        class Count:

            def __init__(self):
                self.value = 0

            def next(self):
                self.value += 1
                return self.value

            def reset(self):
                value, self.value = self.value, 0
                assert value
                return value

        FF_NAMES = [("ffn1", 0), ("ffn2", 0), ("ffn1", 1), ("ffn2", 1)]
        first = {}
        at = 0
        for name, count in (("ff0", FF_CHUNKS), ("rnn_in", R_CHUNKS), ("rnn_out", R_CHUNKS), ("ff1", FF_CHUNKS), ("kv", 8),
                            ("ff2", FF_CHUNKS), ("q", 4), ("o", 4), ("ff3", FF_CHUNKS)):
            first[name] = at
            at += count
        PEEL = FF_CHUNKS % SLOTS
        TURNS = FF_CHUNKS // SLOTS

        IN_CUT = [0, BLK, ATTN_W, ATTN_W + KV_W] + [ATTN_W + 2 * KV_W + BLK * u for u in range(5)]

        def query_job(head, c):
            return c if head == 0 else 3 * head - 1 + c

        def key_job(head):
            return 3 * head + 4 if head < EXPERT_HEADS - 1 else 3 * EXPERT_HEADS - 1

        def attention_units(second):
            return [(t, list(range(GROUP * g, GROUP * g + GROUP)))
                    for t in range(TILES) for g in range((HEADS2 if second else Q_HEADS) // GROUP)]

        block = ctx.enter_context(nc.Block())

        @block.sync
        def _(sp):
            sp.dma_start(c_rows[:], A["c"].rearrange("o (k p) -> (o k) p", p=P)).then_inc(c_loaded, 16)
            sp.dma_start(pos_i[:], A["positions"].rearrange("o (t p) -> (o t) p", p=P)).then_inc(pos_loaded, 16)

            def load(n, parts, given=slot_in):
                sp.wait_ge(slot_free[n % SLOTS], 1)
                sp.sem_inc(slot_free[n % SLOTS], -1)
                for off, rows, k, m, src in parts:
                    sp.dma_start(ring[0:rows, n % SLOTS, off:off + k * m].rearrange("p (k m) -> p k m", k=k), src).then_inc(given[n % SLOTS], 16)

            with sp.Fori(0, DEPTH) as l:
                def of(name):
                    return A[name][bass.ds(l, 1)].rearrange("o a b -> (o a) b")

                w_ada = of("w_ada").rearrange("(k p) n -> p k n", p=P)

                def load_ada(part, i, u):
                    load(u, [(0, P, KC, ADA_N, w_ada[:, :, bass.ds(i * (4 * ADA_N) + (part * 3 * D + u * ADA_N), ADA_N)])])

                def load_gain(name, gain, given, free):
                    sp.wait_ge(free, 1)
                    sp.sem_inc(free, -1)
                    sp.dma_start(gain[:], A[name][bass.ds(l, 1)].to_broadcast([P, D])).then_inc(given, 16)

                load_ada(0, 0, 0)
                sp.wait_ge(params_free, 1)
                sp.sem_inc(params_free, -1)
                sp.dma_start(mix_rows[0:6, :], A["conv_w"][bass.ds(l, 1)].rearrange("o k (c p) -> (o k c) p", p=P)).then_inc(pe_params, 16)
                sp.dma_start(mix_rows[6:8, :], A["pool_scale"][bass.ds(l, 1)].rearrange("o (c p) -> (o c) p", p=P)).then_inc(pe_params, 16)
                sp.dma_start(keys_raw[:], A["peer_keys"][bass.ds(l, 1)].rearrange("o s k d -> k (o s) d")).then_inc(pe_params, 16)
                groups = A["pool_w"][bass.ds(l, 1)].rearrange("o (c s) i e -> s i (o c) e", s=2)
                for s in range(2):
                    sp.dma_start(pool_w[HEAD * s:HEAD * s + HEAD, :, HEAD * s:HEAD * s + HEAD], groups[s]).then_inc(pe_params, 16)
                for part in range(2):
                    sp.dma_start(ada_bias[4 * part:4 * part + 4],
                                 A["b_ada"][bass.ds(l, 1)].rearrange("o (h i u n) -> h (o u) i n", h=2, u=4, n=ADA_N)[part]).then_inc(bias_in, 16)
                for n in range(1, 2 * SLOTS):
                    load_ada(0, n // SLOTS, n % SLOTS)
                load_gain("norm1_g", gain_pre, pre_in, pre_free)
                with sp.Fori(0, ADA_TURNS // 2) as i:
                    for u in range(4):
                        load_ada(1, i, u)
                load_gain("norm2_g", gain_post, post_in, post_free)
                sp.dma_start(qk_gain[:, 0:Q_HEADS, :], A["q_norm_g"][bass.ds(l, 1)].unsqueeze(1).to_broadcast([P, Q_HEADS, HEAD])).then_inc(dve_params, 16)
                sp.dma_start(qk_gain[:, Q_HEADS:QK, :], A["k_norm_g"][bass.ds(l, 1)].unsqueeze(1).to_broadcast([P, KV_HEADS, HEAD])).then_inc(dve_params, 16)
                sp.dma_start(sink[:], A["attn_sink"][bass.ds(l, 1)].to_broadcast([P, Q_HEADS])).then_inc(dve_params, 16)
                w_in = of("w_in").rearrange("(k p) n -> p k n", p=P)
                for u in range(8):
                    load(u, [(0, P, KC, IN_CUT[u + 1] - IN_CUT[u], w_in[:, :, IN_CUT[u]:IN_CUT[u + 1]])])
                w_out = of("w_out").rearrange("(k p) n -> p k n", p=P)
                for u in range(4):
                    load(u, [(0, P, 2, D, w_out[:, 2 * u:2 * u + 2, :])], plain_in)
                w_q = of("peer_wq").rearrange("(k p) n -> p k n", p=P)
                for u in range(8):
                    load(u, [(0, P, KC, BLK, w_q[:, :, u * BLK:(u + 1) * BLK])])

            def gain(name, layer, pre):
                src = A[name][layer:layer + 1, :] if layer is not None else A[name].unsqueeze(0)
                sp.wait_ge(pre_free if pre else post_free, 1)
                sp.sem_inc(pre_free if pre else post_free, -1)
                sp.dma_start((gain_pre if pre else gain_post)[:], src.to_broadcast([P, D])).then_inc(pre_in if pre else post_in, 16)

            def feed_forward(f):
                name, layer = FF_NAMES[f]
                w_g = A[name + "_w_gate_2"][layer].rearrange("(k p) n -> p k n", p=P)
                w_u = A[name + "_w_up_2"][layer].rearrange("(k p) n -> p k n", p=P)
                w_d = A[name + "_w_down_2"][layer].rearrange("(j p) n -> p j n", p=P)
                gain(name + "_pre_g_2", layer, True)

                def chunk(n, j):
                    load(n, [(0, P, KC, P, w_g[:, :, bass.ds(j * P, P)]),
                             (KC * P, P, KC, P, w_u[:, :, bass.ds(j * P, P)]),
                             (2 * KC * P, P, 1, D, w_d[:, bass.ds(j, 1), :])])

                n0 = first[f"ff{f}"]
                for j in range(PEEL):
                    chunk(n0 + j, j)
                with sp.Fori(0, TURNS) as i:
                    for u in range(SLOTS):
                        chunk(n0 + PEEL + u, i * SLOTS + (PEEL + u))
                gain(name + "_post_g_2", layer, False)

            feed_forward(0)
            rows = [("rg_conv_w_2", 0, CONV_K), ("rg_conv_b_2", 4, 1), ("rg_b_a_2", 5, 1), ("rg_b_x_2", 6, 1), ("rg_lambda_2", 7, 1)]
            for name, row, count in rows:
                src = A[name][0] if count > 1 else A[name]
                sp.dma_start(rnn_rows[row * R_CHUNKS:(row + count) * R_CHUNKS, :], src.rearrange("k (c p) -> (k c) p", p=RC)).then_inc(rnn_rows_in, 16)
            gain("mix_pre_g_2", 0, True)
            w = A["rg_w_in_2"][0].rearrange("(k p) n -> p k n", p=P)
            for u in range(R_CHUNKS):
                at = (u + R_CHUNKS // 2) % R_CHUNKS * 2 * RC
                load(first["rnn_in"] + u, [(0, P, KC, 2 * RC, w[:, :, at:at + 2 * RC])])
            gain("mix_post_g_2", 0, False)
            w = A["rg_w_out_2"][0].rearrange("(c p) n -> p c n", p=RC)
            for u in range(R_CHUNKS):
                load(first["rnn_out"] + u, [(0, RC, 1, D, w[:, u:u + 1, :])])
            feed_forward(1)
            sp.dma_start(wf[:], A["w_fgate_2"].rearrange("(k p) n -> p k n", p=P)).then_inc(wf_in, 16)
            sp.dma_start(bf[:], A["b_fgate_2"].unsqueeze(0)).then_inc(wf_in, 16)
            gain("kv_norm_g_2", None, True)
            w = A["w_kv_2"].rearrange("(k p) n -> p k n", p=P)
            for u in range(8):
                load(first["kv"] + u, [(0, P, KC, BLK, w[:, :, u * BLK:(u + 1) * BLK])])
            feed_forward(2)
            gain("mix_pre_g_2", 1, True)
            w = A["attn_w_q_2"][0].rearrange("(k p) n -> p k n", p=P)
            for u in range(4):
                load(first["q"] + u, [(0, P, KC, BLK, w[:, :, u * BLK:(u + 1) * BLK])])
            gain("mix_post_g_2", 1, False)
            w = A["attn_w_o_2"][0].rearrange("(k p) n -> p k n", p=P)
            for u in range(4):
                load(first["o"] + u, [(0, P, ROWS, D, w[:, ROWS * u:ROWS * u + ROWS, :])])
            feed_forward(3)
            sp.wait_ge(x_final, TILES)
            sp.sem_inc(x_final, -TILES)
            sp.dma_start(out.rearrange("o (t p) d -> p (o t) d", p=P), x[:]).then_inc(out_stored, 16)
            sp.wait_ge(out_stored, 16)

        @block.gpsimd
        def _(pool):
            g = nc.gpsimd
            build = Count()

            g.memset(zeros[:], 0.0).then_inc(const_steps, 1)
            pool.wait_ge(const_steps, build.next())
            g.memset(ones[:], 1.0).then_inc(const_steps, 1)
            pool.wait_ge(const_steps, build.next())
            g.affine_select(out=ident[:], in_=zeros[:], compare_op=ALU.not_equal, fill=1.0, base=0,
                            pattern=[[-1, P]], channel_multiplier=1).then_inc(const_steps, 1)
            pool.wait_ge(const_steps, build.next())
            g.affine_select(out=upto[:], in_=ones[:], compare_op=ALU.is_ge, fill=0.0, base=0,
                            pattern=[[1, P]], channel_multiplier=-1).then_inc(const_steps, 1)
            pool.wait_ge(const_steps, build.next())
            for i in range(ROPE // 2):
                g.memset(inv_freq[:, i:i + 1], float(ROPE_THETA ** (-2.0 * i / ROPE))).then_inc(const_steps, 1)
                pool.wait_ge(const_steps, build.next())
            g.memset(eps[:], EPS).then_inc(const_steps, 1)
            pool.wait_ge(const_steps, build.next())
            g.memset(pool_w[:], 0.0).then_inc(const_steps, 1)
            pool.wait_ge(const_steps, build.next())
            g.memset(expert_base[:], float(-EXPERTS)).then_inc(const_steps, 1)
            pool.wait_ge(const_steps, build.next())
            pool.sem_inc(consts, 1)
            pool.sem_inc(params_free, 1)
            g.memset(window[:], 0.0).then_inc(const_steps, 1)
            pool.wait_ge(const_steps, build.next())
            g.affine_select(out=window[:, 0, P:SEQ], in_=window[:, 0, P:SEQ], compare_op=ALU.is_ge, fill=MASKED,
                            base=0, pattern=[[-1, P]], channel_multiplier=1).then_inc(const_steps, 1)
            pool.wait_ge(const_steps, build.next())
            g.affine_select(out=window[:, 1, 0:P], in_=window[:, 1, 0:P], compare_op=ALU.is_ge, fill=MASKED,
                            base=0, pattern=[[1, P]], channel_multiplier=-1).then_inc(const_steps, 1)
            pool.wait_ge(const_steps, build.next())
            g.iota(iota16[:], pattern=[[1, TOPK]], base=0, channel_multiplier=0, allow_small_or_imprecise_dtypes=True).then_inc(const_steps, 1)
            pool.wait_ge(const_steps, build.next())
            token, ends, starts = h_ext[:, 0:SEQ], h_ext[:, SEQ:3 * SEQ], h_ext[:, 3 * SEQ:5 * SEQ]
            ends, starts = [part.rearrange("p (c t) -> p c t", c=2) for part in (ends, starts)]
            g.iota(token, pattern=[[1, SEQ]], base=0, channel_multiplier=0, allow_small_or_imprecise_dtypes=True).then_inc(const_steps, 1)
            pool.wait_ge(const_steps, build.next())
            for n, w in enumerate(WINDOWS):
                rows, cc = slice(HEAD * (n % 2), HEAD * (n % 2) + HEAD), n // 2
                g.tensor_scalar(ends[rows, cc, :], token[rows], float(w // 2), float(SEQ), ALU.add, ALU.min).then_inc(const_steps, 1)
                pool.wait_ge(const_steps, build.next())
                g.tensor_scalar(starts[rows, cc, :], token[rows], float(-(w // 2)), 0.0, ALU.add, ALU.max).then_inc(const_steps, 1)
                pool.wait_ge(const_steps, build.next())
            g.tensor_tensor(window_count[:], ends, starts, ALU.subtract).then_inc(const_steps, 1)
            pool.wait_ge(const_steps, build.next())
            g.memset(qTz[:], 0.0).then_inc(const_steps, 1)
            pool.wait_ge(const_steps, build.next())
            pool.sem_inc(const_steps, -build.reset())
            pool.sem_inc(tables, 1)
            pool.dma_start(x[:], A["x"].rearrange("o (t p) d -> p (o t) d", p=P)).then_inc(x_loaded, 16)

            steps = Count()
            with pool.Fori(0, DEPTH) as l:
                pool.wait_ge(share_ready, 1)
                pool.sem_inc(share_ready, -1)
                pool.wait_ge(zc_ready, 1)
                pool.sem_inc(zc_ready, -1)
                g.tensor_tensor(conv_u[:], zc[:, 4:6, :], zc[:, 0:2, :], ALU.mult).then_inc(pool_steps, 1)
                pool.wait_ge(pool_steps, steps.next())
                for cc in range(2):
                    w = [mix_cols[:, 2 * k + cc:2 * k + cc + 1] for k in range(3)]
                    g.tensor_scalar(conv_o[:, cc, :], conv_u[:, cc, :], w[1], None, ALU.mult).then_inc(pool_steps, 1)
                    pool.wait_ge(pool_steps, steps.next())
                    g.tensor_scalar(conv_t[:, cc, 1:SEQ], conv_u[:, cc, 0:SEQ - 1], w[0], None, ALU.mult).then_inc(pool_steps, 1)
                    pool.wait_ge(pool_steps, steps.next())
                    g.tensor_tensor(conv_o[:, cc, 1:SEQ], conv_o[:, cc, 1:SEQ], conv_t[:, cc, 1:SEQ], ALU.add).then_inc(pool_steps, 1)
                    pool.wait_ge(pool_steps, steps.next())
                    g.tensor_scalar(conv_t[:, cc, 0:SEQ - 1], conv_u[:, cc, 1:SEQ], w[2], None, ALU.mult).then_inc(pool_steps, 1)
                    pool.wait_ge(pool_steps, steps.next())
                    g.tensor_tensor(conv_o[:, cc, 0:SEQ - 1], conv_o[:, cc, 0:SEQ - 1], conv_t[:, cc, 0:SEQ - 1], ALU.add).then_inc(pool_steps, 1)
                    pool.wait_ge(pool_steps, steps.next())
                g.tensor_tensor(mixT[:, 4:6, :], conv_o[:], zc[:, 2:4, :], ALU.mult).then_inc(pool_steps, 1)
                pool.wait_ge(pool_steps, steps.next())
                g.memset(pool_in[:], 0.0).then_inc(pool_steps, 1)
                pool.wait_ge(pool_steps, steps.next())
                g.tensor_copy(pool_in[:, :, PAD:PAD + SEQ], zc[:, 6:8, :]).then_inc(pool_steps, 1)
                pool.wait_ge(pool_steps, steps.next())
                src, lo, hi = pool_in, 0, PADDED
                for n, w in enumerate(WINDOWS):
                    left, right = (1, 0) if w == 2 else (w // 4, w // 4)
                    dst = pool_s[n % 2]
                    lo, hi = lo + left, hi - right
                    g.tensor_tensor(dst[:, :, lo:hi], src[:, :, lo - left:hi - left], src[:, :, lo + right:hi + right], ALU.add).then_inc(pool_steps, 1)
                    pool.wait_ge(pool_steps, steps.next())
                    src = dst
                    rows, cc = slice(HEAD * (n % 2), HEAD * (n % 2) + HEAD), n // 2
                    g.tensor_tensor(pooled[rows, cc, :], src[rows, cc, PAD:PAD + SEQ], window_share[rows, cc, :], ALU.mult).then_inc(pool_steps, 1)
                    pool.wait_ge(pool_steps, steps.next())
                pool.sem_inc(pool_steps, -steps.reset())
                g.tensor_tensor(pooled[:], pooled[:], zc[:, 6:8, :], ALU.subtract).then_inc(pooled_ready, 1)

                def u_row(p, k):
                    pool.wait_ge(u_free, 1)
                    pool.sem_inc(u_free, -1)
                    g.indirect_dma_start(u_ring[:, k % U_SLOTS, :], None, A["peer_u"],
                                         bass.IndirectOffsetOnAxis(expert[:, p, k:k + 1], 0)).then_inc(u_in[k % U_SLOTS], 16)

                def v_row(p, k):
                    pool.wait_ge(v_free, 1)
                    pool.sem_inc(v_free, -1)
                    g.indirect_dma_start(v_ring[:, k, :], None, A["peer_v"],
                                         bass.IndirectOffsetOnAxis(expert[:, p, k:k + 1], 0)).then_inc(v_in[k], 16)

                def unit_rows(p, first_half):
                    for half in range(first_half, TOPK // GRP):
                        for j in range(GRP):
                            u_row(p, half * GRP + j)
                        for j in range(GRP):
                            v_row(p, half * GRP + j)

                pool.wait_ge(expert_ready, 1)
                pool.sem_inc(expert_ready, -1)
                for head in range(EXPERT_HEADS - SLOTS, EXPERT_HEADS):
                    pool.wait_ge(experts_open, 1)
                    pool.sem_inc(experts_open, -1)
                    for k in range(GRP):
                        if u_opened_by[k] == head:
                            u_row(0, k)
                    for k in range(GRP):
                        if EXPERT_HEADS - SLOTS + k // (SLOT // D) == head:
                            v_row(0, k)
                unit_rows(0, 1)
                pool.wait_ge(expert_ready, 1)
                pool.sem_inc(expert_ready, -1)
                unit_rows(1, 0)
                with pool.Fori(0, UNITS // 2 - 1) as n2:
                    for p in range(2):
                        pool.wait_ge(expert_ready, 1)
                        pool.sem_inc(expert_ready, -1)
                        unit_rows(p, 0)

            pool.wait_ge(ff0_over, 1)
            pool.sem_inc(ff0_over, -1)
            g.memset(w_gates[0], 0.0).then_inc(pool_steps, 1)
            pool.wait_ge(pool_steps, steps.next())
            g.memset(w_gates[1], 0.0).then_inc(pool_steps, 1)
            pool.wait_ge(pool_steps, steps.next())
            g.memset(rec_in[:, :, 0:CONV_K - 1], 0.0).then_inc(pool_steps, 1)
            pool.wait_ge(pool_steps, steps.next())
            pool.sem_inc(rnn_zeroed, 1)
            for which, name in enumerate(("rg_w_a_2", "rg_w_x_2")):
                src = A[name][0].rearrange("(s b) i d -> b i s d", b=SUPER)
                for b in range(SUPER):
                    lo = b * LRU
                    while lo < (b + 1) * LRU:
                        hi = min((b + 1) * LRU, (lo // RC + 1) * RC)
                        pool.dma_start(w_gates[which][lo % RC:lo % RC + hi - lo, :, lo // RC, b * LRU:(b + 1) * LRU],
                                       src[b, lo - b * LRU:hi - b * LRU]).then_inc(rnn_w_in, 16)
                        lo = hi
            pool.sem_inc(pool_steps, -steps.reset())
            pool.wait_ge(rnn_over, 1)
            pool.sem_inc(rnn_over, -1)
            g.memset(c_pad, 0.0).then_inc(c_pad_zeroed, 1)
            pool.wait_ge(ff2_over, 1)
            pool.sem_inc(ff2_over, -1)
            g.memset(qTz2, 0.0).then_inc(heads_zeroed, 1)

        @block.scalar
        def _(act):
            a = nc.scalar
            steps = Count()
            act.wait_ge(consts, 1)
            act.sem_inc(job_taken, 4)
            act.wait_ge(c_turned, 1)
            act.sem_inc(c_turned, -1)
            a.activation(c_act[:], ps[:, 0, 0:KC], ACT.Silu).then_inc(c_act_ready, 1)

            def mean_square(source, t, give):
                a.activation(junk, source, ACT.Square, accum_out=mean_sq[:, t:t + 1]).then_inc(act_steps, 1)
                act.wait_ge(act_steps, steps.next())
                a.activation(rms[:, t:t + 1], mean_sq[:, t:t + 1], ACT.Sqrt, bias=eps[:], scale=1.0 / D).then_inc(give, 1)

            def norm_x_tile(t):
                act.wait_ge(x_ready, 1)
                act.sem_inc(x_ready, -1)
                mean_square(x[:, t, :], t, rms_ready)

            def norm_x():
                for t in range(TILES):
                    norm_x_tile(t)
                act.sem_inc(act_steps, -steps.reset())

            def acc_rows(t):
                return ps[:, 2 * t:2 * t + 2, :].rearrange("p b n -> p (b n)")

            def norm_acc(last):
                a.activation(table_use[:], eps[:], ACT.Sqrt).then_inc(act_steps, 1)
                act.wait_ge(act_steps, steps.next())
                for t in range(TILES):
                    act.wait_ge(rows_done, 1)
                    act.sem_inc(rows_done, -1)
                    if t == TILES - 1:
                        act.sem_inc(slot_free[last % SLOTS], 1)
                    mean_square(acc_rows(t), t, rms2_ready)
                act.sem_inc(act_steps, -steps.reset())

            def evacuate_hT_tile(t, target, banks):
                for half in range(2):
                    act.wait_ge(hT_turned, 1)
                    act.sem_inc(hT_turned, -1)
                    a.activation(target[:, 4 * half:4 * half + 4, t * P:(t + 1) * P],
                                 ps[:, banks + 2 * t + half, :].rearrange("p (k t) -> p k t", t=P), ACT.Copy).then_inc(hT_ready, 1)

            def evacuate_hT(target):
                for t in range(TILES):
                    evacuate_hT_tile(t, target, WORK)

            def high(n, hi, width, dmas=1):
                slot = n % SLOTS
                act.wait_ge(slot_in[slot], dmas * 16)
                act.sem_inc(slot_in[slot], -dmas * 16)
                a.activation(hi[slot][:, 0:width], ring[:, slot, 0:width], ACT.Copy).then_inc(w_hi_ready, 1)

            def bank(j):
                return WORK + j % 4

            def softmax_exps(n_units, S, sinks):
                units = attention_units(not sinks)
                a.activation(table_use[:], eps[:], ACT.Exp).then_inc(act_steps, 1)
                act.wait_ge(act_steps, steps.next())
                for u in range(n_units):
                    b = u % 2
                    keys = SEQ if sinks else P * (units[u][0] + 1)
                    act.wait_ge(scores_ready, 1)
                    act.sem_inc(scores_ready, -1)
                    if sinks:
                        a.activation(sink_e[:, u % 4, :], sink_d[:, b, :], ACT.Exp)
                    for i in range(GROUP):
                        ins = a.activation(S[:, b, i, 0:keys], S[:, b, i, 0:keys], ACT.Exp, bias=neg_max[:, b, i:i + 1],
                                           accum_out=row_sum[:, u % 4, i:i + 1])
                    ins.then_inc(probs_ready, 1)
                    fan(act, sums_ready)
                    turned = pT if sinks else pT2
                    for half in range(2):
                        act.wait_ge(p_turned, 1)
                        act.sem_inc(p_turned, -1)
                        a.activation(turned[:, 4 * half:4 * half + 4, :], ps[:, half, :].rearrange("p (i t) -> p i t", t=P),
                                     ACT.Copy).then_inc(pT_ready, 1)

            act.wait_ge(angle_ready, 1)
            act.sem_inc(angle_ready, -1)
            a.activation(sine[:], angle[:, 2], ACT.Sin)
            a.activation(cosine[:], angle[:, 3], ACT.Sin).then_inc(rope_ready, 1)
            act.sem_inc(x_ready, TILES)
            with act.Fori(0, DEPTH) as l:
                for u in range(3):
                    high(u, ada_hi, KC * ADA_N)
                act.wait_ge(x_ready, TILES)
                act.wait_ge(params_turned, 1)
                act.sem_inc(params_turned, -1)
                a.activation(mix_cols[:], ps[:, 0, 0:8], ACT.Copy)
                a.activation(keysT[:].rearrange("p s k -> p (s k)"), ps[:, 1, 0:2 * KEYS], ACT.Copy)

                def mod_block(i, u):
                    act.wait_ge(job_done, 1)
                    act.sem_inc(job_done, -1)
                    act.sem_inc(slot_free[u], 1)
                    a.activation(mod.rearrange("p s d -> p (s d)")[:, bass.ds(i * (4 * ADA_N) + u * ADA_N, ADA_N)], ps[:, bank(u), 0:ADA_N],
                                 ACT.Copy).then_inc(job_taken, 1)

                with act.Fori(0, ADA_TURNS // 2) as i:
                    for u in range(4):
                        mod_block(i, u)
                        high(u + 3, ada_hi, KC * ADA_N)
                fan(act, mod_ready)
                act.wait_ge(x_loaded, 16)
                for n in range(2 * SLOTS):
                    mod_block(ADA_TURNS // 2 + n // SLOTS, n % SLOTS)
                    if n + 3 < 2 * SLOTS:
                        high(n + 3, ada_hi, KC * ADA_N)
                    else:
                        b = n + 3 - 2 * SLOTS
                        high(b, in_hi, KC * (IN_CUT[b + 1] - IN_CUT[b]))
                    if n in (0, 2):
                        norm_x_tile(n // 2)
                    if n in (4, 5):
                        evacuate_hT_tile(n - 4, hT_hi, 0)
                act.sem_inc(act_steps, -steps.reset())
                fan(act, mod_ready)
                job = 0
                for b in range(8):
                    for t in range(2):
                        act.wait_ge(job_done, 1)
                        act.sem_inc(job_done, -1)
                        if t == 1:
                            act.sem_inc(slot_free[b % SLOTS], 1)
                        if b < 2:
                            dst = qk[:, t, 0:Q_HEADS, :].rearrange("p (c g) d -> p g c d", g=KV_HEADS)[:, b]
                            src = ps[:, bank(job), 0:BLK].rearrange("p (c d) -> p c d", d=HEAD)
                        elif b == 2:
                            dst, src = qk[:, t, Q_HEADS:QK, :].rearrange("p h d -> p (h d)"), ps[:, bank(job), 0:KV_W]
                        elif b == 3:
                            dst, src = v_tok[:, t, :], ps[:, bank(job), 0:KV_W]
                        else:
                            dst, src = zc[:, 2 * (b - 4) + t, :], ps[:, bank(job), 0:SEQ]
                        a.activation(dst, src, ACT.Copy).then_inc(job_taken, 1)
                        job += 1
                    if b == 2:
                        fan(act, qk_ready)
                    if b + 3 < 8:
                        high(b + 3, in_hi, KC * (IN_CUT[b + 4] - IN_CUT[b + 3]))
                    if b == 3:
                        act.wait_ge(head_sq_ready, 1)
                        act.sem_inc(head_sq_ready, -1)
                        a.activation(head_rms[:], head_sq[:], ACT.Sqrt, bias=eps[:], scale=1.0 / HEAD).then_inc(head_rms_ready, 1)
                fan(act, zc_ready)
                for t in range(TILES):
                    act.wait_ge(qk_turned, 1)
                    act.sem_inc(qk_turned, -1)
                    for s in range(KV_HEADS):
                        rows = slice(HEAD * s, HEAD * s + HEAD)
                        a.activation(qTz[rows, GROUP * s:GROUP * s + GROUP, t * P:(t + 1) * P],
                                     ps[rows, WORK + t, :].rearrange("p (c t) -> p c t", t=P), ACT.Copy, scale=HEAD ** -0.5)
                act.wait_ge(qk_turned, 1)
                act.sem_inc(qk_turned, -1)
                a.activation(kT, ps[:, WORK + 2, 0:SEQ], ACT.Copy).then_inc(qkT_ready, 1)
                softmax_exps(TILES * KV_HEADS, scores, True)
                act.wait_ge(pool_done, 1)
                act.sem_inc(pool_done, -1)
                for cc in range(2):
                    a.activation(mixT[:, 6 + cc, :], ps[:, WORK + 2, cc * SEQ:(cc + 1) * SEQ], ACT.Copy, scale=mix_cols[:, 6 + cc:7 + cc])
                for t in range(TILES):
                    act.wait_ge(attn_turned, 1)
                    act.sem_inc(attn_turned, -1)
                    a.activation(mixT[:, 0:4, t * P:(t + 1) * P], ps[:, WORK + t, :].rearrange("p (c t) -> p c t", t=P),
                                 ACT.Copy).then_inc(mixT_ready, 1)
                a.activation(table_use[:], eps[:], ACT.Sqrt).then_inc(act_steps, 1)
                act.wait_ge(act_steps, steps.next())
                norm_x_tile(0)
                high(0, in_hi, KC * BLK)
                high(1, in_hi, KC * BLK)
                norm_x_tile(1)
                act.sem_inc(act_steps, -steps.reset())
                evacuate_hT(hT_hi)
                def key_products(head):
                    act.wait_ge(job_done, 1)
                    act.sem_inc(job_done, -1)
                    a.activation(key_s.rearrange("p (t n) h k -> p t n (h k)", t=TILES)[:, :, head, :],
                                 ps[:, bank(key_job(head)), :].rearrange("p (t k) -> p t k", t=TILES),
                                 ACT.Copy).then_inc(job_taken, 1)
                    fan(act, key_s_ready)

                for head in range(EXPERT_HEADS):
                    for c in range(2):
                        act.wait_ge(job_done, 1)
                        act.sem_inc(job_done, -1)
                        if c == 1 and head < EXPERT_HEADS - SLOTS:
                            act.sem_inc(slot_free[head % SLOTS], 1)
                        if c == 1 and head >= EXPERT_HEADS - SLOTS:
                            act.sem_inc(experts_open, 1)
                        ins = a.activation(qpT[:, head % 2, c, :], ps[:, bank(query_job(head, c)), 0:SEQ], ACT.Copy)
                        ins.then_inc(job_taken, 1)
                    fan(act, queries_ready)
                    if head + 2 < EXPERT_HEADS:
                        high(head + 2, in_hi, KC * BLK)
                    if head >= 1:
                        key_products(head - 1)
                key_products(EXPERT_HEADS - 1)
                act.sem_inc(key_s_ready, 1)

                def gate_exp(p):
                    act.wait_ge(top_ready, 1)
                    act.sem_inc(top_ready, -1)
                    a.activation(gate_e[:, p, :], top[:, p, :], ACT.Exp, bias=neg_top[:, p, :], accum_out=gate_sum[:, p, :]).then_inc(gate_ready, 1)

                def gelu(half):
                    act.wait_ge(dots_ready, 1)
                    act.sem_inc(dots_ready, -1)
                    a.activation(acts[:, half, :], dots[:, half, :], ACT.Gelu).then_inc(acts_ready, 1)

                gate_exp(0)
                with act.Fori(0, UNITS // 2 - 1) as n2:
                    for p in range(2):
                        gelu(0)
                        gate_exp(1 - p)
                        gelu(1)
                gelu(0)
                gate_exp(1)
                gelu(1)
                gelu(0)
                gelu(1)

            def high_ff(n):
                high(n, w_hi_slots, FF_SLOT, 3)

            def high_block(n):
                high(n, w_hi_slots, KC * BLK)

            def high_rnn(n):
                slot = n % SLOTS
                act.wait_ge(slot_in[slot], 16)
                act.sem_inc(slot_in[slot], -16)
                rows, width = (P, RNN_IN) if n < first["rnn_out"] else (RC, D)
                a.activation(rnn_hi[0:rows, slot, 0:width], ring[0:rows, slot, 0:width], ACT.Copy).then_inc(w_hi_ready, 1)

            def feed_forward(f, ahead):
                n0 = first[f"ff{f}"]

                def silu(b):
                    act.wait_ge(gu_done, 1)
                    act.sem_inc(gu_done, -1)
                    a.activation(silu_g[:, b, :], ps[:, WORK + b, 0:SEQ], ACT.Silu).then_inc(silu_ready, 1)

                norm_x()
                if f < 2:
                    high_ff(n0)
                evacuate_hT(hT_hi)
                if f < 2:
                    high_ff(n0 + 1)
                with act.Fori(0, (FF_CHUNKS - 2) // SLOTS) as i:
                    for u in range(SLOTS):
                        silu(u % 2)
                        high_ff(n0 + 2 + u)
                for u in range(2):
                    silu(u)
                    if ahead is not None:
                        ahead(n0 + FF_CHUNKS + u)
                norm_acc(n0 + FF_CHUNKS - 1)

            feed_forward(0, high_rnn)
            norm_x()
            evacuate_hT(hT_hi)
            act.wait_ge(rnn_turned, 1)
            act.sem_inc(rnn_turned, -1)
            a.activation(rnn_cols[:].rearrange("p k c -> p (k c)"), ps[0:RC, 0, 0:8 * R_CHUNKS], ACT.Copy).then_inc(rnn_cols_ready, 1)
            act.wait_ge(lam_abs, 1)
            act.sem_inc(lam_abs, -1)
            a.activation(decay[:, 1, :], decay[:, 0, :], ACT.Exp, scale=-1.0).then_inc(lam_exp, 1)
            job = 0

            def evacuate(j, dst, function, gate_half=False):
                nonlocal job
                act.wait_ge(job_done, 1)
                act.sem_inc(job_done, -1)
                block = first["rnn_in"] + j // 2 + (R_CHUNKS // 2 if gate_half else 0)
                if j % 2 == 1:
                    act.sem_inc(slot_free[block % SLOTS], 1)
                a.activation(dst, ps[0:RC, bank(job), 0:SEQ], function).then_inc(job_taken, 1)
                job += 1
                if j % 2 == 1:
                    high_rnn(block + 2)

            def inputs(s):
                for j in range(3 * s, 3 * s + 3):
                    evacuate(j, rec_in[:, j, CONV_K - 1:], ACT.Copy)
                fan(act, rec_in_ready)

            def gates(s):
                nonlocal job
                for dst, row in ((gate_r, 5), (gate_i, 6)):
                    for j in range(3 * s, 3 * s + 3):
                        act.wait_ge(job_done, 1)
                        act.sem_inc(job_done, -1)
                        a.activation(dst[:, j, :], ps[0:RC, bank(job), 0:SEQ], ACT.Sigmoid, bias=rnn_cols[:, row, j:j + 1]).then_inc(job_taken, 1)
                        job += 1
                fan(act, act_steps)
                act.wait_ge(act_steps, steps.next())
                for j in range(3 * s, 3 * s + 3):
                    ins = a.activation(decay_a[:, j, :], gate_r[:, j, :], ACT.Exp, scale=decay_neg[:, j:j + 1])
                ins.then_inc(act_steps, 1)
                act.wait_ge(act_steps, steps.next())
                for j in range(3 * s, 3 * s + 3):
                    ins = a.activation(gate_r[:, j, :], gate_r[:, j, :], ACT.Tanh, scale=decay_pos[:, j:j + 1])
                ins.then_inc(gates_ready, 1)

            def roots(s):
                act.wait_ge(root_in, 1)
                act.sem_inc(root_in, -1)
                part = gate_r[:, 3 * s:3 * s + 3, :]
                a.activation(part, part, ACT.Sqrt).then_inc(root_ready, 1)

            inputs(0)
            inputs(1)
            act.wait_ge(decay_ready, 1)
            act.sem_inc(decay_ready, -1)
            gates(0)
            inputs(2)
            gates(1)
            inputs(3)
            gates(2)
            for j in range(4):
                evacuate(j, gate_g[:, j, :], ACT.Copy, True)
            gates(3)
            for j in range(4, 6):
                evacuate(j, gate_g[:, j, :], ACT.Copy, True)
            for s in range(3):
                roots(s)
            for j in range(6, 8):
                evacuate(j, gate_g[:, j, :], ACT.Copy, True)
            roots(3)
            fan(act, act_steps)
            act.wait_ge(act_steps, steps.next())
            for lo, hi in ((0, 3), (3, 6), (6, 8)):
                ins = a.activation(gate_g[:, lo:hi, :], gate_g[:, lo:hi, :], ACT.Gelu_apprx_tanh)
                if hi % 3 == 0:
                    ins.then_inc(gelu_ready, 1)
            for j in range(8, R_CHUNKS):
                evacuate(j, gate_g[:, j, :], ACT.Gelu_apprx_tanh, True)
                if j % 3 == 2:
                    fan(act, gelu_ready)
            for u in range(2, R_CHUNKS):
                high_rnn(first["rnn_out"] + u)
            act.sem_inc(act_steps, -steps.reset())
            norm_acc(first["rnn_out"] + R_CHUNKS - 1)
            feed_forward(1, high_block)
            norm_x()
            evacuate_hT(hT_hi)
            act.wait_ge(job_done, 1)
            act.sem_inc(job_done, -1)
            a.activation(f_tok[:], ps[:, bank(0), 0:TILES * HEADS2], ACT.Copy).then_inc(f_ready, 1)
            fan(act, job_taken)
            act.wait_ge(f_abs, 1)
            act.sem_inc(f_abs, -1)
            a.activation(logs[:, 1, :], logs[:, 0, :], ACT.Exp, scale=-1.0).then_inc(f_exp, 1)
            n0 = first["kv"]
            for j in range(16):
                act.wait_ge(job_done, 1)
                act.sem_inc(job_done, -1)
                if j % 2 == 1:
                    act.sem_inc(slot_free[(n0 + j // 2) % SLOTS], 1)
                b = j // 2
                dst = kT2[:, j, :] if b < 4 else v2[:, j % 2, (b - 4) * BLK:(b - 3) * BLK]
                a.activation(dst, ps[:, bank(j + 1), 0:BLK], ACT.Copy).then_inc(job_taken, 1)
                if j % 2 == 1:
                    if b + 2 < 8:
                        high_block(n0 + b + 2)
                    else:
                        high_ff(n0 + b + 2)
            act.wait_ge(c_summed, 1)
            act.sem_inc(c_summed, -1)
            a.activation(c_tok[:], ps[:, 0, 0:TILES * HEADS2], ACT.Copy)
            act.wait_ge(c_pad_zeroed, 1)
            a.activation(c_pad[:, :, 0:HEADS2], ps[:, 0, 0:TILES * HEADS2].rearrange("p (t h) -> p t h", t=TILES), ACT.Copy,
                         scale=-1.0).then_inc(c_ready, 1)
            act.wait_ge(c_back, 1)
            act.sem_inc(c_back, -1)
            a.activation(neg_cT, ps[:, 1, 0:SEQ], ACT.Copy).then_inc(neg_cT_ready, 1)
            feed_forward(2, high_block)
            norm_x()
            evacuate_hT(hT_hi)
            act.wait_ge(heads_zeroed, 1)
            act.sem_inc(heads_zeroed, -1)
            n0 = first["q"]
            for j in range(8):
                act.wait_ge(job_done, 1)
                act.sem_inc(job_done, -1)
                if j % 2 == 1:
                    act.sem_inc(slot_free[(n0 + j // 2) % SLOTS], 1)
                for s in range(2):
                    rows, head = slice(HEAD * s, HEAD * s + HEAD), 2 * j + s
                    ins = a.activation(qTz2[rows, head // GROUP, head % GROUP, :], ps[rows, bank(j), 0:SEQ], ACT.Copy, scale=HEAD ** -0.5)
                ins.then_inc(job_taken, 1)
                if j % 2 == 1:
                    high_block(n0 + j // 2 + 2)
            softmax_exps(TILES * HEADS2 // GROUP, scores2, False)
            evacuate_hT(hT_hi)
            n0 = first["o"]
            for u in range(2):
                high_block(n0 + 2 + u)
            for u in range(2):
                high_ff(n0 + 4 + u)
            norm_acc(first["o"] + 3)
            feed_forward(3, None)

        @block.tensor
        def _(pe):
            mm = nc.tensor.matmul
            for one in slot_free:
                pe.sem_inc(one, 1)
            pe.wait_ge(consts, 1)
            pe.wait_ge(c_loaded, 16)
            pe.sem_inc(c_loaded, -16)
            nc.tensor.transpose(ps[:, 0, 0:KC], c_rows[:], ident[0:KC, 0:KC]).then_inc(c_turned, 1)
            pe.wait_ge(pos_float, 1)
            pe.sem_inc(pos_float, -1)
            nc.tensor.transpose(ps[:, 3, 0:TILES], pos_f[:], ident[0:TILES, 0:TILES]).then_inc(pos_turned, 1)
            pe.wait_ge(c_split, 1)
            pe.sem_inc(c_split, -1)

            def bank(j):
                return WORK + j % 4

            def turn_h_tile(t, banks):
                pe.wait_ge(h_ready, 1)
                pe.sem_inc(h_ready, -1)
                for half in range(2):
                    for k in range(4):
                        ins = nc.tensor.transpose(ps[:, banks + 2 * t + half, k * P:(k + 1) * P],
                                                  h[:, t, (4 * half + k) * P:(4 * half + k + 1) * P], ident[:])
                    ins.then_inc(hT_turned, 1)

            def turn_h():
                for t in range(TILES):
                    turn_h_tile(t, WORK)

            def weights(n):
                pe.wait_ge(plain_in[n % SLOTS], 16)
                pe.sem_inc(plain_in[n % SLOTS], -16)
                return ring[:, n % SLOTS, :]

            def three_passes(where, pairs):
                for k, (w_high, w_low, s_high, s_low) in enumerate(pairs):
                    mm(where, w_high, s_high, start=(k == 0), stop=False)
                    mm(where, w_high, s_low, start=False, stop=False)
                    ins = mm(where, w_low, s_high, start=False, stop=(k == len(pairs) - 1))
                return ins

            def split_weights(n, hi, width):
                pe.wait_ge(w_split, 1)
                pe.sem_inc(w_split, -1)
                return [part[:, 0:KC * width].rearrange("p (k n) -> p k n", k=KC) for part in (hi[n % SLOTS], ring_lo[:, n % SLOTS, :])]

            def channel_job(j, w, col, low):
                pe.wait_ge(job_taken, 1)
                pe.sem_inc(job_taken, -1)
                cols = slice(col, col + P)
                three_passes(ps[:, bank(j), 0:SEQ], [(w[0][:, k, cols], w[1][:, k, cols], hT_hi[:, k, :], low[:, k, :])
                                                     for k in range(KC)]).then_inc(job_done, 1)

            def token_job(j, w, width, t, low):
                pe.wait_ge(job_taken, 1)
                pe.sem_inc(job_taken, -1)
                tokens = slice(t * P, (t + 1) * P)
                three_passes(ps[:, bank(j), 0:width], [(hT_hi[:, k, tokens], low[:, k, tokens], w[0][:, k, :], w[1][:, k, :])
                                                       for k in range(KC)]).then_inc(job_done, 1)

            BOTH = (0, 1)

            def accumulate_rows(parts, start, stop, places=((0, BOTH), (1, BOTH))):
                for t, halves in places:
                    for i, (source, w) in enumerate(parts):
                        for c in halves:
                            ins = mm(ps[:, 2 * t + c, :], source[:, t * P:(t + 1) * P], w[:, c * N:(c + 1) * N],
                                     start=start and i == 0, stop=stop and i == len(parts) - 1)
                    if stop:
                        ins.then_inc(rows_done, 1)
                return ins

            def attend(second):
                units = attention_units(second)
                keys_of, turned = (lambda i: kT2[:, i // 2, :], pT2) if second else (lambda i: kT, pT)
                S = scores2 if second else scores

                def score(u):
                    t, heads = units[u]
                    n = P * (t + 1) if second else SEQ
                    for i, head in enumerate(heads):
                        where = ps[:, WORK + 2 * (u % 2) + i // 2, (i % 2) * SEQ:(i % 2) * SEQ + n]
                        query = qTz2[:, head // GROUP, head % GROUP, :] if second else qTz[:, head, :]
                        ins = mm(where, query[:, t * P:(t + 1) * P], keys_of(head)[:, 0:n], start=True, stop=not second)
                        if second:
                            ins = mm(where, ident[:, head:head + 1].to_broadcast([P, P]), neg_cT[:, 0:n], start=False, stop=True)
                    ins.then_inc(scores_done, 1)

                score(0)
                score(1)
                for u, (t, heads) in enumerate(units):
                    chunks = t + 1 if second else TILES
                    pe.wait_ge(probs_ready, 1)
                    pe.sem_inc(probs_ready, -1)
                    for half in range(2):
                        for i in range(2 * half, 2 * half + 2):
                            for k in range(TILES):
                                src = min(k, chunks - 1)
                                ins = nc.tensor.transpose(ps[:, half, ((2 * i + k) % 4) * P:((2 * i + k) % 4 + 1) * P],
                                                          S[:, u % 2, i, src * P:(src + 1) * P], ident[:])
                        ins.then_inc(p_turned, 1)
                    if u + 2 < len(units):
                        score(u + 2)
                    pe.wait_ge(pT_ready, 2)
                    pe.sem_inc(pT_ready, -2)
                    if u >= 2:
                        pe.wait_ge(attn_done, 1)
                        pe.sem_inc(attn_done, -1)
                    for i, head in enumerate(heads):
                        for k in range(chunks):
                            values = v2[:, k, head * HEAD:(head + 1) * HEAD] if second else \
                                v_tok[:, k, (head // GROUP) * HEAD:(head // GROUP + 1) * HEAD]
                            ins = mm(ps[:, 2 + u % 2, i * HEAD:(i + 1) * HEAD], turned[:, 2 * i + k, :], values,
                                     start=(k == 0), stop=(k == chunks - 1))
                    ins.then_inc(pv_done, 1)
                pe.wait_ge(attn_done, 2)
                pe.sem_inc(attn_done, -2)

            with pe.Fori(0, DEPTH) as l:
                pe.wait_ge(pe_params, 5 * 16)
                pe.sem_inc(pe_params, -5 * 16)
                pe.wait_ge(acc_read, 1)
                pe.sem_inc(acc_read, -1)
                nc.tensor.transpose(ps[:, 0, 0:8], mix_rows[:], ident[0:8, 0:8])
                for s in range(2):
                    ins = nc.tensor.transpose(ps[:, 1, s * KEYS:(s + 1) * KEYS], keys_raw[:, s, :], ident[:])
                ins.then_inc(params_turned, 1)
                pe.wait_ge(bias_in, 2 * 16)
                pe.sem_inc(bias_in, -2 * 16)

                def mod_block(part, i, u):
                    w = split_weights(u, ada_hi, ADA_N)
                    pe.wait_ge(job_taken, 1)
                    pe.sem_inc(job_taken, -1)
                    where = ps[:, bank(u), 0:ADA_N]
                    row = 4 * part + u
                    mm(where, ident[0:8, row:row + 1].to_broadcast([8, P]), ada_bias[:, bass.ds(i, 1), :].rearrange("p i n -> p (i n)"),
                       start=True, stop=False)
                    for k in range(KC):
                        c_high, c_low = [part[:, k:k + 1].to_broadcast([P, P]) for part in (c_hi, c_lo)]
                        mm(where, c_high, w[0][:, k, :], start=False, stop=False)
                        mm(where, c_high, w[1][:, k, :], start=False, stop=False)
                        ins = mm(where, c_low, w[0][:, k, :], start=False, stop=(k == KC - 1))
                    ins.then_inc(job_done, 1)

                with pe.Fori(0, ADA_TURNS // 2) as i:
                    for u in range(4):
                        mod_block(0, i, u)
                for n in range(2 * SLOTS):
                    mod_block(1, n // SLOTS, n % SLOTS)
                    if n in (3, 4):
                        turn_h_tile(n - 3, 0)
                pe.wait_ge(hT_split, 4)
                pe.sem_inc(hT_split, -4)
                job = 0
                for b in range(8):
                    width = IN_CUT[b + 1] - IN_CUT[b]
                    w = split_weights(b, in_hi, width)
                    for t in range(2):
                        if b < 4:
                            token_job(job, w, width, t, hT_lo1)
                        else:
                            channel_job(job, w, t * P, hT_lo1)
                        job += 1
                pe.wait_ge(qk_done, 1)
                pe.sem_inc(qk_done, -1)
                pe.wait_ge(job_taken, 4)
                for t in range(TILES):
                    for c in range(4):
                        ins = nc.tensor.transpose(ps[:, WORK + t, c * P:(c + 1) * P],
                                                  qk[:, t, 2 * c:2 * c + 2, :].rearrange("p h d -> p (h d)"), ident[:])
                    ins.then_inc(qk_turned, 1)
                for t in range(TILES):
                    ins = nc.tensor.transpose(ps[:, WORK + 2, t * P:(t + 1) * P],
                                              qk[:, t, Q_HEADS:QK, :].rearrange("p h d -> p (h d)"), ident[:])
                ins.then_inc(qk_turned, 1)
                pe.wait_ge(qkT_ready, 1)
                pe.sem_inc(qkT_ready, -1)
                attend(False)
                pe.wait_ge(pooled_ready, 1)
                pe.sem_inc(pooled_ready, -1)
                for cc in range(2):
                    ins = mm(ps[:, WORK + 2, cc * SEQ:(cc + 1) * SEQ], pool_w[:, cc, :], pooled[:, cc, :], start=True, stop=True)
                ins.then_inc(pool_done, 1)
                for t in range(TILES):
                    for c in range(4):
                        ins = nc.tensor.transpose(ps[:, WORK + t, c * P:(c + 1) * P], attn[:, t, c * P:(c + 1) * P], ident[:])
                    ins.then_inc(attn_turned, 1)
                pe.wait_ge(mixT_ready, TILES)
                pe.sem_inc(mixT_ready, -TILES)
                blocks = []
                for b in range(4):
                    w = weights(b).rearrange("p (k n) -> p k n", n=D)
                    blocks.append([(mixT[:, 2 * b + k, :], w[:, k, :]) for k in range(2)])
                    for k in range(2):
                        accumulate_rows(blocks[b][k:k + 1], b == 0 and k == 0, b == 3 and k == 1, [(0, BOTH)])
                for b in range(4):
                    for k in range(2):
                        ins = accumulate_rows(blocks[b][k:k + 1], b == 0 and k == 0, b == 3 and k == 1, [(1, BOTH)])
                    if b < 3:
                        ins.then_inc(slot_free[b], 1)
                turn_h()
                pe.wait_ge(hT_split, 4)
                pe.sem_inc(hT_split, -4)
                def key_products(head):
                    pe.wait_ge(queries_ready, 1)
                    pe.sem_inc(queries_ready, -1)
                    pe.wait_ge(job_taken, 1)
                    pe.sem_inc(job_taken, -1)
                    for t in range(TILES):
                        for c in range(2):
                            ins = mm(ps[:, bank(key_job(head)), (2 * t + c) * KEYS:(2 * t + c + 1) * KEYS],
                                     qpT[:, head % 2, c, t * P:(t + 1) * P], keysT[:, c, :], start=True, stop=True)
                    ins.then_inc(job_done, 1)

                for head in range(EXPERT_HEADS):
                    w = split_weights(head, in_hi, BLK)
                    for c in range(2):
                        channel_job(query_job(head, c), w, c * P, query_lo)
                    if head >= 1:
                        key_products(head - 1)
                key_products(EXPERT_HEADS - 1)
                pe.wait_ge(diag_ready, 1)
                for b in range(4):
                    mm(ps[:, b, :], zeros[:], h[:, 0, 0:N], start=True, stop=False, skip_group_check=True)
                for t in range(TILES):
                    with pe.Fori(0, EXPERT_HEADS // 2) as i:
                        for p in range(2):
                            for k in range(TOPK):
                                pe.wait_ge(diag_ready, 1)
                                pe.sem_inc(diag_ready, -1)
                                pe.wait_ge(v_in[k], (l * UNITS + (i * 2 + (t * EXPERT_HEADS + p + 1))) * 16)
                                for c in range(2):
                                    ins = mm(ps[:, 2 * t + c, :], diag[:, k, :], v_ring[:, k, c * N:(c + 1) * N],
                                             start=False, stop=False, skip_group_check=True)
                                ins.then_inc(v_free, 1)
                                if k % GRP == GRP - 1:
                                    fan(pe, diag_free)
                    fan(pe, y_ready)

            def feed_forward(f):
                turn_h()
                pe.wait_ge(hT_split, 4)
                pe.sem_inc(hT_split, -4)
                n0 = first[f"ff{f}"]

                def gate_up(n, b):
                    pe.wait_ge(w_split, 1)
                    pe.sem_inc(w_split, -1)
                    hi = w_hi[:, n % SLOTS, :].rearrange("p (k m) -> p k m", m=P)
                    lo = ring_lo[:, n % SLOTS, 0:FF_SLOT].rearrange("p (k m) -> p k m", m=P)
                    for g in range(2):
                        ins = three_passes(ps[:, WORK + b, g * SEQ:(g + 1) * SEQ],
                                           [(hi[:, g * KC + k, :], lo[:, g * KC + k, :], hT_hi[:, k, :], hT_lo[:, k, :]) for k in range(KC)])
                    ins.then_inc(gu_done, 1)

                def down_parts(n, b):
                    pe.wait_ge(ff_ready, 1)
                    pe.sem_inc(ff_ready, -1)
                    hi, lo = w_hi[:, n % SLOTS, 2 * KC * P:], ring_lo[:, n % SLOTS, 2 * KC * P:FF_SLOT]
                    return [(ff_hi[:, b, :], hi), (ff_hi[:, b, :], lo), (ff_lo[:, b, :], hi)]

                def down(n, b, start=False):
                    accumulate_rows(down_parts(n, b), start, False).then_inc(slot_free[n % SLOTS], 1)

                gate_up(n0, 0)
                for j in range(1, PEEL):
                    gate_up(n0 + j, j % 2)
                    down(n0 + j - 1, (j - 1) % 2, start=(j == 1))
                with pe.Fori(0, TURNS - 1) as i:
                    for u in range(SLOTS):
                        gate_up(n0 + PEEL + u, (PEEL + u) % 2)
                        down(n0 + PEEL + u - 1, (PEEL + u - 1) % 2)
                for u in range(SLOTS):
                    gate_up(n0 + PEEL + u, (PEEL + u) % 2)
                    if u < SLOTS - 1:
                        down(n0 + PEEL + u - 1, (PEEL + u - 1) % 2)
                n = n0 + FF_CHUNKS - 2
                before = down_parts(n, FF_CHUNKS % 2)
                accumulate_rows(before, False, False, [(0, BOTH), (1, (0,))])
                last = down_parts(n + 1, (FF_CHUNKS - 1) % 2)
                accumulate_rows(last, False, True, [(0, BOTH)])
                accumulate_rows(before, False, False, [(1, (1,))]).then_inc(slot_free[n % SLOTS], 1)
                accumulate_rows(last, False, True, [(1, BOTH)])

            feed_forward(0)
            turn_h()
            pe.wait_ge(hT_split, 4)
            pe.sem_inc(hT_split, -4)
            pe.wait_ge(rnn_rows_in, 5 * 16)
            pe.sem_inc(rnn_rows_in, -5 * 16)
            nc.tensor.transpose(ps[0:RC, 0, 0:8 * R_CHUNKS], rnn_rows[:], ident[0:8 * R_CHUNKS, 0:8 * R_CHUNKS]).then_inc(rnn_turned, 1)
            job = 0

            def inputs(chunks):
                nonlocal job, w
                for j in chunks:
                    if j % 2 == 0:
                        n = first["rnn_in"] + j // 2 + (R_CHUNKS // 2 if gate_half else 0)
                        pe.wait_ge(w_split, 1)
                        pe.sem_inc(w_split, -1)
                        w = [part[:, n % SLOTS, 0:RNN_IN].rearrange("p (k n) -> p k n", k=KC) for part in (rnn_hi, ring_lo)]
                    pe.wait_ge(job_taken, 1)
                    pe.sem_inc(job_taken, -1)
                    cols = slice(j % 2 * RC, j % 2 * RC + RC)
                    three_passes(ps[0:RC, bank(job), 0:SEQ], [(w[0][:, k, cols], w[1][:, k, cols], hT_hi[:, k, :], hT_lo_r[:, k // 2, k % 2, :])
                                                             for k in range(KC)]).then_inc(job_done, 1)
                    job += 1

            def gates(s):
                nonlocal job
                pe.wait_ge(rec_ready, 1)
                pe.sem_inc(rec_ready, -1)
                for which in range(2):
                    for jj in range(3):
                        pe.wait_ge(job_taken, 1)
                        pe.sem_inc(job_taken, -1)
                        near = [i for i in range(3) if abs(i - jj) <= 1]
                        for i in near:
                            ins = mm(ps[0:RC, bank(job), 0:SEQ], w_gates[which][:, s, i, jj * RC:(jj + 1) * RC], rec[:, 3 * s + i, :],
                                     start=(i == near[0]), stop=(i == near[-1]))
                        ins.then_inc(job_done, 1)
                        job += 1

            w, gate_half = None, False
            inputs(range(0, 3))
            inputs(range(3, 6))
            pe.wait_ge(rnn_w_in, 2 * 6 * 16)
            gates(0)
            inputs(range(6, 9))
            gates(1)
            inputs(range(9, 12))
            gates(2)
            gate_half = True
            inputs(range(0, 4))
            gates(3)
            inputs(range(4, R_CHUNKS))
            late = []
            for u in range(R_CHUNKS):
                if u % 3 == 0:
                    pe.wait_ge(rnn_out_ready, 1)
                    pe.sem_inc(rnn_out_ready, -1)
                slot = (first["rnn_out"] + u) % SLOTS
                pe.wait_ge(w_split, 1)
                pe.sem_inc(w_split, -1)
                hi, lo = rnn_hi[0:RC, slot, 0:D], ring_lo[0:RC, slot, 0:D]
                parts = [(out_hi[0:RC, u, :], hi), (out_hi[0:RC, u, :], lo), (out_lo[0:RC, u, :], hi)]
                if u < R_CHUNKS - 3:
                    accumulate_rows(parts, u == 0, False).then_inc(slot_free[slot], 1)
                else:
                    accumulate_rows(parts, False, u == R_CHUNKS - 1, [(0, BOTH)])
                    late.append((slot, parts))
            for slot, parts in late[:-1]:
                accumulate_rows(parts, False, False, [(1, BOTH)]).then_inc(slot_free[slot], 1)
            accumulate_rows(late[-1][1], False, True, [(1, BOTH)])
            feed_forward(1)
            turn_h()
            pe.wait_ge(hT_split, 4)
            pe.sem_inc(hT_split, -4)
            pe.wait_ge(wf_in, 32)
            pe.sem_inc(wf_in, -32)
            pe.wait_ge(job_taken, 1)
            pe.sem_inc(job_taken, -1)
            for t in range(TILES):
                where = ps[:, bank(0), t * HEADS2:(t + 1) * HEADS2]
                for k in range(KC):
                    for i, part in enumerate((hT_hi, hT_lo)):
                        mm(where, part[:, k, t * P:(t + 1) * P].bitcast(F32), wf[:, k, :], start=(k == 0 and i == 0), stop=False)
                ins = mm(where, ones[0:1, :], bf[:], start=False, stop=True)
            ins.then_inc(job_done, 1)
            for b in range(8):
                w = split_weights(first["kv"] + b, w_hi_slots, BLK)
                for c in range(2):
                    if b < 4:
                        channel_job(2 * b + c + 1, w, c * P, hT_lo)
                    else:
                        token_job(2 * b + c + 1, w, BLK, c, hT_lo)
            pe.wait_ge(log_f_ready, 1)
            pe.sem_inc(log_f_ready, -1)
            mm(ps[:, 0, 0:HEADS2], upto[:], log_f[:, 0:HEADS2], start=True, stop=True)
            mm(ps[:, 0, HEADS2:2 * HEADS2], ones[:], log_f[:, 0:HEADS2], start=True, stop=False)
            mm(ps[:, 0, HEADS2:2 * HEADS2], upto[:], log_f[:, HEADS2:2 * HEADS2], start=False, stop=True).then_inc(c_summed, 1)
            pe.wait_ge(c_ready, 1)
            pe.sem_inc(c_ready, -1)
            for t in range(TILES):
                ins = nc.tensor.transpose(ps[:, 1, t * P:(t + 1) * P], c_pad[:, t, :], ident[:])
            ins.then_inc(c_back, 1)
            pe.wait_ge(neg_cT_ready, 1)
            pe.sem_inc(neg_cT_ready, -1)
            feed_forward(2)
            turn_h()
            pe.wait_ge(hT_split, 4)
            pe.sem_inc(hT_split, -4)
            for b in range(4):
                w = split_weights(first["q"] + b, w_hi_slots, BLK)
                for c in range(2):
                    channel_job(2 * b + c, w, c * P, hT_lo)
            pe.wait_ge(job_taken, 4)
            attend(True)
            turn_h()
            pe.wait_ge(hT_split, 4)
            pe.sem_inc(hT_split, -4)
            late = []
            for b in range(4):
                pe.wait_ge(w_split, 1)
                pe.sem_inc(w_split, -1)
                slot = (first["o"] + b) % SLOTS
                hi, lo = [part[:, slot, 0:ROWS * D].rearrange("p (k n) -> p k n", n=D) for part in (w_hi, ring_lo)]
                parts = [(source[:, b * ROWS + i, :], w[:, i, :]) for i in range(ROWS) for source, w in ((hT_hi, hi), (hT_hi, lo), (hT_lo, hi))]
                if b < 2:
                    accumulate_rows(parts, b == 0, False).then_inc(slot_free[slot], 1)
                else:
                    accumulate_rows(parts, False, b == 3, [(0, BOTH)])
                    late.append((slot, parts))
            accumulate_rows(late[0][1], False, False, [(1, BOTH)]).then_inc(slot_free[late[0][0]], 1)
            accumulate_rows(late[1][1], False, True, [(1, BOTH)])
            feed_forward(3)

        @block.vector
        def _(dve):
            v = nc.vector
            steps = Count()
            dve.wait_ge(consts, 1)
            dve.sem_inc(pre_free, 1)
            dve.sem_inc(post_free, 1)
            dve.sem_inc(u_free, U_SLOTS)
            dve.sem_inc(v_free, V_SLOTS)
            dve.sem_inc(diag_free, 2)
            dve.sem_inc(acc_read, 1)
            dve.wait_ge(pos_loaded, 16)
            dve.sem_inc(pos_loaded, -16)
            v.tensor_copy(pos_f[:], pos_i[:]).then_inc(pos_float, 1)
            dve.wait_ge(c_act_ready, 1)
            dve.sem_inc(c_act_ready, -1)
            v.tensor_copy(c_hi[:], c_act[:]).then_inc(dve_steps, 1)
            dve.wait_ge(dve_steps, steps.next())
            v.tensor_tensor(c_lo[:], c_act[:], c_hi[:].bitcast(F32), ALU.subtract).then_inc(c_split, 1)
            dve.wait_ge(pos_turned, 1)
            dve.sem_inc(pos_turned, -1)
            v.tensor_copy(pos[:], ps[:, 3, 0:TILES]).then_inc(dve_steps, 1)
            dve.wait_ge(dve_steps, steps.next())
            two_pi = 2.0 * np.pi
            part1 = 6.28125
            part2 = float(np.float32(np.round((two_pi - part1) * 2.0 ** 21) / 2.0 ** 21))
            part3 = float(np.float32(two_pi - part1 - part2))
            near = 1.5 * 2.0 ** 23
            pi = float(np.nextafter(np.float32(np.pi), np.float32(0.0)))
            half = ROPE // 2
            for t in range(TILES):
                v.tensor_scalar(angle[:, 0, t, :], inv_freq[:], pos[:, t:t + 1], None, ALU.mult).then_inc(dve_steps, 1)
                dve.wait_ge(dve_steps, steps.next())
            v.tensor_scalar(angle[:, 1], angle[:, 0], float(1.0 / two_pi), None, ALU.mult).then_inc(dve_steps, 1)
            dve.wait_ge(dve_steps, steps.next())
            v.tensor_scalar(angle[:, 1], angle[:, 1], near, None, ALU.add).then_inc(dve_steps, 1)
            dve.wait_ge(dve_steps, steps.next())
            v.tensor_scalar(angle[:, 1], angle[:, 1], near, None, ALU.subtract).then_inc(dve_steps, 1)
            dve.wait_ge(dve_steps, steps.next())
            for part in (part1, part2, part3):
                v.scalar_tensor_tensor(angle[:, 0], angle[:, 1], -part, angle[:, 0], ALU.mult, ALU.add).then_inc(dve_steps, 1)
                dve.wait_ge(dve_steps, steps.next())
            v.tensor_scalar(angle[:, 2], angle[:, 0], pi, -pi, ALU.min, ALU.max).then_inc(dve_steps, 1)
            dve.wait_ge(dve_steps, steps.next())
            v.tensor_scalar(angle[:, 3], angle[:, 2], float(np.pi / 2), None, ALU.add).then_inc(dve_steps, 1)
            dve.wait_ge(dve_steps, steps.next())
            v.tensor_scalar(angle[:, 1], angle[:, 3], pi, None, ALU.is_gt).then_inc(dve_steps, 1)
            dve.wait_ge(dve_steps, steps.next())
            v.scalar_tensor_tensor(angle[:, 3], angle[:, 1], -two_pi, angle[:, 3], ALU.mult, ALU.add).then_inc(dve_steps, 1)
            dve.wait_ge(dve_steps, steps.next())
            v.tensor_scalar(angle[:, 3], angle[:, 3], pi, -pi, ALU.min, ALU.max).then_inc(angle_ready, 1)
            dve.sem_inc(dve_steps, -steps.reset())

            def scaled(t, scale):
                dve.wait_ge(rms_ready, 1)
                dve.sem_inc(rms_ready, -1)
                v.reciprocal(rstd[:, t:t + 1], rms[:, t:t + 1]).then_inc(dve_steps, 1)
                dve.wait_ge(dve_steps, steps.next())
                return v.scalar_tensor_tensor(h[:, t, :], x[:, t, :], rstd[:, t:t + 1], scale, ALU.mult, ALU.mult)

            def normalise_tile(t, scale, shift):
                ins = scaled(t, scale)
                if shift is not None:
                    ins.then_inc(dve_steps, 1)
                    dve.wait_ge(dve_steps, steps.next())
                    ins = v.tensor_tensor(h[:, t, :], h[:, t, :], shift, ALU.add)
                ins.then_inc(h_ready, 1)

            def low(n, hi, width):
                slot = n % SLOTS
                dve.wait_ge(w_hi_ready, 1)
                dve.sem_inc(w_hi_ready, -1)
                v.tensor_tensor(ring_lo[:, slot, 0:width], ring[:, slot, 0:width], hi[slot][:, 0:width].bitcast(F32),
                                ALU.subtract).then_inc(w_split, 1)

            def split_hT_tile(t, low_part, banks):
                for k in range(2):
                    dve.wait_ge(hT_ready, 1)
                    dve.sem_inc(hT_ready, -1)
                    part = (slice(None), slice(4 * k, 4 * k + 4), slice(t * P, (t + 1) * P))
                    v.tensor_tensor(low_part[part], ps[:, banks + 2 * t + k, :].rearrange("p (k t) -> p k t", t=P),
                                    hT_hi[part].bitcast(F32), ALU.subtract).then_inc(hT_split, 1)

            def split_hT(low_part):
                for t in range(TILES):
                    split_hT_tile(t, low_part, WORK)

            def acc_rows(t):
                return ps[:, 2 * t:2 * t + 2, :].rearrange("p b n -> p (b n)")

            def add_gated(t, segment):
                v.tensor_tensor(h[:, t, :], acc_rows(t), mod[:, segment, :], ALU.mult).then_inc(dve_steps, 1)
                dve.wait_ge(dve_steps, steps.next())
                v.tensor_tensor(x[:, t, :], x[:, t, :], h[:, t, :], ALU.add).then_inc(x_ready, 1)

            def add_normed(weight, give):
                dve.wait_ge(post_in, 16)
                dve.sem_inc(post_in, -16)
                for t in range(TILES):
                    dve.wait_ge(rms2_ready, 1)
                    dve.sem_inc(rms2_ready, -1)
                    v.reciprocal(rstd[:, t:t + 1], rms[:, t:t + 1]).then_inc(dve_steps, 1)
                    dve.wait_ge(dve_steps, steps.next())
                    v.scalar_tensor_tensor(h[:, t, :], acc_rows(t), rstd[:, t:t + 1], gain_post[:], ALU.mult, ALU.mult).then_inc(dve_steps, 1)
                    dve.wait_ge(dve_steps, steps.next())
                    v.scalar_tensor_tensor(x[:, t, :], h[:, t, :], weight, x[:, t, :], ALU.mult, ALU.add).then_inc(give, 1)
                dve.sem_inc(post_free, 1)
                dve.sem_inc(dve_steps, -steps.reset())

            def pre_norm():
                dve.wait_ge(pre_in, 16)
                dve.sem_inc(pre_in, -16)
                for t in range(TILES):
                    normalise_tile(t, gain_pre[:], None)
                fan(dve, pre_free)
                dve.sem_inc(dve_steps, -steps.reset())

            def softmax_rows(second):
                units = attention_units(second)
                S = scores2 if second else scores

                def rows(u):
                    t, heads = units[u]
                    b = u % 2
                    n = P * (t + 1) if second else SEQ
                    dve.wait_ge(scores_done, 1)
                    dve.sem_inc(scores_done, -1)
                    if second:
                        mask = window[:, 0, SEQ - n:SEQ]
                        for i, head in enumerate(heads):
                            ins = v.scalar_tensor_tensor(S[:, b, i, 0:n], ps[:, WORK + 2 * b + i // 2, (i % 2) * SEQ:(i % 2) * SEQ + n],
                                                         c_tok[:, t * HEADS2 + head:t * HEADS2 + head + 1], mask, ALU.add, ALU.add)
                    else:
                        for pair in range(2):
                            ins = v.tensor_tensor(S[:, b, 2 * pair:2 * pair + 2, :],
                                                  ps[:, WORK + 2 * b + pair, :].rearrange("p (i t) -> p i t", t=SEQ),
                                                  window[:, t:t + 1, :].to_broadcast([P, 2, SEQ]), ALU.add)
                    ins.then_inc(dve_steps, 1)
                    dve.wait_ge(dve_steps, steps.next())
                    v.tensor_reduce(row_max[:, b, :], S[:, b, :, 0:n], AX_X, ALU.max).then_inc(dve_steps, 1)
                    dve.wait_ge(dve_steps, steps.next())
                    if not second:
                        sinks = sink[:, heads[0]:heads[0] + GROUP]
                        v.tensor_tensor(row_max[:, b, :], row_max[:, b, :], sinks, ALU.max).then_inc(dve_steps, 1)
                        dve.wait_ge(dve_steps, steps.next())
                        v.tensor_tensor(sink_d[:, b, :], sinks, row_max[:, b, :], ALU.subtract).then_inc(dve_steps, 1)
                        dve.wait_ge(dve_steps, steps.next())
                    v.tensor_scalar(neg_max[:, b, :], row_max[:, b, :], -1.0, None, ALU.mult).then_inc(scores_ready, 1)

                def close(u):
                    t, heads = units[u]
                    b = u % 2
                    dve.wait_ge(sums_ready, 1)
                    dve.sem_inc(sums_ready, -1)
                    if not second:
                        v.tensor_tensor(row_sum[:, u % 4, :], row_sum[:, u % 4, :], sink_e[:, u % 4, :], ALU.add).then_inc(dve_steps, 1)
                        dve.wait_ge(dve_steps, steps.next())
                    v.reciprocal(row_inv[:, b, :], row_sum[:, u % 4, :]).then_inc(dve_steps, 1)
                    dve.wait_ge(dve_steps, steps.next())
                    dve.wait_ge(pv_done, 1)
                    dve.sem_inc(pv_done, -1)
                    dst = (h if second else attn)[:, t, heads[0] * HEAD:(heads[0] + GROUP) * HEAD]
                    v.tensor_tensor(dst.rearrange("p (i d) -> p i d", d=HEAD),
                                    ps[:, 2 + b, 0:GROUP * HEAD].rearrange("p (i d) -> p i d", d=HEAD),
                                    row_inv[:, b, :].unsqueeze(2).to_broadcast([P, GROUP, HEAD]), ALU.mult).then_inc(attn_done, 1)

                rows(0)
                rows(1)
                for u in range(len(units)):
                    if u + 2 < len(units):
                        rows(u + 2)
                    close(u)
                dve.sem_inc(dve_steps, -steps.reset())

            with dve.Fori(0, DEPTH) as l:
                v.tensor_scalar(expert_base[:], expert_base[:], float(EXPERTS), None, ALU.add).then_inc(dve_steps, 1)
                dve.wait_ge(dve_steps, steps.next())
                with dve.Fori(0, ADA_TURNS // 2) as i:
                    for u in range(4):
                        low(u, ada_hi, KC * ADA_N)
                for u in range(2):
                    low(u, ada_hi, KC * ADA_N)
                dve.wait_ge(mod_ready, 1)
                dve.sem_inc(mod_ready, -1)
                dve.wait_ge(pre_in, 16)
                dve.sem_inc(pre_in, -16)
                v.scalar_tensor_tensor(mod[:, 1, :], mod[:, 1, :], 1.0, gain_pre[:], ALU.add, ALU.mult).then_inc(dve_steps, 1)
                dve.wait_ge(dve_steps, steps.next())
                dve.sem_inc(pre_free, 1)
                for t in range(TILES):
                    low(2 + 2 * t, ada_hi, KC * ADA_N)
                    scaled(t, mod[:, 1, :]).then_inc(dve_steps, 1)
                    dve.wait_ge(dve_steps, steps.next())
                    low(3 + 2 * t, ada_hi, KC * ADA_N)
                    v.tensor_tensor(h[:, t, :], h[:, t, :], mod[:, 0, :], ALU.add).then_inc(h_ready, 1)
                fan(dve, dve_steps)
                dve.wait_ge(dve_steps, steps.next())
                for t in range(TILES):
                    low(2 + t, ada_hi, KC * ADA_N)
                    split_hT_tile(t, hT_lo1, 0)
                for u in range(2):
                    low(u, in_hi, KC * BLK)
                dve.wait_ge(mod_ready, 1)
                dve.sem_inc(mod_ready, -1)
                dve.wait_ge(post_in, 16)
                dve.sem_inc(post_in, -16)
                v.scalar_tensor_tensor(mod[:, 4, :], mod[:, 4, :], 1.0, gain_post[:], ALU.add, ALU.mult).then_inc(dve_steps, 1)
                dve.wait_ge(dve_steps, steps.next())
                dve.sem_inc(post_free, 1)

                def low_in(b):
                    low(b, in_hi, KC * (IN_CUT[b + 1] - IN_CUT[b]))

                dve.wait_ge(tables, 1)
                v.reciprocal(window_share[:], window_count[:]).then_inc(share_ready, 1)
                for b in range(2, 5):
                    low_in(b)
                dve.wait_ge(dve_params, 3 * 16)
                dve.sem_inc(dve_params, -3 * 16)
                dve.wait_ge(qk_ready, 1)
                dve.sem_inc(qk_ready, -1)
                v.tensor_tensor(qk_sq[:], qk[:], qk[:], ALU.mult).then_inc(dve_steps, 1)
                dve.wait_ge(dve_steps, steps.next())
                v.tensor_reduce(head_sq[:], qk_sq[:], AX_X, ALU.add).then_inc(head_sq_ready, 1)
                low_in(5)
                dve.wait_ge(head_rms_ready, 1)
                dve.sem_inc(head_rms_ready, -1)
                v.reciprocal(head_rms[:], head_rms[:]).then_inc(dve_steps, 1)
                dve.wait_ge(dve_steps, steps.next())
                v.tensor_tensor(qk[:], qk[:], head_rms[:].unsqueeze(3).to_broadcast([P, TILES, QK, HEAD]), ALU.mult).then_inc(dve_steps, 1)
                dve.wait_ge(dve_steps, steps.next())
                low_in(6)
                for t in range(TILES):
                    v.tensor_tensor(qk[:, t], qk[:, t], qk_gain[:], ALU.mult).then_inc(dve_steps, 1)
                    dve.wait_ge(dve_steps, steps.next())
                low_in(7)
                dve.wait_ge(rope_ready, 1)
                first_half, second_half = qk[:, :, :, 0:half], qk[:, :, :, half:ROPE]
                cos = cosine[:].unsqueeze(2).to_broadcast([P, TILES, QK, half])
                sin = sine[:].unsqueeze(2).to_broadcast([P, TILES, QK, half])
                for n, (part, turn) in enumerate(((first_half, cos), (second_half, sin), (second_half, cos), (first_half, sin))):
                    v.tensor_tensor(rope_t[:, n], part, turn, ALU.mult).then_inc(dve_steps, 1)
                    dve.wait_ge(dve_steps, steps.next())
                v.tensor_tensor(first_half, rope_t[:, 0], rope_t[:, 1], ALU.subtract).then_inc(dve_steps, 1)
                dve.wait_ge(dve_steps, steps.next())
                v.tensor_tensor(second_half, rope_t[:, 2], rope_t[:, 3], ALU.add).then_inc(qk_done, 1)
                softmax_rows(False)
                for t in range(TILES):
                    dve.wait_ge(rows_done, 1)
                    dve.sem_inc(rows_done, -1)
                    if t == TILES - 1:
                        dve.sem_inc(slot_free[SLOTS - 1], 1)
                    add_gated(t, 2)
                    normalise_tile(t, mod[:, 4, :], mod[:, 3, :])
                    low(t, in_hi, KC * BLK)

                def best_keys(s):
                    v.max(best[:, s, 0:8], half_s[:, s, :]).then_inc(dve_steps, 1)
                    dve.wait_ge(dve_steps, steps.next())
                    v.max_index(best_i[:, s, 0:8], best[:, s, 0:8], half_s[:, s, :]).then_inc(dve_steps, 1)
                    dve.wait_ge(dve_steps, steps.next())
                    v.match_replace(half_r[:, s, :], best[:, s, 0:8], half_s[:, s, :], LEAST).then_inc(dve_steps, 1)
                    dve.wait_ge(dve_steps, steps.next())
                    v.max(best[:, s, 8:16], half_r[:, s, :]).then_inc(dve_steps, 1)
                    dve.wait_ge(dve_steps, steps.next())
                    v.max_index(best_i[:, s, 8:16], best[:, s, 8:16], half_r[:, s, :]).then_inc(dve_steps, 1)
                    dve.wait_ge(dve_steps, steps.next())

                def best_pairs(p):
                    v.tensor_tensor(cand[:].rearrange("p (i j) -> p i j", i=TOPK), best[:, 0, :].unsqueeze(2).to_broadcast([P, TOPK, TOPK]),
                                    best[:, 1, :].unsqueeze(1).to_broadcast([P, TOPK, TOPK]), ALU.add).then_inc(dve_steps, 1)
                    dve.wait_ge(dve_steps, steps.next())
                    v.max(top[:, p, 0:8], cand[:]).then_inc(dve_steps, 1)
                    dve.wait_ge(dve_steps, steps.next())
                    v.max_index(place[:, 0:8], top[:, p, 0:8], cand[:]).then_inc(dve_steps, 1)
                    dve.wait_ge(dve_steps, steps.next())
                    v.match_replace(cand_r[:], top[:, p, 0:8], cand[:], LEAST).then_inc(dve_steps, 1)
                    dve.wait_ge(dve_steps, steps.next())
                    v.max(top[:, p, 8:16], cand_r[:]).then_inc(dve_steps, 1)
                    dve.wait_ge(dve_steps, steps.next())
                    v.max_index(place[:, 8:16], top[:, p, 8:16], cand_r[:]).then_inc(dve_steps, 1)
                    dve.wait_ge(dve_steps, steps.next())
                    v.tensor_scalar(neg_top[:, p, :], top[:, p, 0:1], -1.0, None, ALU.mult).then_inc(top_ready, 1)
                    v.tensor_scalar(place2[:, 0, :], place[:], 4, None, ALU.logical_shift_right).then_inc(dve_steps, 1)
                    dve.wait_ge(dve_steps, steps.next())
                    v.tensor_scalar(place2[:, 1, :], place[:], TOPK - 1, None, ALU.bitwise_and).then_inc(dve_steps, 1)
                    dve.wait_ge(dve_steps, steps.next())
                    v.tensor_copy(place_f[:], place2[:]).then_inc(dve_steps, 1)
                    dve.wait_ge(dve_steps, steps.next())
                    v.tensor_copy(best_f[:], best_i[:]).then_inc(dve_steps, 1)
                    dve.wait_ge(dve_steps, steps.next())
                    for s in range(2):
                        v.tensor_tensor(onehot[:], place_f[:, s, :].unsqueeze(2).to_broadcast([P, TOPK, TOPK]),
                                        iota16[:].unsqueeze(1).to_broadcast([P, TOPK, TOPK]), ALU.is_equal).then_inc(dve_steps, 1)
                        dve.wait_ge(dve_steps, steps.next())
                        v.tensor_tensor(onehot[:], onehot[:], best_f[:, s, :].unsqueeze(1).to_broadcast([P, TOPK, TOPK]), ALU.mult).then_inc(dve_steps, 1)
                        dve.wait_ge(dve_steps, steps.next())
                        v.tensor_reduce(chosen[:, s, :], onehot[:], AX_X, ALU.add).then_inc(dve_steps, 1)
                        dve.wait_ge(dve_steps, steps.next())
                    v.scalar_tensor_tensor(expert_f[:], chosen[:, 0, :], float(KEYS), chosen[:, 1, :], ALU.mult, ALU.add).then_inc(dve_steps, 1)
                    dve.wait_ge(dve_steps, steps.next())
                    v.tensor_scalar(expert[:, p, :], expert_f[:], expert_base[:], None, ALU.add).then_inc(expert_ready, 1)

                def route(n, p):
                    v.tensor_copy(half_s[:].rearrange("p h k -> p (h k)"), key_s[:, bass.ds(n, 1), :, :].rearrange("p n h k -> p (n h k)")).then_inc(dve_steps, 1)
                    dve.wait_ge(dve_steps, steps.next())
                    for s in range(2):
                        best_keys(s)
                    best_pairs(p)

                split_hT(query_lo)
                for u in range(2, 4):
                    low(u, in_hi, KC * BLK)
                dve.wait_ge(key_s_ready, 1)
                dve.sem_inc(key_s_ready, -1)
                v.tensor_copy(half_s[:].rearrange("p h k -> p (h k)"), key_s[:, 0, :, :].rearrange("p h k -> p (h k)")).then_inc(dve_steps, 1)
                dve.wait_ge(dve_steps, steps.next())
                for s in range(2):
                    best_keys(s)
                    low(4 + s, in_hi, KC * BLK)
                best_pairs(0)
                for u in range(6, 8):
                    low(u, in_hi, KC * BLK)
                dve.sem_inc(dve_steps, -steps.reset())

                def unit(t, n, p, follow):
                    for g in range(2):
                        for j in range(GRP):
                            dve.wait_ge(u_in[j], (l * (2 * UNITS) + (n * 2 + (g + 1))) * 16)
                            v.tensor_tensor_reduce(out=junk, in0=u_ring[:, j, :], in1=h[:, t, :], scale=1.0, scalar=0.0,
                                                   op0=ALU.mult, op1=ALU.add, accum_out=dots[:, g, j:j + 1]).then_inc(dve_steps, 1)
                            dve.wait_ge(dve_steps, steps.next())
                            dve.sem_inc(u_free, 1)
                        dve.sem_inc(dots_ready, 1)
                        if g == 0:
                            dve.wait_ge(gate_ready, 1)
                            dve.sem_inc(gate_ready, -1)
                            v.reciprocal(gate_inv[:], gate_sum[:, p, :]).then_inc(dve_steps, 1)
                            dve.wait_ge(dve_steps, steps.next())
                            v.tensor_scalar(gate[:], gate_e[:, p, :], gate_inv[:], None, ALU.mult).then_inc(dve_steps, 1)
                            dve.wait_ge(dve_steps, steps.next())
                        dve.wait_ge(acts_ready, 1)
                        dve.sem_inc(acts_ready, -1)
                        if g == 0:
                            dve.wait_ge(diag_free, 1)
                            dve.sem_inc(diag_free, -1)
                        for j in range(GRP):
                            k = g * GRP + j
                            v.tensor_scalar(diag[:, k, :], ident[:], acts[:, g, j:j + 1], gate[:, k:k + 1], ALU.mult, ALU.mult).then_inc(diag_ready, 1)
                        if g == 0:
                            dve.wait_ge(diag_free, 1)
                            dve.sem_inc(diag_free, -1)
                            if t == 0:
                                dve.wait_ge(key_s_ready, 1)
                                dve.sem_inc(key_s_ready, -1)
                            if follow:
                                route(n + 1, 1 - p)
                    dve.sem_inc(dve_steps, -steps.reset())

                with dve.Fori(0, EXPERT_HEADS // 2) as i:
                    for p in range(2):
                        unit(0, i * 2 + p, p, True)
                dve.sem_inc(params_free, 1)
                with dve.Fori(0, EXPERT_HEADS // 2 - 1) as i:
                    for p in range(2):
                        unit(1, i * 2 + (EXPERT_HEADS + p), p, True)
                dve.wait_ge(y_ready, 1)
                dve.sem_inc(y_ready, -1)
                add_gated(0, 5)
                dve.sem_inc(dve_steps, -steps.reset())
                unit(1, UNITS - 2, 0, True)
                unit(1, UNITS - 1, 1, False)
                dve.wait_ge(diag_free, 1)
                for one in slot_free[:SLOTS // 2]:
                    dve.sem_inc(one, 1)
                dve.wait_ge(y_ready, 1)
                dve.sem_inc(y_ready, -1)
                for one in slot_free[SLOTS // 2:]:
                    dve.sem_inc(one, 1)
                add_gated(1, 5)
                fan(dve, acc_read)
                dve.sem_inc(dve_steps, -steps.reset())

            def low_ff(n):
                low(n, w_hi_slots, FF_SLOT)

            def low_block(n):
                low(n, w_hi_slots, KC * BLK)

            def feed_forward(f, ahead, give=x_ready):
                n0 = first[f"ff{f}"]

                def gated(b):
                    dve.wait_ge(silu_ready, 1)
                    dve.sem_inc(silu_ready, -1)
                    v.tensor_tensor(silu_g[:, b, :], silu_g[:, b, :], ps[:, WORK + b, SEQ:2 * SEQ], ALU.mult).then_inc(dve_steps, 1)
                    dve.wait_ge(dve_steps, steps.next())
                    v.tensor_copy(ff_hi[:, b, :], silu_g[:, b, :]).then_inc(dve_steps, 1)
                    dve.wait_ge(dve_steps, steps.next())
                    v.tensor_tensor(ff_lo[:, b, :], silu_g[:, b, :], ff_hi[:, b, :].bitcast(F32), ALU.subtract).then_inc(ff_ready, 1)

                pre_norm()
                if f < 2:
                    low_ff(n0)
                split_hT(hT_lo)
                if f < 2:
                    low_ff(n0 + 1)
                with dve.Fori(0, (FF_CHUNKS - 2) // SLOTS) as i:
                    for u in range(SLOTS):
                        gated(u % 2)
                        low_ff(n0 + 2 + u)
                    dve.sem_inc(dve_steps, -steps.reset())
                for u in range(2):
                    gated(u)
                    if ahead is not None:
                        ahead(n0 + FF_CHUNKS + u)
                dve.sem_inc(dve_steps, -steps.reset())
                add_normed(0.5, give)

            def log1p_series(t, total):
                v.tensor_scalar(t[2], t[1], 2.0, None, ALU.add).then_inc(dve_steps, 1)
                dve.wait_ge(dve_steps, steps.next())
                v.reciprocal(t[2], t[2]).then_inc(dve_steps, 1)
                dve.wait_ge(dve_steps, steps.next())
                v.tensor_tensor(t[3], t[1], t[2], ALU.mult).then_inc(dve_steps, 1)
                dve.wait_ge(dve_steps, steps.next())
                v.tensor_tensor(t[4], t[3], t[3], ALU.mult).then_inc(dve_steps, 1)
                dve.wait_ge(dve_steps, steps.next())
                v.tensor_scalar(t[5], t[4], 1.0 / (2 * total + 1), None, ALU.mult).then_inc(dve_steps, 1)
                dve.wait_ge(dve_steps, steps.next())
                for n in range(total - 1, 0, -1):
                    v.scalar_tensor_tensor(t[5], t[5], 1.0 / (2 * n + 1), t[4], ALU.add, ALU.mult).then_inc(dve_steps, 1)
                    dve.wait_ge(dve_steps, steps.next())
                v.scalar_tensor_tensor(t[5], t[5], 1.0, t[3], ALU.add, ALU.mult).then_inc(dve_steps, 1)
                dve.wait_ge(dve_steps, steps.next())
                v.tensor_scalar(t[5], t[5], 2.0, None, ALU.mult).then_inc(dve_steps, 1)
                dve.wait_ge(dve_steps, steps.next())

            def low_rnn(n):
                slot = n % SLOTS
                rows, width = (P, RNN_IN) if n < first["rnn_out"] else (RC, D)
                dve.wait_ge(w_hi_ready, 1)
                dve.sem_inc(w_hi_ready, -1)
                v.tensor_tensor(ring_lo[0:rows, slot, 0:width], ring[0:rows, slot, 0:width], rnn_hi[0:rows, slot, 0:width].bitcast(F32),
                                ALU.subtract).then_inc(w_split, 1)

            feed_forward(0, low_rnn)
            fan(dve, ff0_over)
            pre_norm()
            for t in range(TILES):
                for k in range(2):
                    dve.wait_ge(hT_ready, 1)
                    dve.sem_inc(hT_ready, -1)
                    tokens = slice(t * P, (t + 1) * P)
                    v.tensor_tensor(hT_lo_r[:, 2 * k:2 * k + 2, :, tokens],
                                    ps[:, WORK + 2 * t + k, :].rearrange("p (s k t) -> p s k t", s=2, t=P),
                                    hT_hi[:, 4 * k:4 * k + 4, tokens].rearrange("p (s k) t -> p s k t", s=2).bitcast(F32),
                                    ALU.subtract).then_inc(hT_split, 1)
            dve.wait_ge(rnn_cols_ready, 1)
            dve.sem_inc(rnn_cols_ready, -1)
            lam = rnn_cols[:, 7, :]
            v.scalar_tensor_tensor(decay[:, 0, :], lam, -1.0, lam, ALU.mult, ALU.max).then_inc(lam_abs, 1)
            dve.wait_ge(lam_exp, 1)
            dve.sem_inc(lam_exp, -1)
            log1p_series([decay[:, k, :] for k in range(6)], 8)
            v.tensor_scalar(decay[:, 0, :], lam, -1.0, 0.0, ALU.mult, ALU.max).then_inc(dve_steps, 1)
            dve.wait_ge(dve_steps, steps.next())
            v.tensor_tensor(decay[:, 0, :], decay[:, 0, :], decay[:, 5, :], ALU.add).then_inc(dve_steps, 1)
            dve.wait_ge(dve_steps, steps.next())
            v.tensor_scalar(decay_neg[:], decay[:, 0, :], -8.0, None, ALU.mult).then_inc(dve_steps, 1)
            dve.wait_ge(dve_steps, steps.next())
            v.tensor_scalar(decay_pos[:], decay[:, 0, :], 8.0, None, ALU.mult).then_inc(decay_ready, 1)
            dve.wait_ge(rnn_zeroed, 1)
            dve.sem_inc(rnn_zeroed, -1)

            def convolve(s):
                dve.wait_ge(rec_in_ready, 1)
                dve.sem_inc(rec_in_ready, -1)
                chunks = range(3 * s, 3 * s + 3)
                for j in chunks:
                    ins = v.tensor_scalar(rec[:, j, :], rec_in[:, j, CONV_K - 1:], rnn_cols[:, 3, j:j + 1], rnn_cols[:, 4, j:j + 1], ALU.mult, ALU.add)
                for k in range(CONV_K - 1):
                    ins.then_inc(dve_steps, 1)
                    dve.wait_ge(dve_steps, steps.next())
                    for j in chunks:
                        ins = v.scalar_tensor_tensor(rec[:, j, :], rec_in[:, j, k:k + SEQ], rnn_cols[:, k, j:j + 1], rec[:, j, :], ALU.mult, ALU.add)
                ins.then_inc(rec_ready, 1)

            def squares(s):
                c = slice(3 * s, 3 * s + 3)
                dve.wait_ge(gates_ready, 1)
                dve.sem_inc(gates_ready, -1)
                v.tensor_tensor(gate_i[:, c], gate_i[:, c], rec[:, c], ALU.mult).then_inc(dve_steps, 1)
                dve.wait_ge(dve_steps, steps.next())
                v.tensor_tensor(rec[:, c], decay_a[:, c], decay_a[:, c], ALU.mult).then_inc(dve_steps, 1)
                dve.wait_ge(dve_steps, steps.next())
                v.scalar_tensor_tensor(gate_r[:, c], rec[:, c], 1.0, gate_r[:, c], ALU.add, ALU.mult).then_inc(root_in, 1)

            def recur(s):
                c = slice(3 * s, 3 * s + 3)
                dve.wait_ge(root_ready, 1)
                dve.sem_inc(root_ready, -1)
                v.tensor_tensor(gate_i[:, c], gate_i[:, c], gate_r[:, c], ALU.mult).then_inc(dve_steps, 1)
                dve.wait_ge(dve_steps, steps.next())
                for j in range(3 * s, 3 * s + 3):
                    ins = v.tensor_tensor_scan(rec[:, j, :], decay_a[:, j, :], gate_i[:, j, :], 0.0, ALU.mult, ALU.add)
                ins.then_inc(dve_steps, 1)
                dve.wait_ge(dve_steps, steps.next())

            def gated_rows(s):
                c = slice(3 * s, 3 * s + 3)
                dve.wait_ge(gelu_ready, 1)
                dve.sem_inc(gelu_ready, -1)
                v.tensor_tensor(gate_g[:, c], gate_g[:, c], rec[:, c], ALU.mult).then_inc(dve_steps, 1)
                dve.wait_ge(dve_steps, steps.next())
                v.tensor_copy(out_hi[0:RC, c], gate_g[:, c]).then_inc(dve_steps, 1)
                dve.wait_ge(dve_steps, steps.next())
                v.tensor_tensor(out_lo[0:RC, c], gate_g[:, c], out_hi[0:RC, c].bitcast(F32), ALU.subtract).then_inc(rnn_out_ready, 1)

            n0 = first["rnn_in"]
            low_rnn(n0 + 2)
            convolve(0)
            low_rnn(n0 + 3)
            convolve(1)
            low_rnn(n0 + 4)
            low_rnn(n0 + 5)
            convolve(2)
            low_rnn(n0 + 6)
            squares(0)
            convolve(3)
            low_rnn(n0 + 7)
            squares(1)
            low_rnn(n0 + 8)
            squares(2)
            low_rnn(n0 + 9)
            squares(3)
            low_rnn(n0 + 10)
            for s in range(3):
                recur(s)
            low_rnn(n0 + 11)
            recur(3)
            gated_rows(0)
            gated_rows(1)
            low_rnn(first["rnn_out"])
            gated_rows(2)
            low_rnn(first["rnn_out"] + 1)
            gated_rows(3)
            for u in range(2, R_CHUNKS):
                low_rnn(first["rnn_out"] + u)
            add_normed(1.0, x_ready)
            fan(dve, rnn_over)
            feed_forward(1, low_block)
            pre_norm()
            split_hT(hT_lo)
            dve.wait_ge(f_ready, 1)
            dve.sem_inc(f_ready, -1)
            v.scalar_tensor_tensor(logs[:, 0, :], f_tok[:], -1.0, f_tok[:], ALU.mult, ALU.max).then_inc(f_abs, 1)
            dve.wait_ge(f_exp, 1)
            dve.sem_inc(f_exp, -1)
            for u in range(2, 4):
                low_block(first["kv"] + u)
            log1p_series([logs[:, k, :] for k in range(6)], 8)
            v.scalar_tensor_tensor(log_f[:], f_tok[:], 0.0, logs[:, 5, :], ALU.min, ALU.subtract).then_inc(log_f_ready, 1)
            for u in range(4, 8):
                low_block(first["kv"] + u)
            for u in range(2):
                low_ff(first["ff2"] + u)
            dve.sem_inc(x_ready, TILES)
            dve.sem_inc(dve_steps, -steps.reset())
            feed_forward(2, low_block)
            fan(dve, ff2_over)
            pre_norm()
            split_hT(hT_lo)
            for u in range(2, 4):
                low_block(first["q"] + u)
            for u in range(2):
                low_block(first["o"] + u)
            softmax_rows(True)
            dve.sem_inc(h_ready, TILES)
            split_hT(hT_lo)
            for u in range(2, 4):
                low_block(first["o"] + u)
            for u in range(2):
                low_ff(first["ff3"] + u)
            add_normed(1.0, x_ready)
            feed_forward(3, None, x_final)


INPUTS = [
    "x", "c", "positions", "norm1_g", "norm2_g", "w_ada", "b_ada", "w_in", "q_norm_g", "k_norm_g", "attn_sink",
    "conv_w", "pool_w", "pool_scale", "w_out", "peer_wq", "peer_keys", "peer_u", "peer_v", "ffn1_pre_g_2",
    "ffn1_w_gate_2", "ffn1_w_up_2", "ffn1_w_down_2", "ffn1_post_g_2", "mix_pre_g_2", "mix_post_g_2",
    "ffn2_pre_g_2", "ffn2_w_gate_2", "ffn2_w_up_2", "ffn2_w_down_2", "ffn2_post_g_2", "rg_w_in_2",
    "rg_conv_w_2", "rg_conv_b_2", "rg_w_a_2", "rg_b_a_2", "rg_w_x_2", "rg_b_x_2", "rg_lambda_2", "rg_w_out_2",
    "kv_norm_g_2", "w_kv_2", "w_fgate_2", "b_fgate_2", "attn_w_q_2", "attn_w_o_2",
]


def kernel(**inputs):
    import concourse.bacc as bacc
    from concourse.bass_utils import run_bass_kernel_spmd

    nc = bacc.Bacc("TRN2", target_bir_lowering=False, num_devices=1)
    arrays, views = {}, {}
    for name in INPUTS:
        a = np.ascontiguousarray(inputs[name])
        if name in ("peer_u", "peer_v"):
            a = a.reshape(-1, a.shape[-1])
        arrays["in_" + name] = a
        views[name] = nc.dram_tensor("in_" + name, a.shape, mybir.dt.from_np(a.dtype), kind="ExternalInput").ap()
    out = nc.dram_tensor("out", (1, SEQ, D), F32, kind="ExternalOutput").ap()
    program(nc, views, out)
    return run_bass_kernel_spmd(nc, [arrays], core_ids=[0]).results[0]["out"]
```
